# Optimizing a Trainium2 kernel written in Bass

```python
import math
import jax
import jax.numpy as jnp
from jax import lax
import numpy as np
import jax, jax.numpy as jnp

D_MODEL = 1024
BATCH = 1
SEQ = 256
DEPTH = 1

N_NSA_HEADS = 8
N_KV_HEADS = 2
GQA_GROUP = N_NSA_HEADS // N_KV_HEADS
HEAD_DIM = 64
NSA_WIDTH = N_NSA_HEADS * HEAD_DIM
KV_WIDTH = N_KV_HEADS * HEAD_DIM
N_BRANCHES = 3
N_GATES = N_BRANCHES * N_NSA_HEADS
CMP_BLOCK = 32
CMP_STRIDE = 16
CMP_HIDDEN = 4 * HEAD_DIM
SLC_BLOCK = 64
SLC_TOPK = 16
N_LOCAL_BLOCKS = 2
WINDOW = 512
Q_BLOCK = 128
GMLP_WIDTH = D_MODEL - NSA_WIDTH
N_GMLP_GROUPS = 8
GMLP_GROUP_DIM = GMLP_WIDTH // N_GMLP_GROUPS
GMLP_CHUNK = 128
IN_WIDTH = NSA_WIDTH + 6 * KV_WIDTH + N_GATES + 2 * GMLP_WIDTH
D_FF = ((8 * D_MODEL + 3 * 256 - 1) // (3 * 256)) * 256
N_BUCKETS = 32
REL_MAX_DISTANCE = 128
RMS_EPS = 1e-6
LN_EPS = 1e-5


def rms_norm(x, g):
    xf = x.astype(jnp.float32)
    y = xf * lax.rsqrt(jnp.mean(xf * xf, axis=-1, keepdims=True) + RMS_EPS)
    return (y * g.astype(jnp.float32)).astype(x.dtype)

def layer_norm(x, g, b):
    xf = x.astype(jnp.float32)
    mu = jnp.mean(xf, axis=-1, keepdims=True)
    var = jnp.mean(jnp.square(xf - mu), axis=-1, keepdims=True)
    y = (xf - mu) * lax.rsqrt(var + LN_EPS)
    return (y * g.astype(jnp.float32) + b.astype(jnp.float32)).astype(x.dtype)

def t5_bucket(dist):
    n = jnp.maximum(dist, 0)
    max_exact = N_BUCKETS // 2
    nf = jnp.maximum(n, max_exact).astype(jnp.float32)
    large = max_exact + (jnp.log(nf / max_exact) / math.log(REL_MAX_DISTANCE / max_exact)
                         * (N_BUCKETS - max_exact)).astype(jnp.int32)
    return jnp.where(n < max_exact, n, jnp.minimum(large, N_BUCKETS - 1))

def bias_shared(table, dist):
    b = table.astype(jnp.float32)[t5_bucket(dist)]
    return b.transpose(2, 0, 1).reshape(N_KV_HEADS, GQA_GROUP, *dist.shape)

def bias_grouped(table, dist):
    tab = table.astype(jnp.float32).reshape(N_BUCKETS, N_KV_HEADS, GQA_GROUP)
    b = jax.vmap(lambda t, d: t[d], in_axes=(1, 1), out_axes=1)(tab, t5_bucket(dist))
    return b.transpose(0, 1, 4, 2, 3)

def masked_softmax(logits, mask):
    lg = jnp.where(mask, logits.astype(jnp.float32), -jnp.inf)
    m = jnp.max(lg, axis=-1, keepdims=True)
    m = jnp.where(jnp.isfinite(m), m, 0.0)
    e = jnp.where(mask, jnp.exp(lg - m), 0.0)
    return e / jnp.maximum(jnp.sum(e, axis=-1, keepdims=True), 1e-30)

def compress_tokens(t, pos_emb, w1, w2):
    B, G, S, dh = t.shape
    r = CMP_BLOCK // CMP_STRIDE
    n_chunks = S // CMP_STRIDE
    n_cmp = n_chunks - r + 1
    chunks = t.reshape(B, G, n_chunks, CMP_STRIDE, dh)
    blocks = jnp.concatenate([chunks[:, :, i:i + n_cmp] for i in range(r)], axis=3)
    blocks = (blocks + pos_emb).reshape(B, G, n_cmp, CMP_BLOCK * dh)
    return jax.nn.gelu(blocks @ w1) @ w2

gather_blocks = jax.vmap(jax.vmap(lambda blocks, ix: blocks[ix]))

def nsa_gmlp_mixer(h, w_in, cmp_pos_k, cmp_w1_k, cmp_w2_k, cmp_pos_v, cmp_w1_v, cmp_w2_v,
                   gmlp_ln_g, gmlp_ln_b, gmlp_w_s, gmlp_b_s, w_out, rel_bias):
    B, S, _ = h.shape
    G, R, dh = N_KV_HEADS, GQA_GROUP, HEAD_DIM
    proj = jnp.einsum("bsd,de->bse", h, w_in)
    sizes = [NSA_WIDTH] + [KV_WIDTH] * 6 + [N_GATES, GMLP_WIDTH]
    points = [sum(sizes[:i + 1]) for i in range(len(sizes))]
    q, k_c, v_c, k_s, v_s, k_w, v_w, gate_logits, u, v = jnp.split(proj, points, axis=-1)

    def heads_kv(t):
        return t.reshape(B, S, G, dh).transpose(0, 2, 1, 3)

    q = q.reshape(B, S, G, R, dh).transpose(0, 2, 3, 1, 4) * (HEAD_DIM ** -0.5)
    gates = jax.nn.sigmoid(gate_logits.astype(jnp.float32)).reshape(B, S, G, R, N_BRANCHES)
    gates = gates.transpose(0, 2, 3, 1, 4)

    kc = compress_tokens(heads_kv(k_c), cmp_pos_k, cmp_w1_k, cmp_w2_k)
    vc = compress_tokens(heads_kv(v_c), cmp_pos_v, cmp_w1_v, cmp_w2_v)
    n_cmp = kc.shape[2]
    cmp_start = jnp.arange(n_cmp, dtype=jnp.int32) * CMP_STRIDE
    cmp_end = cmp_start + (CMP_BLOCK - 1)

    n_slc = S // SLC_BLOCK
    ks_blocks = heads_kv(k_s).reshape(B, G, n_slc, SLC_BLOCK, dh)
    vs_blocks = heads_kv(v_s).reshape(B, G, n_slc, SLC_BLOCK, dh)
    slc_start = jnp.arange(n_slc, dtype=jnp.int32) * SLC_BLOCK
    ov = (jnp.minimum(cmp_start[:, None] + CMP_BLOCK, slc_start[None, :] + SLC_BLOCK)
          - jnp.maximum(cmp_start[:, None], slc_start[None, :]))
    overlap = jnp.maximum(ov, 0).astype(jnp.float32) / CMP_BLOCK
    k_sel = min(SLC_TOPK, n_slc)

    pad = ((0, 0), (0, 0), (WINDOW, 0), (0, 0))
    kw_pad = jnp.pad(heads_kv(k_w), pad)
    vw_pad = jnp.pad(heads_kv(v_w), pad)

    def query_block(qi):
        s0 = qi * Q_BLOCK
        tq = s0 + jnp.arange(Q_BLOCK, dtype=jnp.int32)
        qb = lax.dynamic_slice_in_dim(q, s0, Q_BLOCK, axis=3)
        gb = lax.dynamic_slice_in_dim(gates, s0, Q_BLOCK, axis=3)

        d_c = tq[:, None] - cmp_end[None, :]
        lg_c = jnp.einsum("bgrqd,bgkd->bgrqk", qb, kc).astype(jnp.float32) + bias_shared(rel_bias, d_c)
        p_c = masked_softmax(lg_c, d_c >= 0)
        o_c = jnp.einsum("bgrqk,bgkd->bgrqd", p_c.astype(vc.dtype), vc)

        imp = jnp.einsum("bgrqk,kn->bgqn", p_c, overlap)
        jq = (tq // SLC_BLOCK)[:, None]
        blk = jnp.arange(n_slc, dtype=jnp.int32)[None, :]
        forced = (blk == 0) | ((blk <= jq) & (blk > jq - N_LOCAL_BLOCKS))
        score = jnp.where(forced, jnp.inf, jnp.where(blk <= jq, imp, -jnp.inf))
        _, idx = lax.top_k(score, k_sel)
        kb = gather_blocks(ks_blocks, idx).reshape(B, G, Q_BLOCK, k_sel * SLC_BLOCK, dh)
        vb = gather_blocks(vs_blocks, idx).reshape(B, G, Q_BLOCK, k_sel * SLC_BLOCK, dh)
        key_pos = (idx[..., None] * SLC_BLOCK + jnp.arange(SLC_BLOCK, dtype=jnp.int32)
                   ).reshape(B, G, Q_BLOCK, k_sel * SLC_BLOCK)
        d_s = tq[None, None, :, None] - key_pos
        lg_s = jnp.einsum("bgrqd,bgqkd->bgrqk", qb, kb).astype(jnp.float32) + bias_grouped(rel_bias, d_s)
        p_s = masked_softmax(lg_s, (d_s >= 0)[:, :, None])
        o_s = jnp.einsum("bgrqk,bgqkd->bgrqd", p_s.astype(vb.dtype), vb)

        kwb = lax.dynamic_slice_in_dim(kw_pad, s0, WINDOW + Q_BLOCK, axis=2)
        vwb = lax.dynamic_slice_in_dim(vw_pad, s0, WINDOW + Q_BLOCK, axis=2)
        kpos = s0 - WINDOW + jnp.arange(WINDOW + Q_BLOCK, dtype=jnp.int32)
        d_w = tq[:, None] - kpos[None, :]
        mask_w = (d_w >= 0) & (d_w < WINDOW) & (kpos[None, :] >= 0)
        lg_w = jnp.einsum("bgrqd,bgkd->bgrqk", qb, kwb).astype(jnp.float32) + bias_shared(rel_bias, d_w)
        p_w = masked_softmax(lg_w, mask_w)
        o_w = jnp.einsum("bgrqk,bgkd->bgrqd", p_w.astype(vwb.dtype), vwb)

        o = gb[..., 0:1] * o_c + gb[..., 1:2] * o_s + gb[..., 2:3] * o_w
        return o.astype(h.dtype)

    o = lax.map(query_block, jnp.arange(S // Q_BLOCK, dtype=jnp.int32))
    nsa_out = o.transpose(1, 0, 4, 2, 3, 5).reshape(B, S, NSA_WIDTH)

    z_u = jax.nn.gelu(u)
    z_v = layer_norm(jax.nn.gelu(v), gmlp_ln_g, gmlp_ln_b)
    n_chunks = S // GMLP_CHUNK
    zv = z_v.reshape(B, n_chunks, GMLP_CHUNK, N_GMLP_GROUPS, GMLP_GROUP_DIM)
    causal = jnp.tril(jnp.ones((GMLP_CHUNK, GMLP_CHUNK), dtype=bool))
    w_s = jnp.where(causal, gmlp_w_s, 0.0).astype(zv.dtype)
    sv = jnp.einsum("gts,bnsgd->bntgd", w_s, zv) + gmlp_b_s.T[None, None, :, :, None]
    gm = (z_u.reshape(B, n_chunks, GMLP_CHUNK, N_GMLP_GROUPS, GMLP_GROUP_DIM) * sv).reshape(B, S, GMLP_WIDTH)

    mixed = jnp.concatenate([nsa_out, gm.astype(h.dtype)], axis=-1)
    return jnp.einsum("bse,ed->bsd", mixed, w_out)

def swiglu_ffn(h, w_gate_up, w_down):
    gate, up = jnp.split(jnp.einsum("bsd,df->bsf", h, w_gate_up), 2, axis=-1)
    return jnp.einsum("bsf,fd->bsd", jax.nn.silu(gate) * up, w_down)

def first_inputs(seed: int = 0) -> dict:
    key = jax.random.key(seed)
    ks = jax.random.split(key, 20)
    f32 = jnp.float32
    L = DEPTH

    def nrm(k, shape, scale):
        return jax.random.normal(k, shape, f32) * scale

    def gain(k, shape):
        return 1.0 + 0.05 * jax.random.normal(k, shape, f32)

    return {
        "x": nrm(ks[0], (BATCH, SEQ, D_MODEL), 1.0),
        "rel_bias": nrm(ks[1], (N_BUCKETS, N_NSA_HEADS), 0.5),
        "norm_mix_pre": gain(ks[2], (L, D_MODEL)),
        "norm_mix_post": gain(ks[3], (L, D_MODEL)),
        "norm_ffn_pre": gain(ks[4], (L, D_MODEL)),
        "norm_ffn_post": gain(ks[5], (L, D_MODEL)),
        "w_in": nrm(ks[6], (L, D_MODEL, IN_WIDTH), D_MODEL ** -0.5),
        "cmp_pos_k": nrm(ks[7], (L, CMP_BLOCK, HEAD_DIM), 0.1),
        "cmp_w1_k": nrm(ks[8], (L, CMP_BLOCK * HEAD_DIM, CMP_HIDDEN), (CMP_BLOCK * HEAD_DIM) ** -0.5),
        "cmp_w2_k": nrm(ks[9], (L, CMP_HIDDEN, HEAD_DIM), CMP_HIDDEN ** -0.5),
        "cmp_pos_v": nrm(ks[10], (L, CMP_BLOCK, HEAD_DIM), 0.1),
        "cmp_w1_v": nrm(ks[11], (L, CMP_BLOCK * HEAD_DIM, CMP_HIDDEN), (CMP_BLOCK * HEAD_DIM) ** -0.5),
        "cmp_w2_v": nrm(ks[12], (L, CMP_HIDDEN, HEAD_DIM), CMP_HIDDEN ** -0.5),
        "gmlp_ln_g": gain(ks[13], (L, GMLP_WIDTH)),
        "gmlp_ln_b": nrm(ks[14], (L, GMLP_WIDTH), 0.02),
        "gmlp_w_s": nrm(ks[15], (L, N_GMLP_GROUPS, GMLP_CHUNK, GMLP_CHUNK), GMLP_CHUNK ** -0.5),
        "gmlp_b_s": gain(ks[16], (L, N_GMLP_GROUPS, GMLP_CHUNK)),
        "w_out": nrm(ks[17], (L, D_MODEL, D_MODEL), D_MODEL ** -0.5),
        "w_gate_up": nrm(ks[18], (L, D_MODEL, 2 * D_FF), D_MODEL ** -0.5),
        "w_down": nrm(ks[19], (L, D_FF, D_MODEL), D_FF ** -0.5),
    }

def first_block(x, rel_bias, norm_mix_pre, norm_mix_post, norm_ffn_pre, norm_ffn_post, w_in,
              cmp_pos_k, cmp_w1_k, cmp_w2_k, cmp_pos_v, cmp_w1_v, cmp_w2_v,
              gmlp_ln_g, gmlp_ln_b, gmlp_w_s, gmlp_b_s, w_out, w_gate_up, w_down):
    h = x
    for l in range(DEPTH):
        mix = nsa_gmlp_mixer(rms_norm(h, norm_mix_pre[l]), w_in[l],
                             cmp_pos_k[l], cmp_w1_k[l], cmp_w2_k[l],
                             cmp_pos_v[l], cmp_w1_v[l], cmp_w2_v[l],
                             gmlp_ln_g[l], gmlp_ln_b[l], gmlp_w_s[l], gmlp_b_s[l],
                             w_out[l], rel_bias)
        h = h + rms_norm(mix, norm_mix_post[l])
        ffn = swiglu_ffn(rms_norm(h, norm_ffn_pre[l]), w_gate_up[l], w_down[l])
        h = h + rms_norm(ffn, norm_ffn_post[l])
    return h


CHUNK = 64
EPS = 1e-6
ATTN_HEADS = 16
Q_RANK = 256
KV_RANK = 128
IDX_HEADS = 16
IDX_DIM = 64
TOPK_MAX = 256
NUM_BUCKETS = 32
MAX_DISTANCE = 128
D_INNER = 2 * D_MODEL
SSD_HEADDIM = 64
SSD_HEADS = D_INNER // SSD_HEADDIM
SSD_GROUPS = 8
D_STATE = 128
CONV_W = 4
CONV_DIM = D_INNER + 2 * SSD_GROUPS * D_STATE
D_FF_2 = -(-8 * D_MODEL // (3 * 256)) * 256
IN_SIZES = [Q_RANK, KV_RANK, IDX_DIM, IDX_HEADS, D_INNER, CONV_DIM, SSD_HEADS, D_MODEL, D_MODEL]
IN_COLS = int(sum(IN_SIZES))
IN_SPLITS = [int(v) for v in np.cumsum(IN_SIZES)[:-1]]


def rmsnorm(x, w):
    x32 = x.astype(jnp.float32)
    y = x32 * lax.rsqrt(jnp.mean(x32 * x32, axis=-1, keepdims=True) + EPS)
    return (y * w.astype(jnp.float32)).astype(x.dtype)

def t5_bucket_2(rel):
    half = NUM_BUCKETS // 2
    max_exact = half // 2
    side = jnp.where(rel > 0, half, 0)
    n = jnp.abs(rel)
    large = max_exact + (jnp.log(jnp.maximum(n, max_exact).astype(jnp.float32) / max_exact)
                         / math.log(MAX_DISTANCE / max_exact) * (half - max_exact)).astype(jnp.int32)
    large = jnp.minimum(large, half - 1)
    return side + jnp.where(n < max_exact, n, large)

def sparse_mla_attention(q_lat, kv_lat, k_idx_raw, w_idx_raw, positions,
                         q_norm, kv_norm, w_uq, w_uv, w_qidx, kidx_norm, rel_bias):
    Bsz, L, _ = q_lat.shape
    nb = L // Q_BLOCK
    k_sel_n = min(TOPK_MAX, L // 4)
    qn = rmsnorm(q_lat, q_norm)
    q = (qn @ w_uq).reshape(Bsz, L, ATTN_HEADS, KV_RANK)
    q_idx = (qn @ w_qidx).reshape(Bsz, L, IDX_HEADS, IDX_DIM)
    kv = rmsnorm(kv_lat, kv_norm)
    k_idx = rmsnorm(k_idx_raw, kidx_norm)
    w_idx = w_idx_raw * (IDX_HEADS ** -0.5 * IDX_DIM ** -0.5)
    key_chunk = positions // CHUNK
    scale = KV_RANK ** -0.5

    def to_blocks(a):
        return jnp.moveaxis(a.reshape((Bsz, nb, Q_BLOCK) + a.shape[2:]), 1, 0)

    def block_fn(args):
        q_b, qi_b, w_b, pos_b = args
        q_chunk = pos_b // CHUNK
        rel = jax.nn.relu(jnp.einsum('bqhd,bsd->bqhs', qi_b, k_idx).astype(jnp.float32))
        iscore = jnp.einsum('bqh,bqhs->bqs', w_b.astype(jnp.float32), rel)
        admissible = key_chunk[:, None, :] <= q_chunk[:, :, None]
        iscore = jnp.where(admissible, iscore, -jnp.inf)
        _, idx = lax.top_k(iscore, k_sel_n)
        kv_sel = jax.vmap(lambda kv_b, i_b: kv_b[i_b])(kv, idx)
        pos_sel = jax.vmap(lambda p_b, i_b: p_b[i_b])(positions, idx)
        valid = (pos_sel // CHUNK) <= q_chunk[..., None]
        bias = rel_bias[t5_bucket_2(pos_sel - pos_b[..., None])]
        logits = jnp.einsum('bqhc,bqkc->bhqk', q_b, kv_sel).astype(jnp.float32) * scale
        logits = logits + jnp.transpose(bias, (0, 3, 1, 2)).astype(jnp.float32)
        logits = jnp.where(valid[:, None], logits, -jnp.inf)
        probs = jax.nn.softmax(logits, axis=-1).astype(kv_sel.dtype)
        return jnp.einsum('bhqk,bqkc->bqhc', probs, kv_sel)

    o = lax.map(block_fn, (to_blocks(q), to_blocks(q_idx), to_blocks(w_idx), to_blocks(positions)))
    o = jnp.moveaxis(o, 0, 1).reshape(Bsz, L, ATTN_HEADS, KV_RANK)
    o = jnp.einsum('blhc,hcd->blhd', o, w_uv)
    return o.reshape(Bsz, L, ATTN_HEADS * HEAD_DIM)

def ssd_mixer(z, xbc, dt_raw, conv_w, conv_b, dt_bias, a_log, d_skip, ssd_norm):
    Bsz, L, _ = xbc.shape
    nc = L // CHUNK
    R = SSD_HEADS // SSD_GROUPS
    xbc = lax.conv_general_dilated(xbc, conv_w[:, None, :], window_strides=(1,),
                                   padding=[(CONV_W - 1, 0)],
                                   dimension_numbers=('NWC', 'WIO', 'NWC'),
                                   feature_group_count=CONV_DIM) + conv_b
    xbc = jax.nn.silu(xbc)
    xs, Bm, Cm = jnp.split(xbc, [D_INNER, D_INNER + SSD_GROUPS * D_STATE], axis=-1)
    dt = jax.nn.softplus((dt_raw + dt_bias).astype(jnp.float32))
    A = -jnp.exp(a_log.astype(jnp.float32))
    xh = xs.reshape(Bsz, L, SSD_HEADS, SSD_HEADDIM)
    X = (xh * dt[..., None]).reshape(Bsz, nc, CHUNK, SSD_GROUPS, R, SSD_HEADDIM)
    Bc = Bm.reshape(Bsz, nc, CHUNK, SSD_GROUPS, D_STATE)
    Cc = Cm.reshape(Bsz, nc, CHUNK, SSD_GROUPS, D_STATE)
    dA = (dt * A).reshape(Bsz, nc, CHUNK, SSD_GROUPS, R).transpose(0, 1, 3, 4, 2)
    a_cum = jnp.cumsum(dA, axis=-1)
    causal = jnp.tril(jnp.ones((CHUNK, CHUNK), dtype=bool))
    seg = jnp.where(causal, a_cum[..., :, None] - a_cum[..., None, :], -jnp.inf)
    Lmat = jnp.exp(seg)
    CB = jnp.einsum('bclgn,bcsgn->bcgls', Cc, Bc)
    y_diag = jnp.einsum('bcgls,bcgrls,bcsgrp->bclgrp', CB, Lmat, X)
    decay = jnp.exp(a_cum[..., -1:] - a_cum)
    states = jnp.einsum('bclgn,bcgrl,bclgrp->bcgrpn', Bc, decay, X)
    chunk_decay = jnp.exp(a_cum[..., -1])

    def step(h, inp):
        s_c, d_c = inp
        return h * d_c[..., None, None] + s_c, h

    h0 = jnp.zeros_like(states[:, 0])
    _, prev = lax.scan(step, h0, (jnp.moveaxis(states, 1, 0), jnp.moveaxis(chunk_decay, 1, 0)))
    prev = jnp.moveaxis(prev, 0, 1)
    y_off = jnp.einsum('bclgn,bcgrpn,bcgrl->bclgrp', Cc, prev, jnp.exp(a_cum))
    y = (y_diag + y_off).reshape(Bsz, L, SSD_HEADS, SSD_HEADDIM) + d_skip[:, None] * xh
    y = y.reshape(Bsz, L, D_INNER)
    return rmsnorm(y * jax.nn.silu(z), ssd_norm)

def second_inputs(seed: int = 0) -> dict:
    key = jax.random.key(seed)
    ks = jax.random.split(key, 32)
    nrm = lambda k, shape, s: jax.random.normal(k, shape, jnp.float32) * s
    gain = lambda k, n: 1.0 + 0.05 * jax.random.normal(k, (n,), jnp.float32)
    offset = jax.random.randint(ks[2], (BATCH, 1), 0, 16) * CHUNK
    positions = (offset + jnp.arange(SEQ, dtype=jnp.int32)[None, :]).astype(jnp.int32)
    dt0 = jnp.exp(jax.random.uniform(ks[20], (SSD_HEADS,), jnp.float32, math.log(1e-3), math.log(1e-1)))
    return {
        "x": nrm(ks[0], (BATCH, SEQ, D_MODEL), 1.0),
        "c": nrm(ks[1], (BATCH, D_MODEL), 1.0),
        "positions": positions,
        "ada_w": nrm(ks[3], (D_MODEL, 6 * D_MODEL), 0.5 * D_MODEL ** -0.5),
        "ada_b": nrm(ks[4], (6 * D_MODEL,), 0.02),
        "pre_norm_mix": gain(ks[5], D_MODEL),
        "post_norm_mix": gain(ks[6], D_MODEL),
        "pre_norm_ffn": gain(ks[7], D_MODEL),
        "post_norm_ffn": gain(ks[8], D_MODEL),
        "w_in": nrm(ks[9], (D_MODEL, IN_COLS), D_MODEL ** -0.5),
        "q_norm": gain(ks[10], Q_RANK),
        "kv_norm": gain(ks[11], KV_RANK),
        "w_uq": nrm(ks[12], (Q_RANK, ATTN_HEADS * KV_RANK), Q_RANK ** -0.5),
        "w_uv": nrm(ks[13], (ATTN_HEADS, KV_RANK, HEAD_DIM), KV_RANK ** -0.5),
        "rel_bias": nrm(ks[14], (NUM_BUCKETS, ATTN_HEADS), 0.3),
        "w_qidx": nrm(ks[15], (Q_RANK, IDX_HEADS * IDX_DIM), Q_RANK ** -0.5),
        "kidx_norm": gain(ks[16], IDX_DIM),
        "conv_w": nrm(ks[17], (CONV_W, CONV_DIM), CONV_W ** -0.5),
        "conv_b": nrm(ks[18], (CONV_DIM,), 0.02),
        "dt_bias": dt0 + jnp.log(-jnp.expm1(-dt0)),
        "a_log": jnp.log(jax.random.uniform(ks[21], (SSD_HEADS,), jnp.float32, 1.0, 16.0)),
        "d_skip": 1.0 + 0.1 * jax.random.normal(ks[22], (SSD_HEADS,), jnp.float32),
        "ssd_norm": gain(ks[23], D_INNER),
        "w_o_attn": nrm(ks[24], (ATTN_HEADS * HEAD_DIM, D_MODEL), (ATTN_HEADS * HEAD_DIM) ** -0.5),
        "w_o_ssd": nrm(ks[25], (D_INNER, D_MODEL), D_INNER ** -0.5),
        "w_out": nrm(ks[26], (D_MODEL, D_MODEL), D_MODEL ** -0.5),
        "w_ffn_in": nrm(ks[27], (D_MODEL, 2 * D_FF_2), D_MODEL ** -0.5),
        "w_ffn_out": nrm(ks[28], (D_FF_2, D_MODEL), D_FF_2 ** -0.5),
    }

def second_block(x, c, positions, ada_w, ada_b, pre_norm_mix, post_norm_mix, pre_norm_ffn,
              post_norm_ffn, w_in, q_norm, kv_norm, w_uq, w_uv, rel_bias, w_qidx, kidx_norm,
              conv_w, conv_b, dt_bias, a_log, d_skip, ssd_norm, w_o_attn, w_o_ssd, w_out,
              w_ffn_in, w_ffn_out):
    mod = (jax.nn.silu(c) @ ada_w + ada_b)[:, None, :]
    shift_m, scale_m, gate_m, shift_f, scale_f, gate_f = jnp.split(mod, 6, axis=-1)
    for _ in range(DEPTH):
        h = rmsnorm(x, pre_norm_mix) * (1.0 + scale_m) + shift_m
        proj = h @ w_in
        q_lat, kv_lat, k_idx, w_idx, z, xbc, dt_raw, g_a, g_b = jnp.split(proj, IN_SPLITS, axis=-1)
        y_a = sparse_mla_attention(q_lat, kv_lat, k_idx, w_idx, positions, q_norm, kv_norm,
                                   w_uq, w_uv, w_qidx, kidx_norm, rel_bias) @ w_o_attn
        y_b = ssd_mixer(z, xbc, dt_raw, conv_w, conv_b, dt_bias, a_log, d_skip, ssd_norm) @ w_o_ssd
        mix = (jax.nn.sigmoid(g_a) * y_a + jax.nn.sigmoid(g_b) * y_b) @ w_out
        x = x + gate_m * rmsnorm(mix, post_norm_mix)
        h2 = rmsnorm(x, pre_norm_ffn) * (1.0 + scale_f) + shift_f
        u_gate, u_up = jnp.split(h2 @ w_ffn_in, 2, axis=-1)
        f = (jax.nn.silu(u_gate) * u_up) @ w_ffn_out
        x = x + gate_f * rmsnorm(f, post_norm_ffn)
    return x


def setup_inputs(seed=0):
    out = dict(first_inputs(seed))
    for name, value in second_inputs(seed + 1).items():
        if name != "x":
            out[name + "_2"] = value
    return out


def reference(
    x, rel_bias, norm_mix_pre, norm_mix_post, norm_ffn_pre, norm_ffn_post, w_in, cmp_pos_k,
    cmp_w1_k, cmp_w2_k, cmp_pos_v, cmp_w1_v, cmp_w2_v, gmlp_ln_g, gmlp_ln_b, gmlp_w_s, gmlp_b_s,
    w_out, w_gate_up, w_down, c_2, positions_2, ada_w_2, ada_b_2, pre_norm_mix_2,
    post_norm_mix_2, pre_norm_ffn_2, post_norm_ffn_2, w_in_2, q_norm_2, kv_norm_2, w_uq_2,
    w_uv_2, rel_bias_2, w_qidx_2, kidx_norm_2, conv_w_2, conv_b_2, dt_bias_2, a_log_2, d_skip_2,
    ssd_norm_2, w_o_attn_2, w_o_ssd_2, w_out_2, w_ffn_in_2, w_ffn_out_2,
):
    x = first_block(
        x, rel_bias, norm_mix_pre, norm_mix_post, norm_ffn_pre, norm_ffn_post, w_in, cmp_pos_k,
        cmp_w1_k, cmp_w2_k, cmp_pos_v, cmp_w1_v, cmp_w2_v, gmlp_ln_g, gmlp_ln_b, gmlp_w_s,
        gmlp_b_s, w_out, w_gate_up, w_down,
    )
    return second_block(
        x, c_2, positions_2, ada_w_2, ada_b_2, pre_norm_mix_2, post_norm_mix_2, pre_norm_ffn_2,
        post_norm_ffn_2, w_in_2, q_norm_2, kv_norm_2, w_uq_2, w_uv_2, rel_bias_2, w_qidx_2,
        kidx_norm_2, conv_w_2, conv_b_2, dt_bias_2, a_log_2, d_skip_2, ssd_norm_2, w_o_attn_2,
        w_o_ssd_2, w_out_2, w_ffn_in_2, w_ffn_out_2,
    )


_drawn_inputs = setup_inputs


def setup_inputs(seed=0):
    import zlib

    import numpy as np

    out = dict(_drawn_inputs(seed))
    spreads = {}
    factors = {'cmp_pos_k': 8.0,
     'gmlp_ln_b': 6.46,
     'ada_b_2': 2.821,
     'pre_norm_mix_2': 3.737,
     'post_norm_mix_2': 6.491,
     'pre_norm_ffn_2': 4.632,
     'post_norm_ffn_2': 6.746,
     'q_norm_2': 8.0,
     'kv_norm_2': 8.0,
     'rel_bias_2': 7.071,
     'kidx_norm_2': 8.0,
     'conv_b_2': 8.0,
     'd_skip_2': 200.0,
     'ssd_norm_2': 6.615}
    for name, (base, spread) in spreads.items():
        noise = np.random.default_rng([zlib.crc32(name.encode()), seed]).standard_normal(out[name].shape)
        drawn = base * np.exp(spread * noise) if base else spread * noise
        out[name] = jnp.asarray(drawn.astype(out[name].dtype))
    for name, factor in factors.items():
        out[name] = (out[name] * factor).astype(out[name].dtype)
    return out
```

```python
from contextlib import ExitStack

import numpy as np

import concourse.bass as bass
from concourse import mybir

F32 = mybir.dt.float32
F32R = mybir.dt.float32r
BF16 = mybir.dt.bfloat16
I32 = mybir.dt.int32
ALU = mybir.AluOpType
ACT = mybir.ActivationFunctionType
AX = mybir.AxisListType

P = 128
S = 256
TT = S // P
D = 1024
KD = D // P
NEG = -1.0e30
NEG_TAKEN = -3.0e38
H1, G1, DH = 8, 2, 64
KV1 = G1 * DH
NCMP, CSTRIDE, CBLOCK = 15, 16, 32
NCP = 16
FF = 2816
KF = FF // P
GW = 512
T5_FIRST = (0, 1, 2, 3, 4, 5, 6, 7, 8, 9, 10, 11, 12, 13, 14, 15, 16, 19, 21, 24, 27, 31, 35, 40,
            46, 52, 59, 67, 77, 87, 99, 113)
TOEP = 384
H2, CKV = 16, 128
QR = 256
TOPK = 64
T5B_FIRST = (0, 1, 2, 3, 4, 5, 6, 7, 8, 12, 16, 23, 32, 46, 64, 91)
QT = 8
NTILE = S // QT
DI = 2048
KI = DI // P
HS, NG, DS = 32, 8, 128
KX = 4096 // P
CONV = 4
RING = 4
UNIT = 1024
AHEAD = 2


def shape_constants():
    r = np.arange(P)
    ident = np.eye(P, dtype=np.float32)
    tri = (r[:, None] <= r[None, :]).astype(np.float32)
    upper = (r[:, None] > r[None, :]).astype(np.float32)
    ones = np.ones((P, P), np.float32)
    lo, hi = np.zeros(32), np.zeros(32)
    for n in range(16):
        last = T5B_FIRST[n + 1] - 1 if n < 15 else 1.0e9
        lo[n], hi[n] = -last, -T5B_FIRST[n]
        lo[16 + n], hi[16 + n] = T5B_FIRST[n], last
    lo[16], hi[16] = 2.0e9, -2.0e9
    cols = np.zeros((P, 4), np.float32)
    cols[:, 0] = np.tile(lo, 4)
    cols[:, 1] = np.tile(hi, 4)
    cols[:, 2] = r >= CBLOCK - 1
    mats = np.concatenate([ident, upper, tri, ones, tri, ident[::-1], cols], axis=1)
    hot = np.zeros((32, 2 * S), np.float32)
    for c in range(S):
        hot[max(b for b in range(32) if T5_FIRST[b] <= S - 1 - c), c] = 1.0
    return np.ascontiguousarray(mats, np.float32), hot


def at(i, per, const):
    return const if i is None else i * per + const


def two_block_kernel(nc, a, out):
    ctx = ExitStack()
    with ctx:
        _emit(nc, ctx, a, out)


def _emit(nc, ctx, a, out):
    def sem(name):
        return ctx.enter_context(nc.semaphore(name))

    def sb(name, shape, dt=F32, where=ctx):
        return where.enter_context(nc.sbuf_tensor(name, shape, dt))

    bank = [ctx.enter_context(nc.psum_tensor(f"bank{i}", [P, 512], F32)) for i in range(8)]
    bank3 = [b[:, :].rearrange("p (a n) -> p a n", a=2) for b in bank]

    w_raw = sb("w_raw", [P, RING, UNIT])
    w_hi = sb("w_hi", [P, RING, UNIT], F32R)
    w_lo = sb("w_lo", [P, RING, UNIT], F32R)
    h_hi = sb("h_hi", [P, KD, S], F32R)
    h_lo = sb("h_lo", [P, KD, S], F32R)
    ff_hi = sb("ff_hi", [P, KF, S], F32R)
    ff_lo = sb("ff_lo", [P, KF, S], F32R)
    xT = sb("xT", [P, KD, S])
    work = sb("work", [P, KD, S])
    mT = sb("mT", [P, KD, S])
    mats = sb("mats", [P, 6 * P + 4])
    ident, upper, tri, ones = (mats[:, i * P:(i + 1) * P] for i in range(4))
    tri_ones, tri_ones_tri, flip = mats[:, 2 * P:4 * P], mats[:, 2 * P:5 * P], mats[:, 5 * P:6 * P]
    range_lo, range_hi, has_block = (mats[:, 6 * P + i:6 * P + i + 1] for i in range(3))
    cols = sb("cols", [P, 3, P])
    rstd = sb("rstd", [P, S])
    var_sd = sb("var_sd", [P, 2, S])
    var, sd = var_sd[:, 0, :], var_sd[:, 1, :]
    mod = sb("mod", [P, 48])
    gains = sb("gains", [P, 4, KD])
    c_silu = sb("c_silu", [P, KD])

    p1 = ExitStack()
    x_tok = sb("x_tok", [P, TT, D], F32, p1)
    table1 = sb("table1", [32, H1], F32, p1)
    toep = sb("toep", [P, H1, TOEP], F32, p1)
    w_gates = sb("w_gates", [P, KD, 24], F32, p1)
    gates = sb("gates", [P, TT, 24], F32, p1)
    qT = sb("qT", [P, H1 // 2, S], F32, p1)
    kdup = sb("kdup", [P, G1, 2, S], F32, p1)
    v_tok = sb("v_tok", [P, TT, 2 * KV1], F32, p1)
    tblk_hi = sb("tblk_hi", [P, 2, 16, 2 * NCMP], F32R, p1)
    tblk_lo = sb("tblk_lo", [P, 2, 16, 2 * NCMP], F32R, p1)
    tblk = sb("tblk", [P, 2, 16, 2 * NCMP], F32, p1)
    hid = sb("hid", [P, 2, 2, 2 * NCMP], F32, p1)
    w2 = sb("w2", [P, 2, 2, DH], F32, p1)
    kc_dup = sb("kc_dup", [P, 2 * NCMP], F32, p1)
    vc = sb("vc", [NCMP, G1, DH], F32, p1)
    zu = sb("zu", [P, 4, S], F32, p1)
    gv = sb("gv", [P, TT, GW], F32, p1)
    ln_st = sb("ln_st", [P, TT, 8], F32, p1)
    ln_bn = sb("ln_bn", [P, TT, 6], F32, p1)
    wsT = sb("wsT", [P, 8, P], F32, p1)
    bs = sb("bs", [P, 4, P], F32, p1)
    probs = sb("probs", [P, 2, NCP + 2 * S], F32, p1)
    pT = sb("pT", [P, 2, 5, P], F32, p1)
    rows = tblk[:, :, :, :].rearrange("p n t j -> p (n t j)")[:, 0:3 * P].rearrange("p (t n) -> p t n", t=3)
    hot = zu[:, :, :].rearrange("p t s -> p (t s)")[0:32, 0:2 * S]
    bias_row = wsT[:, :, :].rearrange("p g t -> p (g t)")[0:H1, 0:2 * S]
    ln_g, ln_b = (probs[:, :, :].rearrange("p b n -> p (b n)")[:, i * GW:(i + 1) * GW] for i in (0, 1))
    ws = pT[:, :, :, :].rearrange("p b k q -> p (b k) q")[:, 0:8, :]
    st1 = sb("st1", [P, 2, 4, 4], F32, p1)
    mix = x_tok[:, :, :].rearrange("p t d -> p (t d)").rearrange("p (k s) -> p k s", k=KD)
    hankel_a = mT[:, :, :].rearrange("p k s -> p (k s)")[:, 0:5 * TOEP].rearrange("p (h f) -> p h f", h=5)
    hankel_b = x_tok[:, :, :].rearrange("p t d -> p (t d)")[:, 0:3 * TOEP].rearrange("p (h f) -> p h f", h=3)
    bias_dram = nc.dram_tensor("bias_dram", [H1, 2 * S], F32, kind="Internal").ap()
    p1.close()

    pf = ExitStack()
    ada_raw = sb("ada_raw", [P, 4, UNIT], F32, pf)
    ada_acc = sb("ada_acc", [P, 6 * D], F32, pf)
    silu_g = sb("silu_g", [P, 2, S], F32, pf)
    ffv = sb("ffv", [P, 2, S], F32, pf)
    pf.close()

    p2 = ExitStack()
    szT = sb("szT", [P, KI, S], F32, p2)
    dtd = sb("dtd", [P, 2, TT, HS], F32, p2)
    dt_sc = sb("dt_sc", [P, 3, TT, HS], F32, p2)
    dt_bias = sb("dt_bias", [P, HS], F32, p2)
    a_row = sb("a_row", [P, HS], F32, p2)
    w_dt = sb("w_dt", [P, KD, HS], F32, p2)
    skip = sb("skip", [P, KI], F32, p2)
    pa = ExitStack()
    uq = sb("uq", [P, S, H2], F32, pa)
    oT = sb("oT", [P, H2, S], F32, pa)
    qi = mT
    oT_flat = oT[:, :, :].rearrange("p h s -> p (h s)")
    qn = oT_flat[:, 0:512].rearrange("p (t n) -> p t n", t=TT)
    rn = oT_flat[:, 512:1024].rearrange("p (k s) -> p k s", k=2)
    kin = oT_flat[:, 1024:1280].rearrange("p (t a d) -> p t a d", t=TT, a=2)
    junk = oT_flat[:, 1280:1280 + 6 * QR].rearrange("p (n k) -> p n k", n=6)
    mT_flat = mT[:, :, :].rearrange("p k s -> p (k s)")
    pick = mT_flat[:, 0:1024].bitcast(BF16)
    onehot = mT_flat[:, 1024:1536].bitcast(BF16).rearrange("p (b c s) -> p b c s", b=2, c=2)
    in_lo = mT_flat[:, 1536:1792].bitcast(BF16).rearrange("p (c s) -> p c s", c=2)
    work_flat = work[:, :, :].rearrange("p k s -> p (k s)")
    p2buf = work_flat[:, 0:512].rearrange("p (b s) -> p b s", b=2)
    p2T = work_flat[:, 512:1024].rearrange("p (b k r) -> p b k r", b=2, k=2)
    w_uv = work_flat[:, 1024:2048].rearrange("p (h d) -> p h d", h=H2)
    relu_s = work[:, :, :].rearrange("p (b h) k -> p b h k", b=2)
    kv = sb("kv", [P, TT, CKV], F32, pa)
    kv_gain = sb("kv_gain", [P, CKV], F32, pa)
    st2 = sb("st2", [P, TT, 12], F32, pa)
    widx = sb("widx", [P, TT, 16], F32, pa)
    kvT = sb("kvT", [P, S], F32, pa)
    kiT = sb("kiT", [P, S], F32, pa)
    isc = sb("isc", [P, TT, S], F32, pa)
    top8 = sb("top8", [P, 8], F32, pa)
    pos_i = sb("pos_i", [P, S + TT], I32, pa)
    pos_f = sb("pos_f", [P, S + TT], F32, pa)
    last_i = sb("last_i", [P, TT], I32, pa)
    last_f = sb("last_f", [P, TT], F32, pa)
    shut = sb("shut", [P, TT, S], F32, pa)
    mask = sb("mask", [P, TT, S], BF16, pa)
    own_pos = sb("own_pos", [P, 2, S // 4], F32, pa)
    tab2 = sb("tab2", [P, H2], F32, pa)
    tab_r = sb("tab_r", [P, H2], F32, pa)
    tab_s = sb("tab_s", [P, 3, H2], BF16, pa)
    tab_b = sb("tab_b", [P, 2, 3, P], BF16, pa)
    st3 = sb("st3", [P, 2, 4], F32, pa)
    pa.close()
    pb = ExitStack()
    xsT = sb("xsT", [P, KI, S], F32, pb)
    x_dt = sb("x_dt", [P, TT, DI], F32, pb)
    bT = sb("bT", [P, NG, S], F32, pb)
    cT = sb("cT", [P, NG, S], F32, pb)
    cbm = var_sd[:, :, :].rearrange("p a s -> p (a s)")[:, 0:384]
    pb.close()
    p2.close()
    ud = work_flat[:, 0:512].rearrange("p (b t s) -> p b t s", b=2, t=2)
    decay = work_flat[:, 512:1280].rearrange("p (b n) -> p b n", b=2)
    m_buf = work_flat[:, 1280:2048].rearrange("p (b n) -> p b n", b=2)
    out_tok = mT_flat.rearrange("p (t d) -> p t d", t=TT)
    ysq = x_dt[:, :, :].rearrange("p t d -> p (t d)").rearrange("p (k s) -> p k s", k=KI)

    class Stream:

        units, blocks, act_blocks, dve_blocks = 0, 0, 0, 0

        def __init__(self, n, ks, reader):
            self.n, self.ks, self.reader = n, ks, reader
            self.u0, self.b0 = Stream.units, Stream.blocks
            self.act0, self.dve0 = Stream.act_blocks, Stream.dve_blocks
            Stream.units += n * len(ks)
            Stream.blocks += n
            Stream.act_blocks += n * (reader == "act") + (n // 2) * (reader == "pair")
            Stream.dve_blocks += n * (reader == "dve") + (n // 2) * (reader == "pair")

    s_kc = Stream(1, (4, 4), "dve")
    s_in = Stream(8, (4, 4), "act")
    s_cmp = Stream(2, (4, 4, 4, 4), "act")
    s_wo = Stream(4, (4, 4), "act")
    s_gu = Stream(22, (4, 4), "pair")
    s_dn = Stream(4, (4, 4, 4, 4, 4, 2), "act")
    s_lat = Stream(2, (4, 4), "dve")
    s_uq = Stream(8, (2,), "act")
    s_qi = Stream(4, (2,), "act")
    s_z = Stream(8, (4, 4), "act")
    s_ga = Stream(4, (4, 4), "act")
    s_oa = Stream(4, (4, 4), "dve")
    s_xbc = Stream(16, (4, 4), "dve")
    s_gb = Stream(4, (4, 4), "act")
    s_os = Stream(4, (4, 4, 4, 4), "dve")
    s_wo2 = Stream(4, (4, 4), "act")
    s_gu2 = Stream(22, (4, 4), "pair")
    s_dn2 = Stream(4, (4, 4, 4, 4, 4, 2), "act")
    n_units = Stream.units

    landed = [sem(f"landed{i}") for i in range(RING)]
    hi_ready, lo_ready, unit_used = sem("hi_ready"), sem("lo_ready"), sem("unit_used")
    act_read, dve_read = sem("act_read"), sem("dve_read")
    act_own, dve_own, pool_own = sem("act_own"), sem("dve_own"), sem("pool_own")
    consts_in, rows_in, x_in, hot_in = sem("consts_in"), sem("rows_in"), sem("x_in"), sem("hot_in")
    gates_in, mlp_in, gmlp_in, ln_in = sem("gates_in"), sem("mlp_in"), sem("gmlp_in"), sem("ln_in")
    bias_out, toep_in, toep_mm, toep_ready = (sem("bias_out"), sem("toep_in"), sem("toep_mm"),
                                              sem("toep_ready"))
    ada_in = [sem(f"ada_in{i}") for i in range(4)]
    lat_in, pos_in, tab_in, ssd_in, uv_in = (sem("lat_in"), sem("pos_in"), sem("tab_in"),
                                             sem("ssd_in"), sem("uv_in"))
    out_done = sem("out_done")
    rows_T, cols_ready, x_T, x_act, x_dve = (sem("rows_T"), sem("cols_ready"), sem("x_T"),
                                             sem("x_act"), sem("x_dve"))
    bias_mm, bias_ready = sem("bias_mm"), sem("bias_ready")
    sq_ready, ss_ready, var_ready, sd_ready = (sem("sq_ready"), sem("ss_ready"), sem("var_ready"),
                                               sem("sd_ready"))
    h_ready, h_hi_ready, h_lo_ready = sem("h_ready"), sem("h_hi_ready"), sem("h_lo_ready")
    x_ready = sem("x_ready")
    gate_mm, gates_act, gates_ready = sem("gate_mm"), sem("gates_act"), sem("gates_ready")
    tblk_hi_ready, tblk_lo_ready = sem("tblk_hi_ready"), sem("tblk_lo_ready")
    hid_ready, kcvc_mm, kcvc_ready = sem("hid_ready"), sem("kcvc_mm"), sem("kcvc_ready")
    ws_T, wsT_ready, ln_var, ln_sd, zv_ready, sv_mm, mix_gm = (
        sem("ws_T"), sem("wsT_ready"), sem("ln_var"), sem("ln_sd"), sem("zv_ready"), sem("sv_mm"),
        sem("mix_gm"))
    lg_mm, max_ready, exp_ready, pn_ready, pT_mm, pT_ready, pv_mm, att_ready = (
        sem("lg_mm"), sem("max_ready"), sem("exp_ready"), sem("pn_ready"), sem("pT_mm"),
        sem("pT_ready"), sem("pv_mm"), sem("att_ready"))
    ff_hi_ready, ff_lo_ready = sem("ff_hi_ready"), sem("ff_lo_ready")
    ada_used, ada_mm, c_ready, mod_ready = sem("ada_used"), sem("ada_mm"), sem("c_ready"), sem("mod_ready")
    lat_sq, lat_var, lat_sd, lat_ready, lat_T, qn_ready, qn_hi, qn_lo, ki_ready = (
        sem("lat_sq"), sem("lat_var"), sem("lat_sd"), sem("lat_ready"), sem("lat_T"),
        sem("qn_ready"), sem("qn_hi"), sem("qn_lo"), sem("ki_ready"))
    ix_mm, ix_relu, ix_sum, mask_ready, pick_ready, tab_ready = (
        sem("ix_mm"), sem("ix_relu"), sem("ix_sum"), sem("mask_ready"), sem("pick_ready"),
        sem("tab_ready"))
    hot_ready, lt_mm, lt_max, lt_exp, lt_p, lt_T, lt_pT, lt_pv, lt_o = (
        sem("hot_ready"), sem("lt_mm"), sem("lt_max"), sem("lt_exp"), sem("lt_p"), sem("lt_T"),
        sem("lt_pT"), sem("lt_pv"), sem("lt_o"))
    uv_mm, uv_hi, uv_lo = sem("uv_mm"), sem("uv_hi"), sem("uv_lo")
    dt_mm, dt_a, dt_b, dt_ready, xbc_ready = (
        sem("dt_mm"), sem("dt_a"), sem("dt_b"), sem("dt_ready"), sem("xbc_ready"))
    xs_T, xs_ready, cb_mm, cb_ready, ud_ready, seg_mm, dec_ready, m_mat, y_mm, y_ready = (
        sem("xs_T"), sem("xs_ready"), sem("cb_mm"), sem("cb_ready"), sem("ud_ready"),
        sem("seg_mm"), sem("dec_ready"), sem("m_mat"), sem("y_mm"), sem("y_ready"))
    y_gain, y_hi, y_lo, mix2_ready = sem("y_gain"), sem("y_hi"), sem("y_lo"), sem("mix2_ready")
    out_T, out_act, out_ready = sem("out_T"), sem("out_act"), sem("out_ready")

    C_MIX, C_MIXP, C_FFN, C_FFNP, C_MIX2, C_MIXP2, C_FFN2, C_FFNP2, C_C = (8 * i for i in range(9))
    C_SSD, C_CONVB, C_QN, C_KI = 72, 88, 120, 122
    R_USED = (123, 128, 80)
    ADA_B, POS_K, POS_V = 0, 48, 64

    def col(tile, c):
        return cols[:, tile, c:c + 1]

    def fill_rows():
        def v(name):
            x = a[name]
            return (x if len(x.shape) == 1 else x.rearrange("a n -> (a n)")).rearrange(
                "(t p) -> t p", p=P)
        for c, name in ((C_MIX, "norm_mix_pre"), (C_MIXP, "norm_mix_post"), (C_FFN, "norm_ffn_pre"),
                        (C_FFNP, "norm_ffn_post"), (C_MIX2, "pre_norm_mix_2"),
                        (C_MIXP2, "post_norm_mix_2"), (C_FFN2, "pre_norm_ffn_2"),
                        (C_FFNP2, "post_norm_ffn_2"), (C_C, "c_2"), (C_SSD, "ssd_norm_2"),
                        (C_CONVB, "conv_b_2"), (C_QN, "q_norm_2")):
            x = v(name)
            yield rows[c:c + x.shape[0], 0, :], x
        ki = a["kidx_norm_2"].rearrange("(a n) -> a n", a=1)
        yield rows[C_KI:C_KI + 1, 0, 0:64], ki
        yield rows[C_KI:C_KI + 1, 0, 64:128], ki
        yield rows[:, 1, :], a["conv_w_2"].rearrange("w (t p) -> (w t) p", p=P)
        yield rows[0:48, 2, :], v("ada_b_2")
        yield rows[POS_K:POS_K + 16, 2, :], a["cmp_pos_k"][0].rearrange("(t a) d -> t (a d)", a=2)
        yield rows[POS_V:POS_V + 16, 2, :], a["cmp_pos_v"][0].rearrange("(t a) d -> t (a d)", a=2)

    n_rows_dma = 18

    w_in, w_in2 = a["w_in"][0], a["w_in_2"]
    TILES1 = [(h, qt) for hp in range(H1 // 2) for qt in range(TT) for h in (2 * hp, 2 * hp + 1)]

    block = ctx.enter_context(nc.Block())

    @block.sync
    def _(sp):
        sp.dma_start(x_tok[:, :, :], a["x"][0].rearrange("(t p) d -> p t d", p=P)).then_inc(x_in, 16)

        def load(i, per, u, src, nk, ncol, part=None):
            dst = w_raw[:, u % RING, 0:nk * ncol].rearrange("p (k c) -> p k c", k=nk)
            if u >= RING:
                sp.wait_ge(hi_ready, at(i, per, u - RING + 1))
                sp.wait_ge(lo_ready, at(i, per, u - RING + 1))
            sp.dma_start(dst, src.rearrange("(k p) c -> p k c", p=P)).then_inc(landed[u % RING], 16)

        def load_block(st, b, w, c0, i=None, per=0, ci=0, ncol=256):
            k, u = 0, st.u0 + b * len(st.ks)
            for nk in st.ks:
                load(i, per, u, w[k * P:(k + nk) * P, bass.ds(at(i, ci, c0), ncol)], nk, ncol)
                k += nk
                u += 1

        def load_stream(st, w, c0):
            n = 2 * len(st.ks)
            with sp.Fori(0, st.n // 2) as i:
                load_block(st, 0, w, c0, i, n, 512)
                load_block(st, 1, w, c0 + 256, i, n, 512)

        def load_pairs(st, w, half):
            with sp.Fori(0, st.n // 2) as i:
                load_block(st, 0, w, 0, i, 2 * len(st.ks), 256)
                load_block(st, 1, w, half, i, 2 * len(st.ks), 256)

        load_block(s_kc, 0, w_in, 512)
        load_block(s_in, 0, w_in, 768)
        load_block(s_in, 1, w_in, 0)
        load_block(s_in, 2, w_in, 256)
        load_block(s_in, 3, w_in, 1024)
        load_block(s_in, 4, w_in, 1816)
        load_block(s_in, 5, w_in, 2072)
        load_block(s_in, 6, w_in, 1304)
        load_block(s_in, 7, w_in, 1560)
        load_block(s_cmp, 0, a["cmp_w1_k"][0], 0)
        load_block(s_cmp, 1, a["cmp_w1_v"][0], 0)
        load_stream(s_wo, a["w_out"][0], 0)
        load_pairs(s_gu, a["w_gate_up"][0], FF)
        load_stream(s_dn, a["w_down"][0], 0)
        load_block(s_lat, 0, w_in2, 0)
        load_block(s_lat, 1, w_in2, 256, ncol=208)
        for b in range(s_uq.n):
            load_block(s_uq, b, a["w_uq_2"], 256 * b)
        for b in range(s_qi.n):
            load_block(s_qi, b, a["w_qidx_2"], 256 * b)
        load_stream(s_z, w_in2, 464)
        load_stream(s_ga, w_in2, 6640)
        load_stream(s_oa, a["w_o_attn_2"], 0)
        load_stream(s_xbc, w_in2, 2512)
        load_stream(s_gb, w_in2, 7664)
        load_stream(s_os, a["w_o_ssd_2"], 0)
        load_stream(s_wo2, a["w_out_2"], 0)
        load_pairs(s_gu2, a["w_ffn_in_2"], FF)
        load_stream(s_dn2, a["w_ffn_out_2"], 0)
        for t in range(TT):
            sp.wait_ge(out_act, t + 1)
            sp.wait_ge(out_ready, t + 1)
            sp.dma_start(out[0, t * P:(t + 1) * P, :], out_tok[:, t, :]).then_inc(out_done, 16)
        sp.wait_ge(out_done, 16 * TT)

    @block.gpsimd
    def _(pool):
        pool.dma_start(mats[:, :], a["shape_mats"]).then_inc(consts_in, 16)
        n = 0
        for dst, src in fill_rows():
            pool.dma_start(dst, src).then_inc(rows_in, 16)
            n += 1
        assert n == n_rows_dma
        pool.dma_start(hot[:, :], a["shape_hot"]).then_inc(hot_in, 16)
        pool.dma_start(table1[:, :], a["rel_bias"]).then_inc(hot_in, 16)
        pool.dma_start(w_gates[:, :, :], w_in[:, 1280:1304].rearrange("(k p) c -> p k c", p=P)
                       ).then_inc(gates_in, 16)
        for n, name in enumerate(("cmp_w2_k", "cmp_w2_v")):
            pool.dma_start(w2[:, n, :, :], a[name][0].rearrange("(k p) c -> p k c", p=P)
                           ).then_inc(mlp_in, 16)
        pool.dma_start(ws[:, :, :], a["gmlp_w_s"][0].rearrange("g t s -> t g s")).then_inc(gmlp_in, 16)
        for j in range(2):
            pool.dma_start(bs[j * 64:j * 64 + 64, :, :],
                           bass.AP(a["gmlp_b_s"].tensor, j * P, [[0, 64], [2 * P, 4], [1, P]])
                           ).then_inc(gmlp_in, 16)
        for t, name in ((ln_g, "gmlp_ln_g"), (ln_b, "gmlp_ln_b")):
            pool.dma_start(t[:, :], bass.AP(a[name].tensor, 0, [[0, P], [1, GW]])).then_inc(ln_in, 16)
        pool.wait_ge(bias_ready, 1)
        pool.dma_start(bias_dram, bias_row[:, :]).then_inc(bias_out, 16)
        pool.wait_ge(bias_out, 16)
        pool.wait_ge(x_T, 2)
        for h0, h1, dst in ((0, 5, hankel_a), (5, H1, hankel_b)):
            pool.dma_start(dst, bass.AP(bias_dram.tensor, h0 * 2 * S, [[1, P], [2 * S, h1 - h0], [1, TOEP]])
                           ).then_inc(toep_in, 16)
        pool.wait_ge(x_ready, 1)
        ada = a["ada_w_2"].rearrange("(k p) c -> p k c", p=P)

        def load_ada(i, per, c):
            for j in range(4):
                if c or i is not None:
                    pool.wait_ge(ada_used, at(i, per, 8 * c + 2 * j - 6))
                pool.dma_start(ada_raw[:, j, :].rearrange("p (k c) -> p k c", k=2),
                               ada[:, 2 * j:2 * j + 2, bass.ds(at(i, 512, 512 * c), 512)]
                               ).then_inc(ada_in[j], 16)

        load_ada(None, 0, 0)
        with pool.Fori(0, 11) as i:
            load_ada(i, 8, 1)
        pool.wait_ge(x_ready, 2)
        pool.wait_ge(mod_ready, 1)
        pool.dma_start(kv_gain[:, :], bass.AP(a["kv_norm_2"].tensor, 0, [[0, P], [1, CKV]])).then_inc(lat_in, 16)
        pool.dma_start(pos_i[:, 0:S], bass.AP(a["positions_2"].tensor, 0, [[0, P], [1, S]])).then_inc(pos_in, 16)
        pool.dma_start(pos_i[:, S:S + TT], a["positions_2"][0].rearrange("(t p) -> p t", p=P),
                       allow_slow_non_contiguous=True).then_inc(pos_in, 16)
        for j in range(4):
            pool.dma_start(tab2[32 * j:32 * j + 32, :], a["rel_bias_2"]).then_inc(tab_in, 16)
        pool.dma_start(w_dt[:, :, :], w_in2[:, 6608:6640].rearrange("(k p) c -> p k c", p=P)).then_inc(ssd_in, 16)
        pool.dma_start(dt_bias[:, :], bass.AP(a["dt_bias_2"].tensor, 0, [[0, P], [1, HS]])).then_inc(ssd_in, 16)
        pool.dma_start(a_row[:, :], bass.AP(a["a_log_2"].tensor, 0, [[0, P], [1, HS]])).then_inc(ssd_in, 16)
        for j in range(2):
            pool.dma_start(skip[64 * j:64 * j + 64, :],
                           bass.AP(a["d_skip_2"].tensor, j, [[0, 64], [2, KI]]),
                           allow_slow_non_contiguous=True).then_inc(ssd_in, 16)
        pool.wait_ge(ix_sum, 8)
        pool.dma_start(w_uv[:, :, :], a["w_uv_2"].rearrange("h c d -> c h d")).then_inc(uv_in, 16)
        pool.memset(pick[:, :], 1.0).then_inc(pool_own, 1)
        pool.wait_ge(pool_own, 1)
        pool.affine_select(out=pick[:, :], in_=pick[:, :], pattern=[[1, 16 * P]], compare_op=ALU.is_ge,
                           fill=0.0, base=0, channel_multiplier=-16).then_inc(pool_own, 1)
        pool.wait_ge(pool_own, 2)
        pool.affine_select(out=pick[:, :], in_=pick[:, :], pattern=[[-1, 16 * P]], compare_op=ALU.is_ge,
                           fill=0.0, base=15, channel_multiplier=16).then_inc(pick_ready, 1)
        pool.wait_ge(dt_ready, 1)
        for h in range(HS):
            if h >= 2:
                pool.wait_ge(seg_mm, h - 1)
            for t in range(TT):
                ins = pool.tensor_scalar(ud[:, h % 2, t, :], upper, dtd[:, 1, t, h:h + 1], None, ALU.mult)
            ins.then_inc(ud_ready, 1)

    @block.scalar
    def _(act):
        own, done_units = [0], [0]

        def link(ins):
            own[0] += 1
            ins.then_inc(act_own, 1)
            act.wait_ge(act_own, own[0])

        def split(i, per, u, n=UNIT):
            act.wait_ge(landed[u % RING], at(i, 4 * per, 16 * (u // RING + 1)))
            if u >= RING:
                act.wait_ge(unit_used, at(i, per, u - RING + 1))
            act.activation(w_hi[:, u % RING, 0:n], w_raw[:, u % RING, 0:n], ACT.Copy).then_inc(hi_ready, 1)

        def split_to(u_end):
            while done_units[0] < min(u_end, n_units):
                split(None, 0, done_units[0])
                done_units[0] += 1

        def before_block(st, b):
            end = st.u0 + (b + 1) * len(st.ks)
            split_to(end + AHEAD)
            act.wait_ge(unit_used, end)

        def loop_block(st, b, i, blocks_per_turn=2):
            n = len(st.ks)
            for j in range(n):
                split(i, n * blocks_per_turn, st.u0 + b * n + AHEAD + j)
            act.wait_ge(unit_used, at(i, n * blocks_per_turn, st.u0 + (b + 1) * n))

        def end_loop(st):
            done_units[0] = st.u0 + st.n * len(st.ks) + AHEAD

        def square(n, ready, value, src):
            act.wait_ge(ready, value)
            act.activation(work[:, :, :], src, ACT.Square).then_inc(sq_ready, 1)

        def root(n):
            act.wait_ge(var_ready, n)
            act.activation(sd, var, ACT.Sqrt).then_inc(sd_ready, 1)

        def operand_hi(n):
            act.wait_ge(h_ready, n)
            act.activation(h_hi[:, :, :], work[:, :, :], ACT.Copy).then_inc(h_hi_ready, 1)

        def read_m(st):
            with act.Fori(0, st.n // 2) as i:
                for b in range(2):
                    loop_block(st, b, i)
                    ins = act.activation(mT[:, bass.ds(at(i, 4, 2 * b), 2), :],
                                         bank3[(st.b0 + b) % 2], ACT.Copy)
                    ins.then_inc(act_read, 1)
            end_loop(st)
            act.wait_ge(act_read, st.act0 + st.n)

        def read_pairs(st):
            with act.Fori(0, st.n // 2) as i:
                loop_block(st, 0, i)
                act.wait_ge(dve_read, at(i, 1, st.dve0))
                act.activation(silu_g[:, :, :], bank3[st.b0 % 2], ACT.Silu).then_inc(act_read, 1)
                for j in range(2):
                    split(i, 4, st.u0 + 4 + j)
                act.wait_ge(dve_read, at(i, 1, st.dve0 + 1))
                act.activation(ff_hi[:, bass.ds(at(i, 2, 0), 2), :], ffv[:, :, :], ACT.Copy
                               ).then_inc(ff_hi_ready, 1)
            end_loop(st)

        act.wait_ge(x_T, 1)
        for j in (0, 1):
            ins = act.activation(xT[:, 2 * j:2 * j + 2, :], bank3[2 + j], ACT.Copy)
        ins.then_inc(x_act, 1)
        act.wait_ge(x_act, 1)
        square(1, x_dve, 1, xT[:, :, :])
        split_to(AHEAD)
        root(1)
        operand_hi(1)
        split_to(s_kc.u0 + 2 + AHEAD)
        def read_kv(b, br):
            before_block(s_in, b)
            src = bank3[(s_in.b0 + b) % 2]
            for g in range(G1):
                for half in range(2):
                    act.activation(kdup[64 * half:64 * half + 64, g, br, :],
                                   src[64 * g:64 * g + 64, 0, :], ACT.Copy)
            act.activation(v_tok[:, :, br * KV1:(br + 1) * KV1],
                           src[:, 1, :].rearrange("p (t d) -> p t d", t=TT), ACT.Copy
                           ).then_inc(act_read, 1)

        read_kv(0, 0)
        for b in (1, 2):
            before_block(s_in, b)
            act.activation(qT[:, 2 * b - 2:2 * b, :], bank3[(s_in.b0 + b) % 2], ACT.Copy,
                           scale=DH ** -0.5).then_inc(act_read, 1)
        read_kv(3, 1)
        for b in (4, 5):
            before_block(s_in, b)
            act.activation(gv[:, :, 256 * (b - 4):256 * (b - 3)], bank3[(s_in.b0 + b) % 2],
                           ACT.Gelu_apprx_tanh).then_inc(act_read, 1)
        for b in (6, 7):
            before_block(s_in, b)
            act.activation(zu[:, 2 * (b - 6):2 * (b - 5), :], bank3[(s_in.b0 + b) % 2],
                           ACT.Gelu_apprx_tanh).then_inc(act_read, 1)
        act.wait_ge(dve_read, 1)
        act.activation(tblk_hi[:, :, :, :], tblk[:, :, :, :], ACT.Copy).then_inc(tblk_hi_ready, 1)
        for b in range(2):
            before_block(s_cmp, b)
            hid_bank = bank[(s_cmp.b0 + b) % 2][:, 0:4 * NCMP].rearrange("p (m n) -> p m n", m=2)
            act.activation(hid[:, b, :, :], hid_bank, ACT.Gelu_apprx_tanh).then_inc(act_read, 1)
        act.wait_ge(gate_mm, 1)
        act.activation(gates[:, :, :], bank[7][:, 0:48].rearrange("p (t n) -> p t n", t=TT),
                       ACT.Sigmoid).then_inc(gates_act, 1)
        act.wait_ge(ln_var, 1)
        act.activation(ln_st[:, :, 2:3], ln_st[:, :, 1:2], ACT.Sqrt).then_inc(ln_sd, 1)
        act.wait_ge(kcvc_mm, 1)
        act.activation(kc_dup[:, :], bank[6][:, 0:2 * NCMP], ACT.Copy)
        act.activation(vc[:, :, :], bank[6][0:NCMP, 128:256].rearrange("p (g d) -> p g d", g=2),
                       ACT.Copy).then_inc(kcvc_ready, 1)
        for n in range(len(TILES1) + 1):
            if n < len(TILES1):
                nk = P * (TILES1[n][1] + 1)
                act.wait_ge(max_ready, n + 1)
                for br, (c0, cn) in enumerate(((0, NCMP), (NCP, nk), (NCP + S, nk))):
                    ins = act.activation(probs[:, n % 2, c0:c0 + cn], probs[:, n % 2, c0:c0 + cn], ACT.Exp,
                                         bias=st1[:, n % 2, 0, br:br + 1],
                                         accum_out=st1[:, n % 2, 1, br:br + 1])
                ins.then_inc(exp_ready, 1)
            if n >= 1:
                m = n - 1
                half, qt = TILES1[m][0] % 2, TILES1[m][1]
                act.wait_ge(pT_mm, m + 1)
                if m >= 2:
                    act.wait_ge(pv_mm, m - 1)
                act.activation(pT[0:NCMP, m % 2, 0, :], bank[4 + half][0:NCMP, P:2 * P], ACT.Copy)
                act.activation(pT[:, m % 2, 1:3 + 2 * qt, :],
                               bank[6][:, 0:2 * (qt + 1) * P].rearrange("p (k q) -> p k q", q=P),
                               ACT.Copy).then_inc(pT_ready, 1)
        act.wait_ge(att_ready, H1 // 2)
        act.activation(h_hi[:, :, :], mix[:, :, :], ACT.Copy).then_inc(h_hi_ready, 1)
        read_m(s_wo)
        square(2, act_read, s_wo.act0 + s_wo.n, mT[:, :, :])
        root(2)
        square(3, x_ready, 1, xT[:, :, :])
        root(3)
        act.activation(c_silu[:, :], cols[:, 0, C_C:C_C + KD], ACT.Silu).then_inc(c_ready, 1)
        operand_hi(2)
        read_pairs(s_gu)
        read_m(s_dn)
        square(4, act_read, s_dn.act0 + s_dn.n, mT[:, :, :])
        root(4)

        square(5, x_ready, 2, xT[:, :, :])
        root(5)
        operand_hi(3)
        for b in range(2):
            before_block(s_lat, b)
            for t in range(TT):
                if b == 0:
                    act.activation(junk[:, t, :], bank3[s_lat.b0 % 2][:, t, :], ACT.Square,
                                   accum_out=st2[:, t, 0:1])
                else:
                    act.activation(junk[:, 2 + t, 0:CKV], bank3[(s_lat.b0 + 1) % 2][:, t, 0:CKV], ACT.Square,
                                   accum_out=st2[:, t, 1:2])
                    ins = act.activation(junk[:, 4 + t, 0:64], bank3[(s_lat.b0 + 1) % 2][:, t, CKV:CKV + 64],
                                         ACT.Square, accum_out=st2[:, t, 2:3])
        ins.then_inc(lat_sq, 1)
        act.wait_ge(lat_var, 1)
        act.activation(st2[:, :, 6:9], st2[:, :, 3:6], ACT.Sqrt).then_inc(lat_sd, 1)
        act.wait_ge(qn_ready, 1)
        act.activation(ff_hi[:, 0:2, :], rn[:, :, :], ACT.Copy).then_inc(qn_hi, 1)
        for b in range(s_uq.n):
            before_block(s_uq, b)
            act.activation(uq[:, :, 2 * b:2 * b + 2].rearrange("p q h -> p h q"),
                           bank3[(s_uq.b0 + b) % 2], ACT.Copy, scale=CKV ** -0.5).then_inc(act_read, 1)
        for b in range(s_qi.n):
            before_block(s_qi, b)
            act.activation(qi[:, 2 * b:2 * b + 2, :], bank3[(s_qi.b0 + b) % 2], ACT.Copy
                           ).then_inc(act_read, 1)
        for r in range(8):
            act.wait_ge(ix_mm, r + 1)
            if r >= 2:
                act.wait_ge(ix_sum, r - 1)
            for j in range(2):
                ins = act.activation(relu_s[:, r % 2, 2 * j:2 * j + 2, :], bank3[2 + 2 * (r % 2) + j],
                                     ACT.Relu)
            ins.then_inc(ix_relu, 1)
        with act.Fori(0, s_z.n // 2) as i:
            for b in range(2):
                loop_block(s_z, b, i)
                act.activation(szT[:, bass.ds(at(i, 4, 2 * b), 2), :], bank3[(s_z.b0 + b) % 2],
                               ACT.Silu).then_inc(act_read, 1)
        end_loop(s_z)
        for n in range(NTILE + 1):
            if n < NTILE:
                act.wait_ge(lt_max, n + 1)
                act.activation(p2buf[:, n % 2, :], bank[2 + n % 2][:, 0:S], ACT.Exp,
                               bias=st3[:, n % 2, 0:1], accum_out=st3[:, n % 2, 1:2]).then_inc(lt_exp, 1)
            if n >= 1:
                m = n - 1
                act.wait_ge(lt_T, m + 1)
                if m >= 2:
                    act.wait_ge(lt_pv, m - 1)
                act.activation(p2T[:, m % 2, :, :],
                               bank[4 + m % 2][:, 0:S].rearrange("p (k r) -> p k r", k=2),
                               ACT.Copy).then_inc(lt_pT, 1)
        for b in range(4):
            act.wait_ge(uv_mm, b + 1)
            act.activation(ff_hi[:, 8 + 2 * b:10 + 2 * b, :], bank3[2 + b], ACT.Copy).then_inc(uv_hi, 1)
        with act.Fori(0, s_ga.n // 2) as i:
            for b in range(2):
                loop_block(s_ga, b, i)
                act.activation(mT[:, bass.ds(at(i, 4, 2 * b), 2), :], bank3[(s_ga.b0 + b) % 2],
                               ACT.Sigmoid).then_inc(act_read, 1)
        end_loop(s_ga)
        for b in range(s_oa.n):
            split_to(s_oa.u0 + (b + 1) * 2 + AHEAD)
        act.wait_ge(dt_a, 1)
        link(act.activation(dt_sc[:, 1, :, :], dt_sc[:, 1, :, :], ACT.Exp, scale=-1.0))
        link(act.activation(dt_sc[:, 1, :, :], dt_sc[:, 1, :, :], ACT.Ln, bias=1.0))
        act.activation(a_row[:, :], a_row[:, :], ACT.Exp).then_inc(dt_b, 1)
        for b in range(s_xbc.n):
            split_to(s_xbc.u0 + (b + 1) * 2 + AHEAD)
            act.wait_ge(dve_read, s_xbc.dve0 + b + 1)
            dst = (xsT[:, 2 * b:2 * b + 2, :] if b < 8 else bT[:, 2 * b - 16:2 * b - 14, :] if b < 12
                   else cT[:, 2 * b - 24:2 * b - 22, :])
            act.activation(dst, dst, ACT.Silu).then_inc(xbc_ready, 1)
        for h in range(HS):
            act.wait_ge(seg_mm, h + 1)
            if h >= 2:
                act.wait_ge(m_mat, h - 1)
            act.activation(decay[:, h % 2, :], bank[2 + h % 2][:, 0:384], ACT.Exp).then_inc(dec_ready, 1)
        act.wait_ge(y_ready, KI)
        act.activation(ysq, szT[:, :, :], ACT.Square).then_inc(sq_ready, 1)
        root(6)
        act.wait_ge(y_gain, 1)
        act.activation(ff_hi[:, 0:KI, :], szT[:, :, :], ACT.Copy).then_inc(y_hi, 1)
        with act.Fori(0, s_gb.n // 2) as i:
            for b in range(2):
                loop_block(s_gb, b, i)
                act.activation(work[:, bass.ds(at(i, 4, 2 * b), 2), :], bank3[(s_gb.b0 + b) % 2],
                               ACT.Sigmoid).then_inc(act_read, 1)
        end_loop(s_gb)
        for b in range(s_os.n):
            split_to(s_os.u0 + (b + 1) * 4 + AHEAD)
        act.wait_ge(mix2_ready, s_os.n)
        act.activation(h_hi[:, :, :], mT[:, :, :], ACT.Copy).then_inc(h_hi_ready, 1)
        read_m(s_wo2)
        square(7, act_read, s_wo2.act0 + s_wo2.n, mT[:, :, :])
        root(7)
        square(8, x_ready, 3, xT[:, :, :])
        root(8)
        operand_hi(4)
        read_pairs(s_gu2)
        for b in range(s_dn2.n):
            before_block(s_dn2, b)
            act.activation(mT[:, 2 * b:2 * b + 2, :], bank3[(s_dn2.b0 + b) % 2], ACT.Copy
                           ).then_inc(act_read, 1)
        square(9, act_read, s_dn2.act0 + s_dn2.n, mT[:, :, :])
        root(9)
        for j in range(2):
            act.wait_ge(out_T, 2 * j + 1)
            act.activation(out_tok[:, j, 0:512], bank[2 + 2 * j][:, :], ACT.Copy).then_inc(out_act, 1)

    @block.vector
    def _(dve):
        own, done_units = [0], [0]

        def link(ins):
            own[0] += 1
            ins.then_inc(dve_own, 1)
            dve.wait_ge(dve_own, own[0])

        def lo_of(dst, src, hi):
            return dve.tensor_tensor(dst, src, hi.bitcast(F32), ALU.subtract)

        def split(i, per, u):
            r = u % RING
            dve.wait_ge(hi_ready, at(i, per, u + 1))
            lo_of(w_lo[:, r, :], w_raw[:, r, :], w_hi[:, r, :]).then_inc(lo_ready, 1)

        def split_to(u_end):
            while done_units[0] < min(u_end, n_units):
                split(None, 0, done_units[0])
                done_units[0] += 1

        def before_block(st, b):
            end = st.u0 + (b + 1) * len(st.ks)
            split_to(end + AHEAD)
            dve.wait_ge(unit_used, end)

        def end_loop(st):
            done_units[0] = st.u0 + st.n * len(st.ks) + AHEAD

        def follow(st):
            n = 2 * len(st.ks)
            with dve.Fori(0, st.n // 2) as i:
                for j in range(n):
                    split(i, n, st.u0 + AHEAD + j)
            end_loop(st)

        def variance(n, count=D):
            dve.wait_ge(ss_ready, n)
            dve.tensor_scalar(var, bank[7][:, 0:S], 1.0 / count, 1e-6, ALU.mult, ALU.add
                              ).then_inc(var_ready, 1)
            dve.wait_ge(sd_ready, n)
            link(dve.reciprocal(rstd[:, :], sd))

        def pre_norm(gain, shift=None):
            for k in range(KD):
                ins = dve.scalar_tensor_tensor(work[:, k, :], xT[:, k, :], gain(k), rstd[:, :],
                                               ALU.mult, ALU.mult)
            if shift is not None:
                link(ins)
                for k in range(KD):
                    ins = dve.tensor_scalar(work[:, k, :], work[:, k, :], shift(k), None, ALU.add)
            ins.then_inc(h_ready, 1)

        def operand_lo(n, src):
            dve.wait_ge(h_hi_ready, n)
            lo_of(h_lo[:, :, :], src, h_hi[:, :, :]).then_inc(h_lo_ready, 1)

        def post_norm(gain):
            for k in range(KD):
                ins = dve.scalar_tensor_tensor(work[:, k, :], mT[:, k, :], gain(k), rstd[:, :],
                                               ALU.mult, ALU.mult)
            link(ins)
            dve.tensor_tensor(xT[:, :, :], xT[:, :, :], work[:, :, :], ALU.add).then_inc(x_ready, 1)

        def multiply_pairs(st, ff0, extra=None):
            with dve.Fori(0, st.n // 2) as i:
                for j in range(2):
                    split(i, 4, st.u0 + 2 + j)
                if extra:
                    extra(i)
                for j in range(2):
                    split(i, 4, st.u0 + 4 + j)
                dve.wait_ge(unit_used, at(i, 4, st.u0 + 4))
                dve.wait_ge(act_read, at(i, 1, st.act0 + 1))
                dve.tensor_tensor(ffv[:, :, :], silu_g[:, :, :], bank3[(st.b0 + 1) % 2], ALU.mult
                                  ).then_inc(dve_read, 1)
                dve.wait_ge(ff_hi_ready, at(i, 1, ff0 + 1))
                lo_of(ff_lo[:, bass.ds(at(i, 2, 0), 2), :], ffv[:, :, :],
                      ff_hi[:, bass.ds(at(i, 2, 0), 2), :]).then_inc(ff_lo_ready, 1)
            end_loop(st)

        dve.wait_ge(bias_mm, 1)
        dve.tensor_copy(bias_row[:, 0:S], bank[7][0:H1, 0:S])
        dve.memset(bias_row[:, S:2 * S], NEG).then_inc(bias_ready, 1)
        dve.wait_ge(rows_T, 1)
        for t in range(3):
            ins = dve.tensor_copy(cols[:, t, 0:R_USED[t]], bank[6][:, t * P:t * P + R_USED[t]])
        link(ins)
        dve.wait_ge(x_T, 2)
        for j in (2, 3):
            ins = dve.tensor_copy(xT[:, 2 * j:2 * j + 2, :], bank3[2 + j])
        ins.then_inc(x_dve, 1)
        split_to(AHEAD)
        variance(1)
        pre_norm(lambda k: col(0, C_MIX + k))
        operand_lo(1, work[:, :, :])
        before_block(s_kc, 0)
        for n, pos in ((0, POS_K), (1, POS_V)):
            for g in range(G1):
                tok = bank3[s_kc.b0 % 2][64 * g:64 * g + 64, n, :].rearrange("p (j t a) -> p t j a", t=8, a=2)
                for par in range(2):
                    rows64 = slice(64 * par, 64 * par + 64)
                    for c in range(2):
                        ins = dve.tensor_tensor(
                            tblk[rows64, n, 8 * c:8 * c + 8, g * NCMP:(g + 1) * NCMP],
                            tok[:, :, c:c + NCMP, par],
                            cols[rows64, 2, pos + 8 * c:pos + 8 * c + 8].unsqueeze(2).broadcast_to(
                                [64, 8, NCMP]), ALU.add)
        ins.then_inc(dve_read, 1)
        split_to(s_in.u0 + 16 + AHEAD)
        dve.wait_ge(tblk_hi_ready, 1)
        lo_of(tblk_lo[:, :, :, :], tblk[:, :, :, :], tblk_hi[:, :, :, :]).then_inc(tblk_lo_ready, 1)
        for h in range(H1):
            dve.wait_ge(toep_mm, h + 1)
            dve.tensor_copy(toep[:, h, :], bank[2 + h % 4][:, 0:TOEP]).then_inc(toep_ready, 1)
        dve.wait_ge(act_read, s_in.act0 + 6)
        for t in range(TT):
            ins = dve.bn_stats(ln_bn[:, t, :], gv[:, t, :])
        link(ins)
        for t in range(TT):
            ins = dve.bn_aggr(ln_st[:, t, 0:2], ln_bn[:, t, :])
        link(ins)
        dve.tensor_scalar(ln_st[:, :, 1:2], ln_st[:, :, 1:2], 1e-5, None, ALU.add).then_inc(ln_var, 1)
        split_to(s_cmp.u0 + 8 + AHEAD)
        dve.wait_ge(gates_act, 1)
        gate_c = gates[:, 0, 0:24:3]
        dve.tensor_scalar(gate_c, gate_c, has_block, None, ALU.mult).then_inc(gates_ready, 1)
        dve.wait_ge(ws_T, 1)
        for j in range(2):
            ins = dve.tensor_tensor(wsT[:, 4 * j:4 * j + 4, :],
                                    bank[2 + j][:, :].rearrange("p (g t) -> p g t", g=4),
                                    tri.unsqueeze(1).broadcast_to([P, 4, P]), ALU.mult)
        ins.then_inc(wsT_ready, 1)
        dve.wait_ge(ln_sd, 1)
        link(dve.reciprocal(ln_st[:, :, 3:4], ln_st[:, :, 2:3]))
        for t in range(TT):
            ins = dve.tensor_scalar(gv[:, t, :], gv[:, t, :], ln_st[:, t, 0:1], ln_st[:, t, 3:4],
                                    ALU.subtract, ALU.mult)
        link(ins)
        dve.wait_ge(ln_in, 32)
        link(dve.tensor_tensor(gv[:, :, :], gv[:, :, :], ln_g[:, :].unsqueeze(1).broadcast_to([P, TT, GW]),
                               ALU.mult))
        dve.tensor_tensor(gv[:, :, :], gv[:, :, :], ln_b[:, :].unsqueeze(1).broadcast_to([P, TT, GW]),
                          ALU.add).then_inc(zv_ready, 1)
        dve.wait_ge(sv_mm, 1)
        for i in range(4):
            ins = dve.tensor_tensor(mix[:, 4 + i, :].rearrange("p (n t) -> p n t", n=2),
                                    bank[4 + i // 2][:, (i % 2) * S:(i % 2 + 1) * S].rearrange(
                                        "p (n t) -> p n t", n=2),
                                    bs[:, i, :].unsqueeze(1).broadcast_to([P, 2, P]), ALU.add)
        link(ins)
        dve.tensor_tensor(mix[:, 4:8, :], mix[:, 4:8, :], zu[:, :, :], ALU.mult).then_inc(mix_gm, 1)
        for n in range(len(TILES1) + 3):
            if n < len(TILES1):
                h, qt = TILES1[n]
                nk, off = P * (qt + 1), P * (1 - qt)
                dve.wait_ge(lg_mm, n + 1)
                if n >= 2:
                    dve.wait_ge(pT_mm, n - 1)
                sw = probs[:, n % 2, NCP:NCP + 2 * S].rearrange("p (b k) -> p b k", b=2)[:, :, 0:nk]
                dve.tensor_tensor(sw, bank3[2 + h % 2][:, :, 0:nk],
                                  toep[:, h, off:off + nk].unsqueeze(1).broadcast_to([P, 2, nk]), ALU.add)
                first = off + CBLOCK - 1
                link(dve.tensor_tensor(probs[:, n % 2, 0:NCMP], bank[4 + h % 2][:, 0:NCMP],
                                       toep[:, h, first:first + CSTRIDE * (NCMP - 1) + 1:CSTRIDE], ALU.add))
                dve.tensor_reduce(st1[:, n % 2, 0, 1:3], sw, AX.X, ALU.max, negate=True)
                dve.tensor_reduce(st1[:, n % 2, 0, 0:1], probs[:, n % 2, 0:NCMP], AX.X, ALU.max,
                                  negate=True).then_inc(max_ready, 1)
            if 1 <= n <= len(TILES1):
                m = n - 1
                h, qt = TILES1[m]
                nk = P * (qt + 1)
                dve.wait_ge(exp_ready, m + 1)
                link(dve.reciprocal(st1[:, m % 2, 2, 0:3], st1[:, m % 2, 1, 0:3]))
                link(dve.tensor_tensor(st1[:, m % 2, 3, 0:3], st1[:, m % 2, 2, 0:3],
                                       gates[:, qt, 3 * h:3 * h + 3], ALU.mult))
                for br, (c0, cn) in enumerate(((0, NCMP), (NCP, nk), (NCP + S, nk))):
                    ins = dve.tensor_scalar(probs[:, m % 2, c0:c0 + cn], probs[:, m % 2, c0:c0 + cn],
                                            st1[:, m % 2, 3, br:br + 1], None, ALU.mult)
                ins.then_inc(pn_ready, 1)
            if n >= 6 and (n - 6) % 4 == 0:
                hp = (n - 6) // 4
                dve.wait_ge(pv_mm, 4 * hp + 4)
                dve.tensor_copy(mix[:, hp, :], bank3[7][:, hp % 2, :]).then_inc(att_ready, 1)
        operand_lo(2, mix[:, :, :])
        follow(s_wo)
        variance(2)
        post_norm(lambda k: col(0, C_MIXP + k))
        variance(3)
        pre_norm(lambda k: col(0, C_FFN + k))
        operand_lo(3, work[:, :, :])

        def modulate(i, per, c):
            acc = ada_acc[:, bass.ds(at(i, 512, 512 * c), 512)]
            for k in range(KD):
                src = ada_raw[:, k // 2, (k % 2) * 512:(k % 2 + 1) * 512]
                if k % 2 == 0:
                    dve.wait_ge(ada_in[k // 2], at(i, 16, 16 * (c + 1)))
                if k == 0:
                    ins = dve.tensor_scalar(acc, src, c_silu[:, 0:1], None, ALU.mult)
                else:
                    dve.wait_ge(ada_used, at(i, 8, 8 * c + k))
                    ins = dve.scalar_tensor_tensor(acc, src, c_silu[:, k:k + 1], acc, ALU.mult, ALU.add)
                ins.then_inc(ada_used, 1)

        dve.wait_ge(c_ready, 1)
        modulate(None, 0, 0)
        multiply_pairs(s_gu, 0, extra=lambda i: modulate(i, 8, 1))
        dve.wait_ge(ada_mm, 1)
        link(dve.tensor_tensor(mod[:, :], bank[6][:, 0:48], cols[:, 2, ADA_B:ADA_B + 48], ALU.add))
        for n, (m0, c0, plus) in enumerate(((8, C_MIX2, 1.0), (16, C_MIXP2, 0.0), (32, C_FFN2, 1.0),
                                            (40, C_FFNP2, 0.0))):
            ins = dve.scalar_tensor_tensor(gains[:, n, :], mod[:, m0:m0 + 8], plus, cols[:, 0, c0:c0 + 8],
                                           ALU.add, ALU.mult)
        ins.then_inc(mod_ready, 1)
        follow(s_dn)
        variance(4)
        post_norm(lambda k: col(0, C_FFNP + k))

        variance(5)
        pre_norm(lambda k: gains[:, 0, k:k + 1], lambda k: mod[:, k:k + 1])
        operand_lo(4, work[:, :, :])
        dve.wait_ge(pos_in, 32)
        dve.tensor_copy(pos_f[:, :], pos_i[:, :])
        link(dve.tensor_scalar(last_i[:, :], pos_i[:, S:S + TT], -64, None, ALU.bitwise_and))
        link(dve.tensor_copy(last_f[:, :], last_i[:, :]))
        link(dve.tensor_scalar(last_f[:, :], last_f[:, :], 64.0, None, ALU.add))
        for t in range(TT):
            dve.tensor_scalar(shut[:, t, :], pos_f[:, 0:S], last_f[:, t:t + 1], NEG, ALU.is_ge, ALU.mult)
        for q in range(4):
            for n, bound in enumerate((range_lo, range_hi)):
                r32 = slice(32 * q, 32 * q + 32)
                dve.tensor_scalar(own_pos[r32, n, :], pos_f[r32, q:S:4], bound[r32, :], None, ALU.add)
        dve.wait_ge(tab_in, 64)
        link(dve.tensor_copy(tab_s[:, 0, :], tab2[:, :]))
        link(dve.tensor_tensor(tab_r[:, :], tab2[:, :], tab_s[:, 0, :], ALU.subtract))
        link(dve.tensor_copy(tab_s[:, 1, :], tab_r[:, :]))
        link(dve.tensor_tensor(tab_r[:, :], tab_r[:, :], tab_s[:, 1, :], ALU.subtract))
        dve.tensor_copy(tab_s[:, 2, :], tab_r[:, :])
        link(dve.memset(tab_b[:, :, :, :], 0.0))
        for q in range(QT):
            r32 = slice(32 * (q % 4), 32 * (q % 4) + 32)
            ins = dve.tensor_copy(tab_b[r32, q // 4, :, H2 * q:H2 * q + H2], tab_s[r32, :, :])
        ins.then_inc(tab_ready, 1)
        before_block(s_lat, 0)
        before_block(s_lat, 1)
        dve.wait_ge(lat_sq, 1)
        for n, count in enumerate((QR, CKV, 64)):
            ins = dve.tensor_scalar(st2[:, :, 3 + n:4 + n], st2[:, :, n:n + 1], 1.0 / count, 1e-6,
                                    ALU.mult, ALU.add)
        ins.then_inc(lat_var, 1)
        dve.wait_ge(lat_sd, 1)
        link(dve.reciprocal(st2[:, :, 9:12], st2[:, :, 6:9]))
        dve.wait_ge(lat_in, 16)
        b_q, b_k = bank3[s_lat.b0 % 2], bank3[(s_lat.b0 + 1) % 2]
        for t in range(TT):
            ins = dve.tensor_scalar(qn[:, t, :], b_q[:, t, :], st2[:, t, 9:10], None, ALU.mult)
        ins.then_inc(dve_read, 1)
        for t in range(TT):
            dve.scalar_tensor_tensor(kv[:, t, :], b_k[:, t, 0:CKV], st2[:, t, 10:11], kv_gain[:, :],
                                     ALU.mult, ALU.mult)
            dve.tensor_scalar(kin[:, t, :, :], b_k[:, t, CKV:CKV + 64].unsqueeze(1).broadcast_to([P, 2, 64]),
                              st2[:, t, 11:12], None, ALU.mult)
        dve.tensor_scalar(widx[:, :, :], b_k[:, :, 192:208], 16 ** -0.5 * 64 ** -0.5, None, ALU.mult
                          ).then_inc(dve_read, 1)
        dve.wait_ge(lat_T, 1)
        for k in range(2):
            ins = dve.tensor_scalar(rn[:, k, :], bank3[2][:, k, :], col(0, C_QN + k), None, ALU.mult)
        ins.then_inc(qn_ready, 1)
        dve.tensor_copy(kvT[:, :], bank[3][:, 0:S])
        dve.tensor_scalar(kiT[:, :], bank[3][:, S:2 * S], col(0, C_KI), None, ALU.mult).then_inc(ki_ready, 1)
        dve.wait_ge(qn_hi, 1)
        lo_of(ff_lo[:, 0:2, :], rn[:, :, :], ff_hi[:, 0:2, :]).then_inc(qn_lo, 1)
        dve.wait_ge(dt_mm, 1)
        dve.wait_ge(ssd_in, 80)
        link(dve.tensor_tensor(dt_sc[:, 0, :, :], bank[6][:, 0:2 * HS].rearrange("p (t h) -> p t h", t=TT),
                               dt_bias[:, :].unsqueeze(1).broadcast_to([P, TT, HS]), ALU.add))
        link(dve.scalar_tensor_tensor(dt_sc[:, 1, :, :], dt_sc[:, 0, :, :], -1.0, dt_sc[:, 0, :, :],
                                      ALU.mult, ALU.max))
        dve.tensor_scalar(dt_sc[:, 0, :, :], dt_sc[:, 0, :, :], 0.0, None, ALU.max).then_inc(dt_a, 1)
        split_to(s_qi.u0 + 4 + AHEAD)
        for r in range(8):
            qt, r4 = r // 4, r % 4
            dve.wait_ge(ix_relu, r + 1)
            for j in range(4):
                w = widx[:, qt, 4 * r4 + 2 * (j % 2) + j // 2:4 * r4 + 2 * (j % 2) + j // 2 + 1]
                if r4 == 0 and j == 0:
                    ins = dve.tensor_scalar(isc[:, qt, :], relu_s[:, r % 2, j, :], w, None, ALU.mult)
                else:
                    ins = dve.scalar_tensor_tensor(isc[:, qt, :], relu_s[:, r % 2, j, :], w, isc[:, qt, :],
                                                   ALU.mult, ALU.add)
                if j < 3:
                    link(ins)
            ins.then_inc(ix_sum, 1)
            dve.wait_ge(ix_sum, r + 1)
        link(dve.tensor_tensor(isc[:, :, :], isc[:, :, :], shut[:, :, :], ALU.add))
        for qt in range(TT):
            for r in range(TOPK // 8):
                link(dve.max(top8[:, :], isc[:, qt, :]))
                link(dve.match_replace(isc[:, qt, :], top8[:, :], isc[:, qt, :], NEG_TAKEN))
                split_to(s_z.u0 + AHEAD + 8 * qt + r + 1)
        link(dve.tensor_scalar(isc[:, :, :], isc[:, :, :], -2.0e38, NEG, ALU.is_gt, ALU.mult))
        dve.tensor_tensor(mask[:, :, :], isc[:, :, :], shut[:, :, :], ALU.add).then_inc(mask_ready, 1)
        for n in range(NTILE + 2):
            if n < NTILE:
                if n >= 2:
                    dve.wait_ge(lt_mm, n - 1)
                for c in range(2):
                    ins = dve.tensor_scalar(in_lo[:, c, :], pos_f[:, 0:S], own_pos[:, 0, 2 * n + c:2 * n + c + 1],
                                            None, ALU.is_ge)
                link(ins)
                for c in range(2):
                    ins = dve.scalar_tensor_tensor(onehot[:, n % 2, c, :], pos_f[:, 0:S],
                                                   own_pos[:, 1, 2 * n + c:2 * n + c + 1], in_lo[:, c, :],
                                                   ALU.is_le, ALU.mult)
                ins.then_inc(hot_ready, 1)
            if 1 <= n <= NTILE:
                m = n - 1
                dve.wait_ge(lt_exp, m + 1)
                link(dve.reciprocal(st3[:, m % 2, 2:3], st3[:, m % 2, 1:2]))
                dve.tensor_scalar(p2buf[:, m % 2, :], p2buf[:, m % 2, :], st3[:, m % 2, 2:3], None, ALU.mult
                                  ).then_inc(lt_p, 1)
            if n < NTILE:
                dve.wait_ge(lt_mm, n + 1)
                if n >= 2:
                    dve.wait_ge(lt_T, n - 1)
                dve.tensor_reduce(st3[:, n % 2, 0:1], bank[2 + n % 2][:, 0:S], AX.X, ALU.max, negate=True
                                  ).then_inc(lt_max, 1)
            if n >= 2:
                m = n - 2
                dve.wait_ge(lt_pv, m + 1)
                dve.tensor_copy(oT[:, :, QT * m:QT * m + QT],
                                bank[6 + m % 2][:, 0:P].rearrange("p (q h) -> p h q", q=QT)
                                ).then_inc(lt_o, 1)
        for b in range(4):
            dve.wait_ge(uv_hi, b + 1)
            lo_of(ff_lo[:, 8 + 2 * b:10 + 2 * b, :], bank3[2 + b], ff_hi[:, 8 + 2 * b:10 + 2 * b, :]
                  ).then_inc(uv_lo, 1)
        follow(s_ga)
        for b in range(s_oa.n):
            before_block(s_oa, b)
            if b == 0:
                dve.wait_ge(act_read, s_ga.act0 + s_ga.n)
            dve.tensor_tensor(mT[:, 2 * b:2 * b + 2, :], bank3[(s_oa.b0 + b) % 2], mT[:, 2 * b:2 * b + 2, :],
                              ALU.mult).then_inc(dve_read, 1)
        for b in range(s_xbc.n):
            before_block(s_xbc, b)
            src = bank3[(s_xbc.b0 + b) % 2]
            dst = (xsT[:, 2 * b:2 * b + 2, :] if b < 8 else bT[:, 2 * b - 16:2 * b - 14, :] if b < 12
                   else cT[:, 2 * b - 24:2 * b - 22, :])
            for s in range(2):
                tile = 2 * b + s
                ins = dve.tensor_scalar(dst[:, s, :], src[:, s, :], col(1, (CONV - 1) * KX + tile),
                                        col(0, C_CONVB + tile), ALU.mult, ALU.add)
            for w in range(CONV - 2, -1, -1):
                link(ins)
                back = CONV - 1 - w
                for s in range(2):
                    ins = dve.scalar_tensor_tensor(dst[:, s, back:S], src[:, s, 0:S - back],
                                                   col(1, w * KX + 2 * b + s), dst[:, s, back:S],
                                                   ALU.mult, ALU.add)
            ins.then_inc(dve_read, 1)
        dve.wait_ge(dt_b, 1)
        link(dve.tensor_tensor(dtd[:, 0, :, :], dt_sc[:, 0, :, :], dt_sc[:, 1, :, :], ALU.add))
        dve.scalar_tensor_tensor(dtd[:, 1, :, :], dtd[:, 0, :, :], -1.0,
                                 a_row[:, :].unsqueeze(1).broadcast_to([P, TT, HS]), ALU.mult, ALU.mult
                                 ).then_inc(dt_ready, 1)
        for n in range(8):
            t, q = n // 4, n % 4
            dve.wait_ge(xs_T, n + 1)
            dve.tensor_tensor(x_dt[:, t, 512 * q:512 * q + 512].rearrange("p (h d) -> p h d", h=8),
                              bank[4 + n % 2][:, :].rearrange("p (h d) -> p h d", h=8),
                              dtd[:, 0, t, 8 * q:8 * q + 8].unsqueeze(2).broadcast_to([P, 8, 64]), ALU.mult
                              ).then_inc(xs_ready, 1)
        for h in range(HS + 2):
            if h < HS:
                g = h // 4
                if h % 4 == 0:
                    dve.wait_ge(cb_mm, g + 1)
                    dve.tensor_tensor(cbm, bank[6][:, 0:384], tri_ones_tri, ALU.mult
                                      ).then_inc(cb_ready, 1)
                    dve.wait_ge(cb_ready, g + 1)
                dve.wait_ge(dec_ready, h + 1)
                if h >= 2:
                    dve.wait_ge(y_mm, h - 1)
                dve.tensor_tensor(m_buf[:, h % 2, :], decay[:, h % 2, :], cbm, ALU.mult
                                  ).then_inc(m_mat, 1)
            if h >= 3 and h % 2 == 1:
                i = (h - 3) // 2
                dve.wait_ge(y_mm, 2 * i + 2)
                link(dve.scalar_tensor_tensor(xsT[:, i, :], xsT[:, i, :], skip[:, i:i + 1],
                                              bank[4 + i % 2][:, 0:S], ALU.mult, ALU.add))
                dve.tensor_tensor(szT[:, i, :], szT[:, i, :], xsT[:, i, :], ALU.mult).then_inc(y_ready, 1)
        dve.wait_ge(sq_ready, 6)
        for k in range(KI):
            ins = dve.tensor_scalar(szT[:, k, :], szT[:, k, :], col(0, C_SSD + k), None, ALU.mult)
        ins.then_inc(y_gain, 1)
        variance(6, DI)
        dve.wait_ge(y_hi, 1)
        lo_of(ff_lo[:, 0:KI, :], szT[:, :, :], ff_hi[:, 0:KI, :]).then_inc(y_lo, 1)
        follow(s_gb)
        for b in range(s_os.n):
            before_block(s_os, b)
            if b == 0:
                dve.wait_ge(act_read, s_gb.act0 + s_gb.n)
            part = work[:, 2 * b:2 * b + 2, :]
            dve.tensor_tensor(part, bank3[(s_os.b0 + b) % 2], part, ALU.mult).then_inc(dve_read, 1)
            dve.wait_ge(dve_read, s_os.dve0 + b + 1)
            link(dve.tensor_tensor(part, part, rstd[:, :].unsqueeze(1).broadcast_to([P, 2, S]), ALU.mult))
            dve.tensor_tensor(mT[:, 2 * b:2 * b + 2, :], mT[:, 2 * b:2 * b + 2, :], part, ALU.add
                              ).then_inc(mix2_ready, 1)
        operand_lo(5, mT[:, :, :])
        follow(s_wo2)
        variance(7)
        post_norm(lambda k: gains[:, 1, k:k + 1])
        variance(8)
        pre_norm(lambda k: gains[:, 2, k:k + 1], lambda k: mod[:, 24 + k:25 + k])
        operand_lo(6, work[:, :, :])
        multiply_pairs(s_gu2, 11)
        split_to(n_units)
        variance(9)
        post_norm(lambda k: gains[:, 3, k:k + 1])
        for j in range(2):
            dve.wait_ge(out_T, 2 * j + 2)
            dve.tensor_copy(out_tok[:, j, 512:1024], bank[3 + 2 * j][:, :]).then_inc(out_ready, 1)

    @block.tensor
    def _(pe):
        def free_bank(st, n, i=None):
            b = st.b0 + n
            if i is None and n >= 2 or i is not None:
                for s, e0 in ((act_read, st.act0), (dve_read, st.dve0)):
                    if (st.reader == "act") == (s is act_read) and st.reader != "pair":
                        pe.wait_ge(s, at(i, 2, e0 + n - 1))
                if st.reader == "pair":
                    if n % 2 == 0:
                        pe.wait_ge(act_read, at(i, 1, st.act0 + n // 2))
                    else:
                        pe.wait_ge(dve_read, at(i, 1, st.dve0 + n // 2))

        def enter(st):
            if st.act0:
                pe.wait_ge(act_read, st.act0)
            if st.dve0:
                pe.wait_ge(dve_read, st.dve0)

        def fm_block(st, n, x_hi, x_lo, i=None, turn=2, k0=0):
            free_bank(st, n, i)
            out_b = bank3[(st.b0 + n) % 2]
            u, k, first, per = st.u0 + n * len(st.ks), k0, True, turn * len(st.ks)
            for nk in st.ks:
                pe.wait_ge(lo_ready, at(i, per, u + 1))
                hi = w_hi[:, u % RING, 0:nk * 256].rearrange("p (k c) -> p k c", k=nk)
                lo = w_lo[:, u % RING, 0:nk * 256].rearrange("p (k c) -> p k c", k=nk)
                for kk in range(nk):
                    end = kk == nk - 1 and u == st.u0 + (n + 1) * len(st.ks) - 1
                    for s in range(2):
                        c = slice(s * P, s * P + P)
                        for w, x, last in ((hi, x_hi, False), (hi, x_lo, False), (lo, x_hi, True)):
                            ins = pe.matmul(out_b[:, s, :], w[:, kk, c], x[:, k, :], start=first,
                                            stop=end and last and s == 1, skip_group_check=True)
                            first = False
                    k += 1
                ins.then_inc(unit_used, 1)
                u += 1

        def tm_block(st, n, x_hi, x_lo, ncol=256):
            free_bank(st, n)
            out_b = bank3[(st.b0 + n) % 2]
            u, k, first = st.u0 + n * len(st.ks), 0, True
            for nk in st.ks:
                pe.wait_ge(lo_ready, u + 1)
                hi = w_hi[:, u % RING, 0:nk * ncol].rearrange("p (k c) -> p k c", k=nk)
                lo = w_lo[:, u % RING, 0:nk * ncol].rearrange("p (k c) -> p k c", k=nk)
                for kk in range(nk):
                    end = kk == nk - 1 and u == st.u0 + (n + 1) * len(st.ks) - 1
                    for t in range(TT):
                        c = slice(t * P, t * P + P)
                        for w, x, last in ((hi, x_hi, False), (hi, x_lo, False), (lo, x_hi, True)):
                            ins = pe.matmul(out_b[:, t, 0:ncol], x[:, k, c], w[:, kk, :], start=first,
                                            stop=end and last and t == 1, skip_group_check=True)
                            first = False
                    k += 1
                ins.then_inc(unit_used, 1)
                u += 1

        def kv_block(st, n):
            free_bank(st, n)
            out_b = bank3[(st.b0 + n) % 2]
            first = True
            for j in range(2):
                u = st.u0 + 2 * n + j
                pe.wait_ge(lo_ready, u + 1)
                hi = w_hi[:, u % RING, :].rearrange("p (k c) -> p k c", k=4)
                lo = w_lo[:, u % RING, :].rearrange("p (k c) -> p k c", k=4)
                for kk in range(4):
                    k = 4 * j + kk
                    for w, x in ((hi, h_hi), (hi, h_lo), (lo, h_hi)):
                        pe.matmul(out_b[:, 0, :], w[:, kk, 0:P], x[:, k, :], start=first, stop=False,
                                  skip_group_check=True)
                        first = False
                    for t in range(TT):
                        c = slice(t * P, t * P + P)
                        for w, x, last in ((hi, h_hi, False), (hi, h_lo, False), (lo, h_hi, True)):
                            ins = pe.matmul(out_b[:, 1, c], x[:, k, c], w[:, kk, P:2 * P], start=False,
                                            stop=k == KD - 1 and t == 1 and last, skip_group_check=True)
                ins.then_inc(unit_used, 1)

        def fm_stream(st, x_hi, x_lo, k0=0):
            enter(st)
            with pe.Fori(0, st.n // 2) as i:
                for n in range(2):
                    fm_block(st, n, x_hi, x_lo, i, 2, k0)

        def sum_squares(n, sq, tiles=KD):
            pe.wait_ge(sq_ready, n)
            for k in range(tiles):
                ins = pe.matmul(bank[7][:, 0:S], ones, sq[:, k, :], start=k == 0, stop=k == tiles - 1)
            ins.then_inc(ss_ready, 1)

        pe.wait_ge(consts_in, 16)
        pe.wait_ge(hot_in, 32)
        pe.matmul(bank[7][0:H1, :], table1[:, :], hot[:, :], start=True, stop=True).then_inc(bias_mm, 1)
        pe.wait_ge(rows_in, 16 * n_rows_dma)
        for t in range(3):
            ins = pe.transpose(bank[6][:, t * P:t * P + R_USED[t]], rows[0:R_USED[t], t, :],
                               ident[0:R_USED[t], 0:R_USED[t]])
        ins.then_inc(rows_T, 1)
        pe.wait_ge(x_in, 16)
        for j in range(4):
            for k in (0, 1):
                for t in range(TT):
                    ins = pe.transpose(bank[2 + j][:, k * S + t * P:k * S + (t + 1) * P],
                                       x_tok[:, t, (2 * j + k) * P:(2 * j + k + 1) * P], ident)
            if j % 2:
                ins.then_inc(x_T, 1)
        pe.wait_ge(bias_ready, 1)
        sum_squares(1, work)
        pe.wait_ge(h_lo_ready, 1)
        fm_block(s_kc, 0, h_hi, h_lo)
        kv_block(s_in, 0)
        pe.wait_ge(dve_read, 1)
        fm_block(s_in, 1, h_hi, h_lo)
        fm_block(s_in, 2, h_hi, h_lo)
        kv_block(s_in, 3)
        tm_block(s_in, 4, h_hi, h_lo)
        tm_block(s_in, 5, h_hi, h_lo)
        fm_block(s_in, 6, h_hi, h_lo)
        fm_block(s_in, 7, h_hi, h_lo)
        pe.wait_ge(gates_in, 16)
        for t in range(TT):
            for k in range(KD):
                ins = pe.matmul(bank[7][:, 24 * t:24 * t + 24], work[:, k, t * P:(t + 1) * P],
                                w_gates[:, k, :], start=k == 0, stop=k == KD - 1)
        ins.then_inc(gate_mm, 1)
        pe.wait_ge(toep_in, 32)
        for h in range(H1):
            if h >= 4:
                pe.wait_ge(toep_ready, h - 3)
            pe.matmul(bank[2 + h % 4][:, 0:TOEP], flip, hankel_a[:, h, :] if h < 5 else hankel_b[:, h - 5, :],
                      start=True, stop=True).then_inc(toep_mm, 1)
        enter(s_cmp)
        pe.wait_ge(tblk_lo_ready, 1)
        for n in range(2):
            out_b = bank[(s_cmp.b0 + n) % 2][:, 0:4 * NCMP].rearrange("p (m n) -> p m n", m=2)
            first = True
            for j in range(4):
                u = s_cmp.u0 + 4 * n + j
                pe.wait_ge(lo_ready, u + 1)
                hi = w_hi[:, u % RING, :].rearrange("p (k c) -> p k c", k=4)
                lo = w_lo[:, u % RING, :].rearrange("p (k c) -> p k c", k=4)
                for kk in range(4):
                    for m in range(2):
                        c = slice(m * P, m * P + P)
                        for w, x, last in ((hi, tblk_hi, False), (hi, tblk_lo, False), (lo, tblk_hi, True)):
                            ins = pe.matmul(out_b[:, m, :], w[:, kk, c], x[:, n, 4 * j + kk, :],
                                            start=first, stop=j == 3 and kk == 3 and m == 1 and last,
                                            skip_group_check=True)
                            first = False
                ins.then_inc(unit_used, 1)
        pe.wait_ge(gmlp_in, 48)
        pe.wait_ge(toep_ready, H1)
        for g in range(8):
            ins = pe.transpose(bank[2 + g // 4][:, (g % 4) * P:(g % 4 + 1) * P], ws[:, g, :], ident)
        ins.then_inc(ws_T, 1)
        pe.wait_ge(mlp_in, 32)
        pe.wait_ge(act_read, s_cmp.act0 + 2)
        for half in range(2):
            for m in range(2):
                pe.matmul(bank[6][64 * half:64 * half + 64, 0:2 * NCMP], w2[:, 0, m, :], hid[:, 0, m, :],
                          start=m == 0, stop=m == 1)
        for g in range(G1):
            for m in range(2):
                ins = pe.matmul(bank[6][0:NCMP, P + 64 * g:P + 64 * g + 64],
                                hid[:, 1, m, g * NCMP:(g + 1) * NCMP], w2[:, 1, m, :],
                                start=m == 0, stop=m == 1)
        ins.then_inc(kcvc_mm, 1)
        pe.wait_ge(wsT_ready, 1)
        pe.wait_ge(zv_ready, 1)
        for g in range(8):
            for t in range(TT):
                c0 = (g // 2 % 2) * S + t * P
                ins = pe.matmul(bank[4 + g // 4][64 * (g % 2):64 * (g % 2) + 64, c0:c0 + P],
                                gv[:, t, 64 * g:64 * g + 64], wsT[:, g, :], start=True, stop=True)
        ins.then_inc(sv_mm, 1)
        pe.wait_ge(mix_gm, 1)
        pe.wait_ge(kcvc_ready, 1)
        pe.wait_ge(gates_ready, 1)
        for n in range(len(TILES1) + 2):
            if n < len(TILES1):
                h, qt = TILES1[n]
                half, g, nk = h % 2, h // 4, P * (qt + 1)
                r64 = slice(64 * half, 64 * half + 64)
                q = qT[r64, h // 2, qt * P:(qt + 1) * P]
                if n >= 2:
                    pe.wait_ge(max_ready, n - 1)
                    pe.wait_ge(pT_ready, n - 1)
                for br in range(2):
                    pe.matmul(bank3[2 + half][:, br, 0:nk], q, kdup[r64, g, br, 0:nk], start=True, stop=True)
                pe.matmul(bank[4 + half][:, 0:NCMP], q, kc_dup[r64, g * NCMP:(g + 1) * NCMP],
                          start=True, stop=True).then_inc(lg_mm, 1)
            if 1 <= n <= len(TILES1):
                m = n - 1
                h, qt = TILES1[m]
                pe.wait_ge(pn_ready, m + 1)
                if m >= 1:
                    pe.wait_ge(pT_ready, m)
                pe.transpose(bank[4 + h % 2][0:NCMP, P:2 * P], probs[:, m % 2, 0:NCMP], ident)
                for br in range(2):
                    for kt in range(qt + 1):
                        c0 = (br * (qt + 1) + kt) * P
                        k0 = NCP + br * S + kt * P
                        ins = pe.transpose(bank[6][:, c0:c0 + P], probs[:, m % 2, k0:k0 + P], ident)
                ins.then_inc(pT_mm, 1)
            if n >= 2:
                m = n - 2
                h, qt = TILES1[m]
                half, g, hp = h % 2, h // 4, m // 4
                pe.wait_ge(pT_ready, m + 1)
                if m % 4 == 0 and hp >= 1:
                    pe.wait_ge(att_ready, hp)
                o = bank[7][64 * half:64 * half + 64, (hp % 2) * S + qt * P:(hp % 2) * S + (qt + 1) * P]
                pe.matmul(o, vc[:, g, :], pT[0:NCMP, m % 2, 0, :], start=True, stop=False)
                for br in range(2):
                    for kt in range(qt + 1):
                        ins = pe.matmul(o, v_tok[:, kt, br * KV1 + 64 * g:br * KV1 + 64 * g + 64],
                                        pT[:, m % 2, 1 + br * (qt + 1) + kt, :], start=False,
                                        stop=br == 1 and kt == qt)
                ins.then_inc(pv_mm, 1)
        pe.wait_ge(h_lo_ready, 2)
        fm_stream(s_wo, h_hi, h_lo)
        sum_squares(2, work)
        sum_squares(3, work)
        pe.wait_ge(h_lo_ready, 3)
        fm_stream(s_gu, h_hi, h_lo)
        pe.wait_ge(ada_used, 8 * 12)
        for c in range(48):
            ins = pe.matmul(bank[6][:, c:c + 1], ada_acc[:, c * P:(c + 1) * P], ones[:, 0:1],
                            start=True, stop=True)
        ins.then_inc(ada_mm, 1)
        pe.wait_ge(ff_lo_ready, 11)
        fm_stream(s_dn, ff_hi, ff_lo)
        sum_squares(4, work)

        sum_squares(5, work)
        pe.wait_ge(h_lo_ready, 4)
        enter(s_lat)
        tm_block(s_lat, 0, h_hi, h_lo)
        tm_block(s_lat, 1, h_hi, h_lo, ncol=208)
        pe.wait_ge(ssd_in, 80)
        for t in range(TT):
            for k in range(KD):
                ins = pe.matmul(bank[6][:, HS * t:HS * t + HS], work[:, k, t * P:(t + 1) * P],
                                w_dt[:, k, :], start=k == 0, stop=k == KD - 1)
        ins.then_inc(dt_mm, 1)
        pe.wait_ge(dve_read, s_lat.dve0 + 2)
        for t in range(TT):
            for k in range(2):
                pe.transpose(bank[2][:, k * S + t * P:k * S + (t + 1) * P], qn[:, t, k * P:(k + 1) * P], ident)
            pe.transpose(bank[3][:, t * P:(t + 1) * P], kv[:, t, :], ident)
            ins = pe.transpose(bank[3][:, S + t * P:S + (t + 1) * P],
                               kin[:, t, :, :].rearrange("p a d -> p (a d)"), ident)
        ins.then_inc(lat_T, 1)
        pe.wait_ge(qn_lo, 1)
        enter(s_uq)
        for b in range(s_uq.n):
            fm_block(s_uq, b, ff_hi, ff_lo)
        enter(s_qi)
        for b in range(s_qi.n):
            fm_block(s_qi, b, ff_hi, ff_lo)
        pe.wait_ge(ki_ready, 1)
        pe.wait_ge(act_read, s_qi.act0 + s_qi.n)
        for r in range(8):
            qt, r4 = r // 4, r % 4
            if r >= 2:
                pe.wait_ge(ix_relu, r - 1)
            for j in range(4):
                half, h = j // 2, 4 * r4 + 2 * (j % 2) + j // 2
                r64 = slice(64 * half, 64 * half + 64)
                ins = pe.matmul(bank3[2 + 2 * (r % 2) + half][:, j % 2, :],
                                qi[r64, h // 2, qt * P:(qt + 1) * P], kiT[r64, :], start=True, stop=True)
            ins.then_inc(ix_mm, 1)
        fm_stream(s_z, h_hi, h_lo)
        pe.wait_ge(mask_ready, 1)
        pe.wait_ge(pick_ready, 1)
        pe.wait_ge(tab_ready, 1)
        for n in range(NTILE + 2):
            if n < NTILE:
                lg = bank[2 + n % 2][:, 0:S]
                pe.wait_ge(hot_ready, n + 1)
                if n >= 2:
                    pe.wait_ge(lt_exp, n - 1)
                pe.matmul(lg, uq[:, QT * n:QT * n + QT, :].rearrange("p q h -> p (q h)"), kvT[:, :],
                          start=True, stop=False)
                for c in range(2):
                    for part in range(3):
                        pe.matmul(lg, tab_b[:, c, part, :], onehot[:, n % 2, c, :], start=False, stop=False)
                pe.matmul(lg, pick[:, (n % 16) * P:(n % 16 + 1) * P], mask[:, n // 16, :],
                          start=False, stop=True).then_inc(lt_mm, 1)
            if 1 <= n <= NTILE:
                m = n - 1
                pe.wait_ge(lt_p, m + 1)
                if m >= 2:
                    pe.wait_ge(lt_pT, m - 1)
                for k in range(2):
                    ins = pe.transpose(bank[4 + m % 2][:, k * P:(k + 1) * P],
                                       p2buf[:, m % 2, k * P:(k + 1) * P], ident)
                ins.then_inc(lt_T, 1)
            if n >= 2:
                m = n - 2
                pe.wait_ge(lt_pT, m + 1)
                if m >= 2:
                    pe.wait_ge(lt_o, m - 1)
                for k in range(2):
                    ins = pe.matmul(bank[6 + m % 2][:, 0:P], kv[:, k, :], p2T[:, m % 2, k, :],
                                    start=k == 0, stop=k == 1)
                ins.then_inc(lt_pv, 1)
        pe.wait_ge(uv_in, 16)
        pe.wait_ge(lt_o, NTILE)
        for h in range(H2):
            half = h % 2
            ins = pe.matmul(bank3[2 + h // 4][64 * half:64 * half + 64, h // 2 % 2, :], w_uv[:, h, :],
                            oT[:, h, :], start=True, stop=True)
            if h % 4 == 3:
                ins.then_inc(uv_mm, 1)
        fm_stream(s_ga, h_hi, h_lo)
        pe.wait_ge(uv_lo, 4)
        enter(s_oa)
        fm_stream(s_oa, ff_hi, ff_lo, k0=8)
        fm_stream(s_xbc, h_hi, h_lo)
        pe.wait_ge(act_read, s_ga.act0 + s_ga.n)
        pe.wait_ge(xbc_ready, 8)
        for n in range(8):
            t, q = n // 4, n % 4
            if n >= 2:
                pe.wait_ge(xs_ready, n - 1)
            for j in range(4):
                ins = pe.transpose(bank[4 + n % 2][:, j * P:(j + 1) * P],
                                   xsT[:, 4 * q + j, t * P:(t + 1) * P], ident)
            ins.then_inc(xs_T, 1)
        pe.wait_ge(xbc_ready, s_xbc.n)
        pe.wait_ge(xs_ready, 8)
        for h in range(HS + 1):
            if h < HS:
                g = h // 4
                if h % 4 == 0:
                    if g >= 1:
                        pe.wait_ge(cb_ready, g)
                    pe.matmul(bank[6][:, 0:S], bT[:, g, 0:P], cT[:, g, :], start=True, stop=True)
                    pe.matmul(bank[6][:, S:S + P], bT[:, g, P:S], cT[:, g, P:S], start=True, stop=True
                              ).then_inc(cb_mm, 1)
                pe.wait_ge(ud_ready, h + 1)
                if h >= 2:
                    pe.wait_ge(dec_ready, h - 1)
                sg = bank[2 + h % 2]
                pe.matmul(sg[:, 0:S], ud[:, h % 2, 0, :], tri_ones, start=True, stop=False,
                          skip_group_check=True)
                pe.matmul(sg[:, P:S], dtd[:, 1, 1, h:h + 1].broadcast_to([P, P]), tri, start=False,
                          stop=False, skip_group_check=True)
                pe.matmul(sg[:, S:S + P], ud[:, h % 2, 1, :], tri, start=False, stop=True,
                          skip_group_check=True).then_inc(seg_mm, 1)
            if h >= 1:
                m = h - 1
                i, half = m // 2, m % 2
                pe.wait_ge(m_mat, m + 1)
                if half == 0 and i >= 2:
                    pe.wait_ge(y_ready, i - 1)
                r64 = slice(64 * half, 64 * half + 64)
                pe.matmul(bank[4 + i % 2][r64, 0:S], x_dt[:, 0, 64 * m:64 * m + 64], m_buf[:, m % 2, 0:S],
                          start=True, stop=False)
                pe.matmul(bank[4 + i % 2][r64, P:S], x_dt[:, 1, 64 * m:64 * m + 64],
                          m_buf[:, m % 2, S:S + P], start=False, stop=True).then_inc(y_mm, 1)
        sum_squares(6, ysq, KI)
        fm_stream(s_gb, h_hi, h_lo)
        pe.wait_ge(y_lo, 1)
        enter(s_os)
        fm_stream(s_os, ff_hi, ff_lo)
        pe.wait_ge(h_lo_ready, 5)
        fm_stream(s_wo2, h_hi, h_lo)
        sum_squares(7, work)
        sum_squares(8, work)
        pe.wait_ge(h_lo_ready, 6)
        fm_stream(s_gu2, h_hi, h_lo)
        pe.wait_ge(ff_lo_ready, 22)
        fm_stream(s_dn2, ff_hi, ff_lo)
        sum_squares(9, work)
        pe.wait_ge(x_ready, 4)
        for t in range(TT):
            for k in range(KD):
                ins = pe.transpose(bank[2 + 2 * t + k // 4][:, (k % 4) * P:(k % 4 + 1) * P],
                                   xT[:, k, t * P:(t + 1) * P], ident)
                if k % 4 == 3:
                    ins.then_inc(out_T, 1)


def kernel(**inputs):
    import concourse.bacc as bacc
    from concourse.bass_utils import run_bass_kernel_spmd

    nc = bacc.Bacc("TRN2", target_bir_lowering=False, num_devices=1)
    mats, hot = shape_constants()
    arrays = {name: np.ascontiguousarray(x) for name, x in inputs.items()}
    arrays["shape_mats"], arrays["shape_hot"] = mats, hot
    a = {name: nc.dram_tensor(f"in_{name}", x.shape, mybir.dt.from_np(x.dtype),
                              kind="ExternalInput").ap() for name, x in arrays.items()}
    out = nc.dram_tensor("out", (1, S, D), F32, kind="ExternalOutput").ap()
    two_block_kernel(nc, a, out)
    r = run_bass_kernel_spmd(nc, [{f"in_{name}": x for name, x in arrays.items()}], core_ids=[0])
    return r.results[0]["out"]
```

```python
from contextlib import ExitStack

import numpy as np

import concourse.bass as bass
from concourse import mybir

F32 = mybir.dt.float32
F32R = mybir.dt.float32r
BF16 = mybir.dt.bfloat16
I32 = mybir.dt.int32
ALU = mybir.AluOpType
ACT = mybir.ActivationFunctionType
AX = mybir.AxisListType

P = 128
S = 256
TT = S // P
D = 1024
KD = D // P
MCOL = 384
CT = 2
NCH = KD // CT
RMS_EPS = 1.0e-6
NEG = -1.0e30
NEG_TAKEN = -3.0e38
H1, G1, DH = 8, 2, 64
KV1 = G1 * DH
NCMP, CSTRIDE, CBLOCK = 15, 16, 32
NCP = 16
FF = 2816
KF = FF // P
GW = 512
T5_FIRST = (0, 1, 2, 3, 4, 5, 6, 7, 8, 9, 10, 11, 12, 13, 14, 15, 16, 19, 21, 24, 27, 31, 35, 40,
            46, 52, 59, 67, 77, 87, 99, 113)
TOEP = 384
H2, CKV = 16, 128
QR = 256
TOPK = 64
T5B_FIRST = (0, 1, 2, 3, 4, 5, 6, 7, 8, 12, 16, 23, 32, 46, 64, 91)
QT = 8
NTILE = S // QT
DI = 2048
KI = DI // P
HS, NG, DS = 32, 8, 128
KX = 4096 // P
CONV = 4
RING = 4
UNIT = 1024
AHEAD = 2


def shape_constants():
    r = np.arange(P)
    ident = np.eye(P, dtype=np.float32)
    tri = (r[:, None] <= r[None, :]).astype(np.float32)
    upper = (r[:, None] > r[None, :]).astype(np.float32)
    ones = np.ones((P, P), np.float32)
    first, steps = np.zeros(32), np.zeros((32, 32), np.float32)
    for n in range(16):
        first[n] = -(T5B_FIRST[n + 1] - 1) if n < 15 else -1.0e9
        first[16 + n] = T5B_FIRST[n]
        steps[n, n] = steps[16 + n, 16 + n] = 1.0
        if n < 15:
            steps[n + 1, n] = -1.0
        if n:
            steps[15 + n if n > 1 else 0, 16 + n] = -1.0
    first[16], steps[:, 16] = 2.0e9, 0.0
    steps = np.tile(steps, (4, 4))
    cols = np.zeros((P, 4), np.float32)
    cols[:, 0] = np.tile(first, 4)
    cols[:, 2] = r >= CBLOCK - 1
    cols[:, 3] = RMS_EPS
    mats = np.concatenate([ident, upper, tri, ones, tri, ident[::-1], cols, steps], axis=1)
    hot = np.zeros((32, 2 * S), np.float32)
    for c in range(S):
        hot[max(b for b in range(32) if T5_FIRST[b] <= S - 1 - c), c] = 1.0
    return np.ascontiguousarray(mats, np.float32), hot


def at(i, per, const):
    return const if i is None else i * per + const


def two_block_kernel(nc, a, out):
    ctx = ExitStack()
    with ctx:
        _emit(nc, ctx, a, out)


def _emit(nc, ctx, a, out):
    def sem(name):
        return ctx.enter_context(nc.semaphore(name))

    def sb(name, shape, dt=F32, where=ctx):
        return where.enter_context(nc.sbuf_tensor(name, shape, dt))

    bank = [ctx.enter_context(nc.psum_tensor(f"bank{i}", [P, 512], F32)) for i in range(8)]
    bank3 = [b[:, :].rearrange("p (a n) -> p a n", a=2) for b in bank]

    w_raw = sb("w_raw", [P, RING, UNIT])
    w_hi = sb("w_hi", [P, RING, UNIT], F32R)
    w_lo = sb("w_lo", [P, RING, UNIT], F32R)
    h_hi = sb("h_hi", [P, KD, S], F32R)
    h_lo = sb("h_lo", [P, KD, S], F32R)
    ff_hi = sb("ff_hi", [P, KF, S], F32R)
    ff_lo = sb("ff_lo", [P, KF, S], F32R)
    xT = sb("xT", [P, KD, S])
    work = sb("work", [P, KD, S])
    mT = sb("mT", [P, KD, S])
    mats = sb("mats", [P, 6 * P + 4])
    ident, upper, tri, ones = (mats[:, i * P:(i + 1) * P] for i in range(4))
    tri_ones, tri_ones_tri, flip = mats[:, 2 * P:4 * P], mats[:, 2 * P:5 * P], mats[:, 5 * P:6 * P]
    reach_from, _, has_block, eps = (mats[:, 6 * P + i:6 * P + i + 1] for i in range(4))
    cols = sb("cols", [P, 3, P])
    rstd = sb("rstd", [P, S])
    var_sd = sb("var_sd", [P, 2, S])
    sd = var_sd[:, 1, :]
    warm = sb("warm", [P, 16])
    mod = sb("mod", [P, 48])
    gains = sb("gains", [P, 4, KD])
    c_silu = sb("c_silu", [P, KD])

    p1 = ExitStack()
    x_tok = sb("x_tok", [P, TT, D], F32, p1)
    table1 = sb("table1", [32, H1], F32, p1)
    toep = sb("toep", [P, H1, TOEP], F32, p1)
    w_gates = sb("w_gates", [P, KD, 24], F32, p1)
    gates = sb("gates", [P, TT, 24], F32, p1)
    qT = sb("qT", [P, H1 // 2, S], F32, p1)
    kdup = sb("kdup", [P, G1, 2, S], F32, p1)
    v_tok = sb("v_tok", [P, TT, 2 * KV1], F32, p1)
    tblk_hi = sb("tblk_hi", [P, 2, 16, 2 * NCMP], F32R, p1)
    tblk_lo = sb("tblk_lo", [P, 2, 16, 2 * NCMP], F32R, p1)
    tblk = sb("tblk", [P, 2, 16, 2 * NCMP], F32, p1)
    hid = sb("hid", [P, 2, 2, 2 * NCMP], F32, p1)
    w2 = sb("w2", [P, 2, 2, DH], F32, p1)
    kc_dup = sb("kc_dup", [P, 2 * NCMP], F32, p1)
    vc = sb("vc", [NCMP, G1, DH], F32, p1)
    zu = sb("zu", [P, 4, S], F32, p1)
    gv = sb("gv", [P, TT, GW], F32, p1)
    ln_st = sb("ln_st", [P, TT, 8], F32, p1)
    ln_bn = sb("ln_bn", [P, TT, 6], F32, p1)
    wsT = sb("wsT", [P, 8, P], F32, p1)
    bs = sb("bs", [P, 4, P], F32, p1)
    probs01 = sb("probs01", [P, 2, NCP + 2 * S], F32, p1)
    pT = sb("pT", [P, 2, 5, P], F32, p1)
    rows = tblk[:, :, :, :].rearrange("p n t j -> p (n t j)")[:, 0:3 * P].rearrange("p (t n) -> p t n", t=3)
    hot = zu[:, :, :].rearrange("p t s -> p (t s)")[0:32, 0:2 * S]
    bias_row = wsT[:, :, :].rearrange("p g t -> p (g t)")[0:H1, 0:2 * S]
    probs = [probs01[:, 0, :], probs01[:, 1, :],
             gv[:, :, :].rearrange("p t n -> p (t n)")[:, 0:NCP + 2 * S],
             tblk[:, :, :, :].rearrange("p n t j -> p (n t j)")[:, 0:NCP + 2 * S]]
    hid_tok = tblk[:, :, :, :].rearrange("p n t j -> p (n t j)")[0:2 * NCMP, 0:512].rearrange(
        "p (n c) -> p n c", n=2)
    ln_g, ln_b = (probs01[:, :, :].rearrange("p b n -> p (b n)")[:, i * GW:(i + 1) * GW] for i in (0, 1))
    ws = pT[:, :, :, :].rearrange("p b k q -> p (b k) q")[:, 0:8, :]
    st1 = sb("st1", [P, 4, 4, 4], F32, p1)
    mix = x_tok[:, :, :].rearrange("p t d -> p (t d)").rearrange("p (k s) -> p k s", k=KD)
    hankel_a = mT[:, :, :].rearrange("p k s -> p (k s)")[:, 0:5 * TOEP].rearrange("p (h f) -> p h f", h=5)
    hankel_b = x_tok[:, :, :].rearrange("p t d -> p (t d)")[:, 0:3 * TOEP].rearrange("p (h f) -> p h f", h=3)
    bias_dram = nc.dram_tensor("bias_dram", [H1, 2 * S], F32, kind="Internal").ap()
    p1.close()

    pf = ExitStack()
    ada_raw = sb("ada_raw", [P, 4, UNIT], F32, pf)
    ada_acc = sb("ada_acc", [P, 6 * D], F32, pf)
    row_of = sb("row_of", [P, 2 * 48 - 1], F32, pf)
    mod_rows = sb("mod_rows", [48, P], F32, pf)
    silu_g = sb("silu_g", [P, 2, S], F32, pf)
    ffv = sb("ffv", [P, 2, S], F32, pf)
    pf.close()

    p2 = ExitStack()
    szT = sb("szT", [P, KI, S], F32, p2)
    dtd = sb("dtd", [P, 2, TT, HS], F32, p2)
    dt_sc = sb("dt_sc", [P, 3, TT, HS], F32, p2)
    dt_bias = sb("dt_bias", [P, HS], F32, p2)
    a_row = sb("a_row", [P, HS], F32, p2)
    w_dt = sb("w_dt", [P, KD, HS], F32, p2)
    skip = sb("skip", [P, KI], F32, p2)
    pa = ExitStack()
    uq = sb("uq", [P, S, H2], F32, pa)
    oT = sb("oT", [P, H2, S], F32, pa)
    qi = mT
    oT_flat = oT[:, :, :].rearrange("p h s -> p (h s)")
    qn = oT_flat[:, 0:512].rearrange("p (t n) -> p t n", t=TT)
    rn = oT_flat[:, 512:1024].rearrange("p (k s) -> p k s", k=2)
    kin = oT_flat[:, 1024:1280].rearrange("p (t a d) -> p t a d", t=TT, a=2)
    junk = oT_flat[:, 1280:1280 + 6 * QR].rearrange("p (n k) -> p n k", n=6)
    mT_flat = mT[:, :, :].rearrange("p k s -> p (k s)")
    pick = mT_flat[:, 0:1024].bitcast(BF16)
    reached = mT_flat[:, 1024:1536].bitcast(BF16).rearrange("p (b c s) -> p b c s", b=2, c=2)
    work_flat = work[:, :, :].rearrange("p k s -> p (k s)")
    p2T = work_flat[:, 512:1024].rearrange("p (b k r) -> p b k r", b=2, k=2)
    w_uv = work_flat[:, 1024:2048].rearrange("p (h d) -> p h d", h=H2)
    relu_s = work[:, :, :].rearrange("p (b h) k -> p b h k", b=2)
    kv = sb("kv", [P, TT, CKV], F32, pa)
    kv_gain = sb("kv_gain", [P, CKV], F32, pa)
    st2 = sb("st2", [P, TT, 12], F32, pa)
    widx = sb("widx", [P, TT, 16], F32, pa)
    kvT = sb("kvT", [P, S], F32, pa)
    kiT = sb("kiT", [P, S], F32, pa)
    isc = sb("isc", [P, TT, S], F32, pa)
    p2buf = [work_flat[:, 0:S], work_flat[:, S:2 * S], isc[:, 0, :], isc[:, 1, :]]
    top8 = sb("top8", [P, 8], F32, pa)
    pos_i = sb("pos_i", [P, S + TT], I32, pa)
    pos_f = sb("pos_f", [P, S + TT], F32, pa)
    last_i = sb("last_i", [P, TT], I32, pa)
    last_f = sb("last_f", [P, TT], F32, pa)
    shut = sb("shut", [P, TT, S], F32, pa)
    mask = sb("mask", [P, TT, S], BF16, pa)
    own_pos = sb("own_pos", [P, S // 4], F32, pa)
    tab2 = sb("tab2", [32, H2], F32, pa)
    steps = sb("steps", [32, P], F32, pa)
    tab_r = sb("tab_r", [P, H2], F32, pa)
    tab_s = sb("tab_s", [P, 3, H2], BF16, pa)
    tab_b = sb("tab_b", [P, 2, 3, P], BF16, pa)
    st3 = sb("st3", [P, 4, 4], F32, pa)
    pa.close()
    pb = ExitStack()
    xsT = sb("xsT", [P, KI, S], F32, pb)
    x_dt = sb("x_dt", [P, TT, DI], F32, pb)
    bT = sb("bT", [P, NG, S], F32, pb)
    cT = sb("cT", [P, NG, S], F32, pb)
    cbm = var_sd[:, :, :].rearrange("p a s -> p (a s)")[:, 0:384]
    pb.close()
    p2.close()
    ud = work_flat[:, 0:512].rearrange("p (b t s) -> p b t s", b=2, t=2)
    decay = work_flat[:, 512:1280].rearrange("p (b n) -> p b n", b=2)
    m_buf = work_flat[:, 1280:2048].rearrange("p (b n) -> p b n", b=2)
    out_tok = w_raw[:, 0:TT, :]

    class Stream:

        units, blocks, act_blocks, dve_blocks = 0, 0, 0, 0

        def __init__(self, n, ks, reader):
            self.n, self.ks, self.reader = n, ks, reader
            self.u0, self.b0 = Stream.units, Stream.blocks
            self.act0, self.dve0 = Stream.act_blocks, Stream.dve_blocks
            Stream.units += n * len(ks)
            Stream.blocks += n
            Stream.act_blocks += n * (reader == "act") + (n // 2) * (reader == "pair")
            Stream.dve_blocks += n * (reader == "dve") + (n // 2) * (reader == "pair")

    s_kc = Stream(1, (4, 4), "dve")
    s_in = Stream(6, (4, 4), "act")
    s_cmp = Stream(2, (4, 4, 4, 4), "act")
    s_u = Stream(2, (4, 4), "act")
    s_wo = Stream(4, (4, 4), "act")
    s_gu = Stream(22, (4, 4), "pair")
    s_dn = Stream(4, (4, 4, 4, 4, 4, 2), "act")
    s_lat = Stream(2, (4, 4), "dve")
    s_qi = Stream(4, (2,), "act")
    s_uq = Stream(8, (2,), "act")
    s_z = Stream(4, (4, 4), "act")
    s_z2 = Stream(4, (4, 4), "act")
    s_ga = Stream(4, (4, 4), "act")
    s_oa = Stream(4, (4, 4), "dve")
    s_xbc = Stream(16, (4, 4), "dve")
    s_gb = Stream(4, (4, 4), "act")
    s_os = Stream(4, (4, 4, 4, 4), "dve")
    s_wo2 = Stream(4, (4, 4), "act")
    s_gu2 = Stream(22, (4, 4), "pair")
    s_dn2 = Stream(4, (4, 4, 4, 4, 4, 2), "act")
    n_units = Stream.units

    landed = [sem(f"landed{i}") for i in range(RING)]
    hi_ready, lo_ready, unit_used = sem("hi_ready"), sem("lo_ready"), sem("unit_used")
    act_read, dve_read = sem("act_read"), sem("dve_read")
    act_own, dve_own, pool_own = sem("act_own"), sem("dve_own"), sem("pool_own")
    consts_in, rows_in, x_in, hot_in = sem("consts_in"), sem("rows_in"), sem("x_in"), sem("hot_in")
    gates_in, mlp_in, gmlp_in, ln_in = sem("gates_in"), sem("mlp_in"), sem("gmlp_in"), sem("ln_in")
    bias_out, toep_in, toep_mm, toep_ready = (sem("bias_out"), sem("toep_in"), sem("toep_mm"),
                                              sem("toep_ready"))
    ada_in = [sem(f"ada_in{i}") for i in range(4)]
    lat_in, pos_in, tab_in, ssd_in, uv_in = (sem("lat_in"), sem("pos_in"), sem("tab_in"),
                                             sem("ssd_in"), sem("uv_in"))
    out_done = sem("out_done")
    rows_T, cols_ready, x_T, x_act, x_dve = (sem("rows_T"), sem("cols_ready"), sem("x_T"),
                                             sem("x_act"), sem("x_dve"))
    bias_mm, bias_ready = sem("bias_mm"), sem("bias_ready")
    sq_ready, ss_ready, sd_ready = sem("sq_ready"), sem("ss_ready"), sem("sd_ready")
    h_ready, h_hi_ready, h_lo_ready = sem("h_ready"), sem("h_hi_ready"), sem("h_lo_ready")
    x_ready = sem("x_ready")
    gate_mm, gates_act, gates_ready = sem("gate_mm"), sem("gates_act"), sem("gates_ready")
    tblk_hi_ready, tblk_lo_ready = sem("tblk_hi_ready"), sem("tblk_lo_ready")
    hid_T = sem("hid_T")
    hid_ready, kcvc_mm, kcvc_ready = sem("hid_ready"), sem("kcvc_mm"), sem("kcvc_ready")
    ws_T, wsT_ready, ln_var, ln_sd, zv_ready, sv_mm, mix_gm = (
        sem("ws_T"), sem("wsT_ready"), sem("ln_var"), sem("ln_sd"), sem("zv_ready"), sem("sv_mm"),
        sem("mix_gm"))
    lg_mm, max_ready, exp_ready, pn_ready, pT_mm, pT_ready, pv_mm, att_ready = (
        sem("lg_mm"), sem("max_ready"), sem("exp_ready"), sem("pn_ready"), sem("pT_mm"),
        sem("pT_ready"), sem("pv_mm"), sem("att_ready"))
    ff_hi_ready, ff_lo_ready = sem("ff_hi_ready"), sem("ff_lo_ready")
    ada_used, ada_mm, c_ready, mod_ready = sem("ada_used"), sem("ada_mm"), sem("c_ready"), sem("mod_ready")
    lat_sq, lat_var, lat_sd, lat_ready, lat_T, qn_ready, qn_hi, qn_lo, ki_ready = (
        sem("lat_sq"), sem("lat_var"), sem("lat_sd"), sem("lat_ready"), sem("lat_T"),
        sem("qn_ready"), sem("qn_hi"), sem("qn_lo"), sem("ki_ready"))
    ix_mm, ix_relu, ix_sum, mask_ready, pick_ready, tab_ready = (
        sem("ix_mm"), sem("ix_relu"), sem("ix_sum"), sem("mask_ready"), sem("pick_ready"),
        sem("tab_ready"))
    reach_ready, lt_mm, lt_max, lt_exp, lt_p, lt_T, lt_pT, lt_pv, lt_o = (
        sem("reach_ready"), sem("lt_mm"), sem("lt_max"), sem("lt_exp"), sem("lt_p"), sem("lt_T"),
        sem("lt_pT"), sem("lt_pv"), sem("lt_o"))
    step_mm = sem("step_mm")
    row_ready, mod_mm, mod_copied = sem("row_ready"), sem("mod_mm"), sem("mod_copied")
    uv_mm, uv_hi, uv_lo = sem("uv_mm"), sem("uv_hi"), sem("uv_lo")
    dt_mm, dt_a, dt_b, dt_ready, xbc_ready = (
        sem("dt_mm"), sem("dt_a"), sem("dt_b"), sem("dt_ready"), sem("xbc_ready"))
    xs_T, xs_ready, cb_mm, cb_ready, ud_ready, seg_mm, dec_ready, m_mat, y_mm, y_ready = (
        sem("xs_T"), sem("xs_ready"), sem("cb_mm"), sem("cb_ready"), sem("ud_ready"),
        sem("seg_mm"), sem("dec_ready"), sem("m_mat"), sem("y_mm"), sem("y_ready"))
    tap_ready = sem("tap_ready")
    sz_ready = sem("sz_ready")
    y_gain, y_hi, y_lo, mix2_ready = sem("y_gain"), sem("y_hi"), sem("y_lo"), sem("mix2_ready")
    out_T, out_act, out_ready = sem("out_T"), sem("out_act"), sem("out_ready")

    C_MIX, C_MIXP, C_FFN, C_FFNP, C_MIX2, C_MIXP2, C_FFN2, C_FFNP2, C_C = (8 * i for i in range(9))
    C_SSD, C_CONVB, C_QN, C_KI = 72, 88, 120, 122
    R_USED = (123, 128, 80)
    ADA_B, POS_K, POS_V = 0, 48, 64

    SQ0 = (None, 0, 4, 8, 12, 16, 20, 28, 32, 36)

    def xbc_tiles(b):
        return (xsT[:, 2 * b:2 * b + 2, :] if b < 8 else bT[:, 2 * b - 16:2 * b - 14, :] if b < 12
                else cT[:, 2 * b - 24:2 * b - 22, :])

    def chunk(c):
        return slice(CT * c, CT * c + CT)

    def col(tile, c):
        return cols[:, tile, c:c + 1]

    def fill_rows():
        def v(name):
            x = a[name]
            return (x if len(x.shape) == 1 else x.rearrange("a n -> (a n)")).rearrange(
                "(t p) -> t p", p=P)
        for c, name in ((C_MIX, "norm_mix_pre"), (C_MIXP, "norm_mix_post"), (C_FFN, "norm_ffn_pre"),
                        (C_FFNP, "norm_ffn_post"), (C_MIX2, "pre_norm_mix_2"),
                        (C_MIXP2, "post_norm_mix_2"), (C_FFN2, "pre_norm_ffn_2"),
                        (C_FFNP2, "post_norm_ffn_2"), (C_C, "c_2"), (C_SSD, "ssd_norm_2"),
                        (C_CONVB, "conv_b_2"), (C_QN, "q_norm_2")):
            x = v(name)
            yield rows[c:c + x.shape[0], 0, :], x
        ki = a["kidx_norm_2"].rearrange("(a n) -> a n", a=1)
        yield rows[C_KI:C_KI + 1, 0, 0:64], ki
        yield rows[C_KI:C_KI + 1, 0, 64:128], ki
        yield rows[:, 1, :], a["conv_w_2"].rearrange("w (t p) -> (w t) p", p=P)
        yield rows[0:48, 2, :], v("ada_b_2")
        yield rows[POS_K:POS_K + 16, 2, :], a["cmp_pos_k"][0].rearrange("(t a) d -> t (a d)", a=2)
        yield rows[POS_V:POS_V + 16, 2, :], a["cmp_pos_v"][0].rearrange("(t a) d -> t (a d)", a=2)

    n_rows_dma = 18

    w_in, w_in2 = a["w_in"][0], a["w_in_2"]
    TILES1 = [(h, qt) for hp in range(H1 // 2) for qt in range(TT) for h in (2 * hp, 2 * hp + 1)]

    block = ctx.enter_context(nc.Block())

    @block.sync
    def _(sp):
        for t in range(TT):
            sp.dma_start(x_tok[:, t, :], a["x"][0, t * P:(t + 1) * P, :]).then_inc(x_in, 16)
        for dst, src in list(fill_rows())[::2]:
            sp.dma_start(dst, src).then_inc(rows_in, 16)

        def load(i, per, u, src, nk, ncol, part=None):
            dst = w_raw[:, u % RING, 0:nk * ncol].rearrange("p (k c) -> p k c", k=nk)
            if u >= RING:
                sp.wait_ge(hi_ready, at(i, per, u - RING + 1))
                sp.wait_ge(lo_ready, at(i, per, u - RING + 1))
            sp.dma_start(dst, src.rearrange("(k p) c -> p k c", p=P)).then_inc(landed[u % RING], 16)

        def load_block(st, b, w, c0, i=None, per=0, ci=0, ncol=256):
            k, u = 0, st.u0 + b * len(st.ks)
            for nk in st.ks:
                load(i, per, u, w[k * P:(k + nk) * P, bass.ds(at(i, ci, c0), ncol)], nk, ncol)
                k += nk
                u += 1

        def load_stream(st, w, c0):
            n = 2 * len(st.ks)
            with sp.Fori(0, st.n // 2) as i:
                load_block(st, 0, w, c0, i, n, 512)
                load_block(st, 1, w, c0 + 256, i, n, 512)

        def load_pairs(st, w, half):
            with sp.Fori(0, st.n // 2) as i:
                load_block(st, 0, w, 0, i, 2 * len(st.ks), 256)
                load_block(st, 1, w, half, i, 2 * len(st.ks), 256)

        load_block(s_kc, 0, w_in, 512)
        load_block(s_in, 0, w_in, 768)
        load_block(s_in, 1, w_in, 0)
        load_block(s_in, 2, w_in, 256)
        load_block(s_in, 3, w_in, 1024)
        load_block(s_in, 4, w_in, 1816)
        load_block(s_in, 5, w_in, 2072)
        load_block(s_cmp, 0, a["cmp_w1_k"][0], 0)
        load_block(s_cmp, 1, a["cmp_w1_v"][0], 0)
        load_block(s_u, 0, w_in, 1304)
        load_block(s_u, 1, w_in, 1560)
        load_stream(s_wo, a["w_out"][0], 0)
        load_pairs(s_gu, a["w_gate_up"][0], FF)
        load_stream(s_dn, a["w_down"][0], 0)
        load_block(s_lat, 0, w_in2, 0)
        load_block(s_lat, 1, w_in2, 256, ncol=208)
        for b in range(s_qi.n):
            load_block(s_qi, b, a["w_qidx_2"], 256 * b)
        for b in range(s_uq.n):
            load_block(s_uq, b, a["w_uq_2"], 256 * b)
        load_stream(s_z, w_in2, 464)
        load_stream(s_z2, w_in2, 464 + 256 * s_z.n)
        load_stream(s_ga, w_in2, 6640)
        load_stream(s_oa, a["w_o_attn_2"], 0)
        load_stream(s_xbc, w_in2, 2512)
        load_stream(s_gb, w_in2, 7664)
        load_stream(s_os, a["w_o_ssd_2"], 0)
        load_stream(s_wo2, a["w_out_2"], 0)
        load_pairs(s_gu2, a["w_ffn_in_2"], FF)
        load_stream(s_dn2, a["w_ffn_out_2"], 0)
        for half, ready in ((0, out_act), (1, out_ready)):
            for t in range(TT):
                sp.wait_ge(ready, t + 1)
                c = slice(512 * half, 512 * half + 512)
                sp.dma_start(out[0, t * P:(t + 1) * P, c], out_tok[:, t, c]).then_inc(out_done, 16)
        sp.wait_ge(out_done, 2 * 16 * TT)

    @block.gpsimd
    def _(pool):
        pool.dma_start(hot[:, :], a["shape_hot"]).then_inc(hot_in, 16)
        pool.dma_start(table1[:, :], a["rel_bias"]).then_inc(hot_in, 16)
        pool.dma_start(w_gates[:, :, :], w_in[:, 1280:1304].rearrange("(k p) c -> p k c", p=P)
                       ).then_inc(gates_in, 16)
        for n, name in enumerate(("cmp_w2_k", "cmp_w2_v")):
            pool.dma_start(w2[:, n, :, :], a[name][0].rearrange("(k p) c -> p k c", p=P)
                           ).then_inc(mlp_in, 16)
        pool.dma_start(ws[:, :, :], a["gmlp_w_s"][0].rearrange("g t s -> t g s")).then_inc(gmlp_in, 16)
        for j in range(2):
            pool.dma_start(bs[j * 64:j * 64 + 64, :, :],
                           bass.AP(a["gmlp_b_s"].tensor, j * P, [[0, 64], [2 * P, 4], [1, P]])
                           ).then_inc(gmlp_in, 16)
        for t, name in ((ln_g, "gmlp_ln_g"), (ln_b, "gmlp_ln_b")):
            pool.dma_start(t[:, :], bass.AP(a[name].tensor, 0, [[0, P], [1, GW]])).then_inc(ln_in, 16)
        pool.wait_ge(bias_ready, 1)
        pool.dma_start(bias_dram, bias_row[:, :]).then_inc(bias_out, 16)
        pool.wait_ge(bias_out, 16)
        pool.wait_ge(x_T, 2)
        for h0, h1, dst in ((0, 5, hankel_a), (5, H1, hankel_b)):
            pool.dma_start(dst, bass.AP(bias_dram.tensor, h0 * 2 * S, [[1, P], [2 * S, h1 - h0], [1, TOEP]])
                           ).then_inc(toep_in, 16)
        pool.wait_ge(x_ready, NCH)
        ada = a["ada_w_2"].rearrange("(k p) c -> p k c", p=P)

        def load_ada(i, per, c):
            for j in range(4):
                if c or i is not None:
                    pool.wait_ge(ada_used, at(i, per, 8 * c + 2 * j - 6))
                pool.dma_start(ada_raw[:, j, 0:2 * MCOL].rearrange("p (k c) -> p k c", k=2),
                               ada[:, 2 * j:2 * j + 2, bass.ds(at(i, MCOL, MCOL * c), MCOL)]
                               ).then_inc(ada_in[j], 16)

        pool.memset(row_of[:, 0:47], 0.0)
        pool.memset(row_of[:, 48:95], 0.0)
        pool.memset(row_of[:, 47:48], 1.0).then_inc(row_ready, 1)
        load_ada(None, 0, 0)
        with pool.Fori(0, 11) as i:
            load_ada(i, 8, 1)
        for c in range(12, 6 * D // MCOL):
            load_ada(None, 0, c)
        pool.wait_ge(x_ready, 2 * NCH)
        pool.wait_ge(mod_ready, 1)
        pool.dma_start(kv_gain[:, :], bass.AP(a["kv_norm_2"].tensor, 0, [[0, P], [1, CKV]])).then_inc(lat_in, 16)
        pool.dma_start(pos_i[:, 0:S], bass.AP(a["positions_2"].tensor, 0, [[0, P], [1, S]])).then_inc(pos_in, 16)
        pool.dma_start(pos_i[:, S:S + TT], a["positions_2"][0].rearrange("(t p) -> p t", p=P),
                       allow_slow_non_contiguous=True).then_inc(pos_in, 16)
        pool.dma_start(tab2[:, :], a["rel_bias_2"]).then_inc(tab_in, 16)
        pool.dma_start(steps[:, :], a["shape_mats"][0:32, 6 * P + 4:]).then_inc(tab_in, 16)
        pool.dma_start(w_dt[:, :, :], w_in2[:, 6608:6640].rearrange("(k p) c -> p k c", p=P)).then_inc(ssd_in, 16)
        pool.dma_start(dt_bias[:, :], bass.AP(a["dt_bias_2"].tensor, 0, [[0, P], [1, HS]])).then_inc(ssd_in, 16)
        pool.dma_start(a_row[:, :], bass.AP(a["a_log_2"].tensor, 0, [[0, P], [1, HS]])).then_inc(ssd_in, 16)
        for j in range(2):
            pool.dma_start(skip[64 * j:64 * j + 64, :],
                           bass.AP(a["d_skip_2"].tensor, j, [[0, 64], [2, KI]]),
                           allow_slow_non_contiguous=True).then_inc(ssd_in, 16)
        pool.wait_ge(ix_sum, 8)
        pool.dma_start(w_uv[:, :, :], a["w_uv_2"].rearrange("h c d -> c h d")).then_inc(uv_in, 16)
        pool.memset(pick[:, :], 1.0).then_inc(pool_own, 1)
        pool.wait_ge(pool_own, 1)
        pool.affine_select(out=pick[:, :], in_=pick[:, :], pattern=[[1, 16 * P]], compare_op=ALU.is_ge,
                           fill=0.0, base=0, channel_multiplier=-16).then_inc(pool_own, 1)
        pool.wait_ge(pool_own, 2)
        pool.affine_select(out=pick[:, :], in_=pick[:, :], pattern=[[-1, 16 * P]], compare_op=ALU.is_ge,
                           fill=0.0, base=15, channel_multiplier=16).then_inc(pick_ready, 1)
        pool.wait_ge(tab_ready, 1)
        for n in range(NTILE):
            if n >= 2:
                pool.wait_ge(lt_mm, n - 1)
            for c in range(2):
                ins = pool.tensor_scalar(reached[:, n % 2, c, :], pos_f[:, 0:S],
                                         own_pos[:, 2 * n + c:2 * n + c + 1], None, ALU.is_ge)
            ins.then_inc(reach_ready, 1)
        pool.wait_ge(dt_ready, 1)
        for h in range(HS):
            if h >= 2:
                pool.wait_ge(seg_mm, h - 1)
            for t in range(TT):
                ins = pool.tensor_scalar(ud[:, h % 2, t, :], upper, dtd[:, 1, t, h:h + 1], None, ALU.mult)
            ins.then_inc(ud_ready, 1)

    @block.scalar
    def _(act):
        own, done_units = [0], [0]

        def link(ins):
            own[0] += 1
            ins.then_inc(act_own, 1)
            act.wait_ge(act_own, own[0])

        def split(i, per, u, n=UNIT):
            act.wait_ge(landed[u % RING], at(i, 4 * per, 16 * (u // RING + 1)))
            if u >= RING:
                act.wait_ge(unit_used, at(i, per, u - RING + 1))
            act.activation(w_hi[:, u % RING, 0:n], w_raw[:, u % RING, 0:n], ACT.Copy).then_inc(hi_ready, 1)

        def split_to(u_end):
            while done_units[0] < min(u_end, n_units):
                split(None, 0, done_units[0])
                done_units[0] += 1

        def before_block(st, b):
            end = st.u0 + (b + 1) * len(st.ks)
            split_to(end + AHEAD)
            act.wait_ge(unit_used, end)

        def loop_block(st, b, i, blocks_per_turn=2):
            n = len(st.ks)
            for j in range(n):
                split(i, n * blocks_per_turn, st.u0 + b * n + AHEAD + j)
            act.wait_ge(unit_used, at(i, n * blocks_per_turn, st.u0 + (b + 1) * n))

        def end_loop(st):
            done_units[0] = st.u0 + st.n * len(st.ks) + AHEAD

        def square_x(m):
            for c in range(NCH):
                act.wait_ge(x_ready, NCH * (m - 1) + c + 1)
                act.activation(work[:, chunk(c), :], xT[:, chunk(c), :], ACT.Square).then_inc(sq_ready, 1)

        def root(n, count=D):
            act.activation(warm[:, n:n + 1], eps, ACT.Sqrt)
            act.wait_ge(ss_ready, n)
            act.activation(sd, bank[7][:, 0:S], ACT.Sqrt, bias=eps, scale=1.0 / count).then_inc(sd_ready, 1)

        def operand_hi(n, src, ready, base):
            for c in range(NCH):
                act.wait_ge(ready, base + c + 1)
                act.activation(h_hi[:, chunk(c), :], src[:, chunk(c), :], ACT.Copy).then_inc(h_hi_ready, 1)

        def read_m(st):
            for b in range(st.n):
                before_block(st, b)
                act.activation(work[:, chunk(b), :], bank3[(st.b0 + b) % 2], ACT.Square).then_inc(sq_ready, 1)
                act.activation(mT[:, chunk(b), :], bank3[(st.b0 + b) % 2], ACT.Copy).then_inc(act_read, 1)

        def read_pairs(st):
            with act.Fori(0, st.n // 2) as i:
                loop_block(st, 0, i)
                act.wait_ge(dve_read, at(i, 1, st.dve0))
                act.activation(silu_g[:, :, :], bank3[st.b0 % 2], ACT.Silu).then_inc(act_read, 1)
                for j in range(2):
                    split(i, 4, st.u0 + 4 + j)
                act.wait_ge(dve_read, at(i, 1, st.dve0 + 1))
                act.activation(ff_hi[:, bass.ds(at(i, 2, 0), 2), :], ffv[:, :, :], ACT.Copy
                               ).then_inc(ff_hi_ready, 1)
            end_loop(st)

        act.dma_start(mats[:, :], a["shape_mats"][:, 0:6 * P + 4]).then_inc(consts_in, 16)
        for dst, src in list(fill_rows())[1::2]:
            act.dma_start(dst, src).then_inc(rows_in, 16)
        for j in (0, 1):
            act.wait_ge(x_T, j + 1)
            act.activation(xT[:, chunk(j), :], bank3[2 + j], ACT.Copy)
            act.activation(work[:, chunk(j), :], bank3[2 + j], ACT.Square).then_inc(sq_ready, 1)
        for j in (2, 3):
            act.wait_ge(x_dve, j - 1)
            act.activation(work[:, chunk(j), :], xT[:, chunk(j), :], ACT.Square).then_inc(sq_ready, 1)
        root(1)
        split_to(AHEAD)
        operand_hi(1, work, h_ready, 0)
        split_to(s_kc.u0 + 2 + AHEAD)
        def read_kv(b, br):
            before_block(s_in, b)
            src = bank3[(s_in.b0 + b) % 2]
            for g in range(G1):
                for half in range(2):
                    act.activation(kdup[64 * half:64 * half + 64, g, br, :],
                                   src[64 * g:64 * g + 64, 0, :], ACT.Copy)
            act.activation(v_tok[:, :, br * KV1:(br + 1) * KV1],
                           src[:, 1, :].rearrange("p (t d) -> p t d", t=TT), ACT.Copy
                           ).then_inc(act_read, 1)

        read_kv(0, 0)
        act.wait_ge(dve_read, 1)
        act.activation(tblk_hi[:, :, :, :], tblk[:, :, :, :], ACT.Copy).then_inc(tblk_hi_ready, 1)
        for b in (1, 2):
            before_block(s_in, b)
            act.activation(qT[:, 2 * b - 2:2 * b, :], bank3[(s_in.b0 + b) % 2], ACT.Copy,
                           scale=DH ** -0.5).then_inc(act_read, 1)
        read_kv(3, 1)
        for b in (4, 5):
            before_block(s_in, b)
            act.activation(gv[:, :, 256 * (b - 4):256 * (b - 3)], bank3[(s_in.b0 + b) % 2],
                           ACT.Gelu_apprx_tanh).then_inc(act_read, 1)
        act.wait_ge(ln_var, 1)
        act.activation(ln_st[:, :, 2:3], ln_st[:, :, 1:2], ACT.Sqrt).then_inc(ln_sd, 1)
        act.wait_ge(gate_mm, 1)
        act.activation(gates[:, :, :], bank[7][:, 0:48].rearrange("p (t n) -> p t n", t=TT),
                       ACT.Sigmoid).then_inc(gates_act, 1)
        for b in range(2):
            before_block(s_cmp, b)
            act.activation(hid_tok[:, b, :], bank[(s_cmp.b0 + b) % 2][0:2 * NCMP, 0:256],
                           ACT.Gelu_apprx_tanh).then_inc(act_read, 1)
        for b in range(s_u.n):
            if b == 1:
                act.wait_ge(hid_T, 1)
                act.activation(hid[:, :, :, :].rearrange("p n m j -> p (n m j)"), bank[4][:, 0:8 * NCMP],
                               ACT.Copy).then_inc(hid_ready, 1)
            before_block(s_u, b)
            act.activation(zu[:, 2 * b:2 * b + 2, :], bank3[(s_u.b0 + b) % 2],
                           ACT.Gelu_apprx_tanh).then_inc(act_read, 1)
        act.wait_ge(kcvc_mm, 1)
        act.activation(kc_dup[:, :], bank[6][:, 0:2 * NCMP], ACT.Copy)
        act.activation(vc[:, :, :], bank[6][0:NCMP, 128:256].rearrange("p (g d) -> p g d", g=2),
                       ACT.Copy).then_inc(kcvc_ready, 1)
        for n in range(len(TILES1) + 2):
            if n < len(TILES1):
                nk = P * (TILES1[n][1] + 1)
                act.wait_ge(max_ready, n + 1)
                for br, (c0, cn) in enumerate(((0, NCMP), (NCP, nk), (NCP + S, nk))):
                    ins = act.activation(probs[n % 4][:, c0:c0 + cn], probs[n % 4][:, c0:c0 + cn], ACT.Exp,
                                         bias=st1[:, n % 4, 0, br:br + 1],
                                         accum_out=st1[:, n % 4, 1, br:br + 1])
                ins.then_inc(exp_ready, 1)
            if n >= 2:
                m = n - 2
                qt = TILES1[m][1]
                act.wait_ge(pT_mm, m + 1)
                if m >= 2:
                    act.wait_ge(pv_mm, m - 1)
                act.activation(pT[0:NCMP, m % 2, 0, :], bank[6][0:NCMP, 0:P], ACT.Copy)
                act.activation(pT[:, m % 2, 1:3 + 2 * qt, :],
                               bank[m % 2][:, 0:2 * (qt + 1) * P].rearrange("p (k q) -> p k q", q=P),
                               ACT.Copy).then_inc(pT_ready, 1)
        act.wait_ge(att_ready, H1 // 2)
        for c in range(NCH):
            act.activation(h_hi[:, chunk(c), :], mix[:, chunk(c), :], ACT.Copy).then_inc(h_hi_ready, 1)
        read_m(s_wo)
        root(2)
        square_x(1)
        root(3)
        act.activation(c_silu[:, :], cols[:, 0, C_C:C_C + KD], ACT.Silu).then_inc(c_ready, 1)
        operand_hi(3, work, h_ready, NCH)
        read_pairs(s_gu)
        read_m(s_dn)
        root(4)

        square_x(2)
        root(5)
        operand_hi(4, work, h_ready, 2 * NCH)
        for b in range(2):
            before_block(s_lat, b)
            for t in range(TT):
                if b == 0:
                    act.activation(junk[:, t, :], bank3[s_lat.b0 % 2][:, t, :], ACT.Square,
                                   accum_out=st2[:, t, 0:1])
                else:
                    act.activation(junk[:, 2 + t, 0:CKV], bank3[(s_lat.b0 + 1) % 2][:, t, 0:CKV], ACT.Square,
                                   accum_out=st2[:, t, 1:2])
                    ins = act.activation(junk[:, 4 + t, 0:64], bank3[(s_lat.b0 + 1) % 2][:, t, CKV:CKV + 64],
                                         ACT.Square, accum_out=st2[:, t, 2:3])
        ins.then_inc(lat_sq, 1)
        act.wait_ge(lat_var, 1)
        act.activation(st2[:, :, 6:9], st2[:, :, 3:6], ACT.Sqrt).then_inc(lat_sd, 1)
        act.wait_ge(qn_ready, 1)
        act.activation(ff_hi[:, 0:2, :], rn[:, :, :], ACT.Copy).then_inc(qn_hi, 1)
        for b in range(s_qi.n):
            before_block(s_qi, b)
            act.activation(qi[:, 2 * b:2 * b + 2, :], bank3[(s_qi.b0 + b) % 2], ACT.Copy
                           ).then_inc(act_read, 1)
        for r in range(8):
            act.wait_ge(ix_mm, r + 1)
            if r >= 2:
                act.wait_ge(ix_sum, r - 1)
            for j in range(2):
                ins = act.activation(relu_s[:, r % 2, 2 * j:2 * j + 2, :], bank3[2 + 2 * (r % 2) + j],
                                     ACT.Relu)
            ins.then_inc(ix_relu, 1)
        for b in range(s_uq.n):
            before_block(s_uq, b)
            act.activation(uq[:, :, 2 * b:2 * b + 2].rearrange("p q h -> p h q"),
                           bank3[(s_uq.b0 + b) % 2], ACT.Copy, scale=CKV ** -0.5).then_inc(act_read, 1)

        def read_z(st, b, tile):
            before_block(st, b)
            act.activation(szT[:, tile:tile + 2, :], bank3[(st.b0 + b) % 2], ACT.Copy).then_inc(act_read, 1)

        for b in range(s_z.n):
            read_z(s_z, b, 2 * b)
        for n in range(NTILE + 2):
            if n < NTILE:
                act.wait_ge(lt_max, n + 1)
                if n >= 4:
                    act.wait_ge(lt_T, n - 3)
                act.activation(p2buf[n % 4], bank[2 + n % 2][:, 0:S], ACT.Exp,
                               bias=st3[:, n % 4, 0:1], accum_out=st3[:, n % 4, 1:2]).then_inc(lt_exp, 1)
            if n >= 2:
                m = n - 2
                act.wait_ge(lt_T, m + 1)
                if m >= 2:
                    act.wait_ge(lt_pv, m - 1)
                act.activation(p2T[:, m % 2, :, :],
                               bank[4 + m % 2][:, 0:S].rearrange("p (k r) -> p k r", k=2),
                               ACT.Copy).then_inc(lt_pT, 1)
            if n % 4 == 0 and n < NTILE:
                split_to(s_z2.u0 + n // 4 + 1 + AHEAD)
            if n % 8 == 1 and n > 8:
                read_z(s_z2, n // 8 - 1, 2 * s_z.n + 2 * (n // 8 - 1))
        for b in range(4):
            act.wait_ge(uv_mm, b + 1)
            act.activation(ff_hi[:, 8 + 2 * b:10 + 2 * b, :], bank3[2 + b], ACT.Copy).then_inc(uv_hi, 1)
        act.wait_ge(act_read, s_z2.act0 + s_z2.n)
        act.activation(szT[:, :, :], szT[:, :, :], ACT.Silu).then_inc(sz_ready, 1)
        with act.Fori(0, s_ga.n // 2) as i:
            for b in range(2):
                loop_block(s_ga, b, i)
                act.activation(mT[:, bass.ds(at(i, 4, 2 * b), 2), :], bank3[(s_ga.b0 + b) % 2],
                               ACT.Sigmoid).then_inc(act_read, 1)
        end_loop(s_ga)
        for b in range(s_oa.n):
            split_to(s_oa.u0 + (b + 1) * 2 + AHEAD)
        act.wait_ge(dt_a, 1)
        link(act.activation(dt_sc[:, 1, :, :], dt_sc[:, 1, :, :], ACT.Exp, scale=-1.0))
        link(act.activation(dt_sc[:, 1, :, :], dt_sc[:, 1, :, :], ACT.Ln, bias=1.0))
        act.activation(a_row[:, :], a_row[:, :], ACT.Exp).then_inc(dt_b, 1)
        for b in range(s_xbc.n + 1):
            if b < s_xbc.n:
                before_block(s_xbc, b)
                for s in range(2):
                    ins = act.activation(xbc_tiles(b)[:, s, :], bank3[(s_xbc.b0 + b) % 2][:, s, :], ACT.Identity,
                                         scale=col(1, (CONV - 1) * KX + 2 * b + s),
                                         bias=col(0, C_CONVB + 2 * b + s))
                ins.then_inc(tap_ready, 1)
            if b >= 1:
                act.wait_ge(dve_read, s_xbc.dve0 + b)
                act.activation(xbc_tiles(b - 1), xbc_tiles(b - 1), ACT.Silu).then_inc(xbc_ready, 1)
        def square_y(i):
            act.wait_ge(y_ready, i + 1)
            ins = act.activation(xsT[:, i, :], szT[:, i, :], ACT.Square)
            if i % CT == CT - 1:
                ins.then_inc(sq_ready, 1)

        for h in range(HS):
            act.wait_ge(seg_mm, h + 1)
            if h >= 2:
                act.wait_ge(m_mat, h - 1)
            act.activation(decay[:, h % 2, :], bank[2 + h % 2][:, 0:384], ACT.Exp).then_inc(dec_ready, 1)
            if h >= 4 and h % 2 == 0:
                square_y((h - 4) // 2)
        square_y(KI - 2)
        square_y(KI - 1)
        root(6, DI)
        act.wait_ge(y_gain, 1)
        act.activation(ff_hi[:, 0:KI, :], szT[:, :, :], ACT.Copy).then_inc(y_hi, 1)
        with act.Fori(0, s_gb.n // 2) as i:
            for b in range(2):
                loop_block(s_gb, b, i)
                act.activation(work[:, bass.ds(at(i, 4, 2 * b), 2), :], bank3[(s_gb.b0 + b) % 2],
                               ACT.Sigmoid).then_inc(act_read, 1)
        end_loop(s_gb)
        for b in range(s_os.n):
            split_to(s_os.u0 + (b + 1) * 4 + AHEAD)
        operand_hi(5, mT, mix2_ready, 0)
        read_m(s_wo2)
        root(7)
        square_x(3)
        root(8)
        operand_hi(6, work, h_ready, 3 * NCH)
        read_pairs(s_gu2)
        read_m(s_dn2)
        root(9)
        act.wait_ge(out_T, 1)
        for t in range(TT):
            act.activation(out_tok[:, t, 0:512], bank[2 + 2 * t][:, :], ACT.Copy).then_inc(out_act, 1)

    @block.vector
    def _(dve):
        own, done_units = [0], [0]

        def link(ins):
            own[0] += 1
            ins.then_inc(dve_own, 1)
            dve.wait_ge(dve_own, own[0])

        def lo_of(dst, src, hi):
            return dve.tensor_tensor(dst, src, hi.bitcast(F32), ALU.subtract)

        def split(i, per, u):
            r = u % RING
            dve.wait_ge(hi_ready, at(i, per, u + 1))
            lo_of(w_lo[:, r, :], w_raw[:, r, :], w_hi[:, r, :]).then_inc(lo_ready, 1)

        def split_to(u_end):
            while done_units[0] < min(u_end, n_units):
                split(None, 0, done_units[0])
                done_units[0] += 1

        def before_block(st, b):
            end = st.u0 + (b + 1) * len(st.ks)
            split_to(end + AHEAD)
            dve.wait_ge(unit_used, end)

        def end_loop(st):
            done_units[0] = st.u0 + st.n * len(st.ks) + AHEAD

        def follow(st):
            n = 2 * len(st.ks)
            with dve.Fori(0, st.n // 2) as i:
                for j in range(n):
                    split(i, n, st.u0 + AHEAD + j)
            end_loop(st)

        def rstd_of(n):
            dve.wait_ge(sd_ready, n)
            link(dve.reciprocal(rstd[:, :], sd))

        def normed(c, src, gain):
            for k in range(CT * c, CT * c + CT):
                ins = dve.scalar_tensor_tensor(work[:, k, :], src[:, k, :], gain(k), rstd[:, :],
                                               ALU.mult, ALU.mult)
            return ins

        def operand_lo(c, n, src):
            dve.wait_ge(h_hi_ready, NCH * (n - 1) + c + 1)
            lo_of(h_lo[:, chunk(c), :], src[:, chunk(c), :], h_hi[:, chunk(c), :]).then_inc(h_lo_ready, 1)

        def pre_norm(n, gain, shift=None):
            for c in range(NCH + 1):
                if c < NCH:
                    ins = normed(c, xT, gain)
                    if shift is not None:
                        link(ins)
                        for k in range(CT * c, CT * c + CT):
                            ins = dve.tensor_scalar(work[:, k, :], work[:, k, :], shift(k), None, ALU.add)
                    ins.then_inc(h_ready, 1)
                if c >= 1:
                    operand_lo(c - 1, n, work)

        def post_norm(gain):
            for c in range(NCH):
                link(normed(c, mT, gain))
                dve.tensor_tensor(xT[:, chunk(c), :], xT[:, chunk(c), :], work[:, chunk(c), :], ALU.add
                                  ).then_inc(x_ready, 1)

        def multiply_pairs(st, ff0, extra=None):
            with dve.Fori(0, st.n // 2) as i:
                for j in range(2):
                    split(i, 4, st.u0 + 2 + j)
                if extra:
                    extra(i)
                for j in range(2):
                    split(i, 4, st.u0 + 4 + j)
                dve.wait_ge(unit_used, at(i, 4, st.u0 + 4))
                dve.wait_ge(act_read, at(i, 1, st.act0 + 1))
                dve.tensor_tensor(ffv[:, :, :], silu_g[:, :, :], bank3[(st.b0 + 1) % 2], ALU.mult
                                  ).then_inc(dve_read, 1)
                dve.wait_ge(ff_hi_ready, at(i, 1, ff0 + 1))
                lo_of(ff_lo[:, bass.ds(at(i, 2, 0), 2), :], ffv[:, :, :],
                      ff_hi[:, bass.ds(at(i, 2, 0), 2), :]).then_inc(ff_lo_ready, 1)
            end_loop(st)

        for j in (2, 3):
            dve.wait_ge(x_T, j + 1)
            dve.tensor_copy(xT[:, chunk(j), :], bank3[2 + j]).then_inc(x_dve, 1)
        dve.wait_ge(bias_mm, 1)
        dve.tensor_copy(bias_row[:, 0:S], bank[1][0:H1, 0:S])
        dve.memset(bias_row[:, S:2 * S], NEG).then_inc(bias_ready, 1)
        dve.wait_ge(rows_T, 1)
        for t in range(3):
            ins = dve.tensor_copy(cols[:, t, 0:R_USED[t]], bank[6][:, t * P:t * P + R_USED[t]])
        link(ins)
        split_to(AHEAD)
        rstd_of(1)
        pre_norm(1, lambda k: col(0, C_MIX + k))
        before_block(s_kc, 0)
        for n, pos in ((0, POS_K), (1, POS_V)):
            for g in range(G1):
                tok = bank3[s_kc.b0 % 2][64 * g:64 * g + 64, n, :].rearrange("p (j t a) -> p t j a", t=8, a=2)
                for par in range(2):
                    rows64 = slice(64 * par, 64 * par + 64)
                    for c in range(2):
                        ins = dve.tensor_tensor(
                            tblk[rows64, n, 8 * c:8 * c + 8, g * NCMP:(g + 1) * NCMP],
                            tok[:, :, c:c + NCMP, par],
                            cols[rows64, 2, pos + 8 * c:pos + 8 * c + 8].unsqueeze(2).broadcast_to(
                                [64, 8, NCMP]), ALU.add)
        ins.then_inc(dve_read, 1)
        split_to(s_in.u0 + 6 + AHEAD)
        for h in range(H1):
            dve.wait_ge(toep_mm, h + 1)
            dve.tensor_copy(toep[:, h, :], bank[2 + h % 4][:, 0:TOEP]).then_inc(toep_ready, 1)
        split_to(s_in.u0 + 8 + AHEAD)
        dve.wait_ge(tblk_hi_ready, 1)
        lo_of(tblk_lo[:, :, :, :], tblk[:, :, :, :], tblk_hi[:, :, :, :]).then_inc(tblk_lo_ready, 1)
        split_to(s_in.u0 + 12 + AHEAD)
        dve.wait_ge(act_read, s_in.act0 + 6)
        for t in range(TT):
            ins = dve.bn_stats(ln_bn[:, t, :], gv[:, t, :])
        link(ins)
        for t in range(TT):
            ins = dve.bn_aggr(ln_st[:, t, 0:2], ln_bn[:, t, :])
        link(ins)
        dve.tensor_scalar(ln_st[:, :, 1:2], ln_st[:, :, 1:2], 1e-5, None, ALU.add).then_inc(ln_var, 1)
        split_to(s_cmp.u0 + 4)
        dve.wait_ge(ln_sd, 1)
        link(dve.reciprocal(ln_st[:, :, 3:4], ln_st[:, :, 2:3]))
        for t in range(TT):
            ins = dve.tensor_scalar(gv[:, t, :], gv[:, t, :], ln_st[:, t, 0:1], ln_st[:, t, 3:4],
                                    ALU.subtract, ALU.mult)
        link(ins)
        dve.wait_ge(gates_act, 1)
        gate_c = gates[:, 0, 0:24:3]
        dve.tensor_scalar(gate_c, gate_c, has_block, None, ALU.mult).then_inc(gates_ready, 1)
        split_to(s_cmp.u0 + 6)
        dve.wait_ge(ws_T, 1)
        for j in range(2):
            ins = dve.tensor_tensor(wsT[:, 4 * j:4 * j + 4, :],
                                    bank[2 + j][:, :].rearrange("p (g t) -> p g t", g=4),
                                    tri.unsqueeze(1).broadcast_to([P, 4, P]), ALU.mult)
        ins.then_inc(wsT_ready, 1)
        split_to(s_cmp.u0 + 8)
        dve.wait_ge(ln_in, 32)
        link(dve.tensor_tensor(gv[:, :, :], gv[:, :, :], ln_g[:, :].unsqueeze(1).broadcast_to([P, TT, GW]),
                               ALU.mult))
        split_to(s_u.u0 + 2)
        dve.tensor_tensor(gv[:, :, :], gv[:, :, :], ln_b[:, :].unsqueeze(1).broadcast_to([P, TT, GW]),
                          ALU.add).then_inc(zv_ready, 1)
        split_to(s_u.u0 + 4 + AHEAD)
        dve.wait_ge(zv_ready, 1)
        for n in range(len(TILES1) + 4):
            if n >= 7 and (n - 7) % 4 == 0:
                hp = (n - 7) // 4
                dve.wait_ge(pv_mm, 4 * hp + 4)
                dve.tensor_copy(mix[:, hp, :], bank3[7][:, hp % 2, :]).then_inc(att_ready, 1)
            if n < len(TILES1):
                h, qt = TILES1[n]
                nk, off = P * (qt + 1), P * (1 - qt)
                dve.wait_ge(lg_mm, n + 1)
                if n >= 4:
                    dve.wait_ge(pT_mm, n - 3)
                sw = probs[n % 4][:, NCP:NCP + 2 * S].rearrange("p (b k) -> p b k", b=2)[:, :, 0:nk]
                dve.tensor_tensor(sw, bank3[2 + n % 2][:, :, 0:nk],
                                  toep[:, h, off:off + nk].unsqueeze(1).broadcast_to([P, 2, nk]), ALU.add)
                first = off + CBLOCK - 1
                link(dve.tensor_tensor(probs[n % 4][:, 0:NCMP], bank[4 + n % 2][:, 0:NCMP],
                                       toep[:, h, first:first + CSTRIDE * (NCMP - 1) + 1:CSTRIDE], ALU.add))
                dve.tensor_reduce(st1[:, n % 4, 0, 1:3], sw, AX.X, ALU.max, negate=True)
                dve.tensor_reduce(st1[:, n % 4, 0, 0:1], probs[n % 4][:, 0:NCMP], AX.X, ALU.max,
                                  negate=True).then_inc(max_ready, 1)
            if 1 <= n <= len(TILES1):
                m = n - 1
                h, qt = TILES1[m]
                nk = P * (qt + 1)
                dve.wait_ge(exp_ready, m + 1)
                link(dve.reciprocal(st1[:, m % 4, 2, 0:3], st1[:, m % 4, 1, 0:3]))
                link(dve.tensor_tensor(st1[:, m % 4, 3, 0:3], st1[:, m % 4, 2, 0:3],
                                       gates[:, qt, 3 * h:3 * h + 3], ALU.mult))
                for br, (c0, cn) in enumerate(((0, NCMP), (NCP, nk), (NCP + S, nk))):
                    ins = dve.tensor_scalar(probs[m % 4][:, c0:c0 + cn], probs[m % 4][:, c0:c0 + cn],
                                            st1[:, m % 4, 3, br:br + 1], None, ALU.mult)
                ins.then_inc(pn_ready, 1)
            if n == 1:
                dve.wait_ge(sv_mm, 1)
                for i in range(4):
                    ins = dve.tensor_tensor(mix[:, 4 + i, :].rearrange("p (n t) -> p n t", n=2),
                                            bank[i // 2][:, (i % 2) * S:(i % 2 + 1) * S].rearrange(
                                                "p (n t) -> p n t", n=2),
                                            bs[:, i, :].unsqueeze(1).broadcast_to([P, 2, P]), ALU.add)
                link(ins)
                dve.tensor_tensor(mix[:, 4:8, :], mix[:, 4:8, :], zu[:, :, :], ALU.mult).then_inc(mix_gm, 1)
        for c in range(NCH):
            operand_lo(c, 2, mix)
        follow(s_wo)
        rstd_of(2)
        post_norm(lambda k: col(0, C_MIXP + k))
        rstd_of(3)
        pre_norm(3, lambda k: col(0, C_FFN + k))

        def modulate(i, per, c):
            acc = ada_acc[:, bass.ds(at(i, MCOL, MCOL * c), MCOL)]
            for k in range(KD):
                src = ada_raw[:, k // 2, (k % 2) * MCOL:(k % 2 + 1) * MCOL]
                if k % 2 == 0:
                    dve.wait_ge(ada_in[k // 2], at(i, 16, 16 * (c + 1)))
                if k == 0:
                    ins = dve.tensor_scalar(acc, src, c_silu[:, 0:1], None, ALU.mult)
                else:
                    dve.wait_ge(ada_used, at(i, 8, 8 * c + k))
                    ins = dve.scalar_tensor_tensor(acc, src, c_silu[:, k:k + 1], acc, ALU.mult, ALU.add)
                ins.then_inc(ada_used, 1)

        dve.wait_ge(c_ready, 1)
        modulate(None, 0, 0)
        multiply_pairs(s_gu, 0, extra=lambda i: modulate(i, 8, 1))
        for c in range(12, 6 * D // MCOL):
            split_to(s_dn.u0 + AHEAD + 2 * (c - 11))
            modulate(None, 0, c)
        split_to(s_dn.u0 + 12 + AHEAD)
        dve.wait_ge(mod_mm, 1)
        dve.tensor_copy(mod_rows[:, :], bank[6][0:48, 0:P]).then_inc(mod_copied, 1)
        split_to(s_dn.u0 + 22 + AHEAD)
        dve.wait_ge(ada_mm, 1)
        link(dve.tensor_tensor(mod[:, :], bank[5][:, 0:48], cols[:, 2, ADA_B:ADA_B + 48], ALU.add))
        for n, (m0, c0, plus) in enumerate(((8, C_MIX2, 1.0), (16, C_MIXP2, 0.0), (32, C_FFN2, 1.0),
                                            (40, C_FFNP2, 0.0))):
            ins = dve.scalar_tensor_tensor(gains[:, n, :], mod[:, m0:m0 + 8], plus, cols[:, 0, c0:c0 + 8],
                                           ALU.add, ALU.mult)
        ins.then_inc(mod_ready, 1)
        split_to(s_dn.u0 + 24 + AHEAD)
        rstd_of(4)
        post_norm(lambda k: col(0, C_FFNP + k))

        rstd_of(5)
        pre_norm(4, lambda k: gains[:, 0, k:k + 1], lambda k: mod[:, k:k + 1])
        dve.wait_ge(pos_in, 32)
        dve.tensor_copy(pos_f[:, :], pos_i[:, :])
        link(dve.tensor_scalar(last_i[:, :], pos_i[:, S:S + TT], -64, None, ALU.bitwise_and))
        link(dve.tensor_copy(last_f[:, :], last_i[:, :]))
        link(dve.tensor_scalar(last_f[:, :], last_f[:, :], 64.0, None, ALU.add))
        for t in range(TT):
            dve.tensor_scalar(shut[:, t, :], pos_f[:, 0:S], last_f[:, t:t + 1], NEG, ALU.is_ge, ALU.mult)
        for q in range(4):
            r32 = slice(32 * q, 32 * q + 32)
            dve.tensor_scalar(own_pos[r32, :], pos_f[r32, q:S:4], reach_from[r32, :], None, ALU.add)
        dve.wait_ge(step_mm, 1)
        link(dve.tensor_copy(tab_s[:, 0, :], bank[5][:, 0:H2]))
        link(dve.tensor_tensor(tab_r[:, :], bank[5][:, 0:H2], tab_s[:, 0, :], ALU.subtract))
        link(dve.tensor_copy(tab_s[:, 1, :], tab_r[:, :]))
        link(dve.tensor_tensor(tab_r[:, :], tab_r[:, :], tab_s[:, 1, :], ALU.subtract))
        dve.tensor_copy(tab_s[:, 2, :], tab_r[:, :])
        link(dve.memset(tab_b[:, :, :, :], 0.0))
        for q in range(QT):
            r32 = slice(32 * (q % 4), 32 * (q % 4) + 32)
            ins = dve.tensor_copy(tab_b[r32, q // 4, :, H2 * q:H2 * q + H2], tab_s[r32, :, :])
        ins.then_inc(tab_ready, 1)
        before_block(s_lat, 0)
        before_block(s_lat, 1)
        dve.wait_ge(lat_sq, 1)
        for n, count in enumerate((QR, CKV, 64)):
            ins = dve.tensor_scalar(st2[:, :, 3 + n:4 + n], st2[:, :, n:n + 1], 1.0 / count, 1e-6,
                                    ALU.mult, ALU.add)
        ins.then_inc(lat_var, 1)
        dve.wait_ge(lat_sd, 1)
        link(dve.reciprocal(st2[:, :, 9:12], st2[:, :, 6:9]))
        dve.wait_ge(lat_in, 16)
        b_q, b_k = bank3[s_lat.b0 % 2], bank3[(s_lat.b0 + 1) % 2]
        for t in range(TT):
            ins = dve.tensor_scalar(qn[:, t, :], b_q[:, t, :], st2[:, t, 9:10], None, ALU.mult)
        ins.then_inc(dve_read, 1)
        for t in range(TT):
            dve.scalar_tensor_tensor(kv[:, t, :], b_k[:, t, 0:CKV], st2[:, t, 10:11], kv_gain[:, :],
                                     ALU.mult, ALU.mult)
            dve.tensor_scalar(kin[:, t, :, :], b_k[:, t, CKV:CKV + 64].unsqueeze(1).broadcast_to([P, 2, 64]),
                              st2[:, t, 11:12], None, ALU.mult)
        dve.tensor_scalar(widx[:, :, :], b_k[:, :, 192:208], 16 ** -0.5 * 64 ** -0.5, None, ALU.mult
                          ).then_inc(dve_read, 1)
        dve.wait_ge(lat_T, 1)
        for k in range(2):
            ins = dve.tensor_scalar(rn[:, k, :], bank3[2][:, k, :], col(0, C_QN + k), None, ALU.mult)
        ins.then_inc(qn_ready, 1)
        dve.tensor_copy(kvT[:, :], bank[3][:, 0:S])
        dve.tensor_scalar(kiT[:, :], bank[3][:, S:2 * S], col(0, C_KI), None, ALU.mult).then_inc(ki_ready, 1)
        dve.wait_ge(qn_hi, 1)
        lo_of(ff_lo[:, 0:2, :], rn[:, :, :], ff_hi[:, 0:2, :]).then_inc(qn_lo, 1)
        dve.wait_ge(dt_mm, 1)
        dve.wait_ge(ssd_in, 80)
        link(dve.tensor_tensor(dt_sc[:, 0, :, :], bank[6][:, 0:2 * HS].rearrange("p (t h) -> p t h", t=TT),
                               dt_bias[:, :].unsqueeze(1).broadcast_to([P, TT, HS]), ALU.add))
        link(dve.scalar_tensor_tensor(dt_sc[:, 1, :, :], dt_sc[:, 0, :, :], -1.0, dt_sc[:, 0, :, :],
                                      ALU.mult, ALU.max))
        dve.tensor_scalar(dt_sc[:, 0, :, :], dt_sc[:, 0, :, :], 0.0, None, ALU.max).then_inc(dt_a, 1)
        split_to(s_uq.u0 + AHEAD)
        for r in range(8):
            qt, r4 = r // 4, r % 4
            dve.wait_ge(ix_relu, r + 1)
            for j in range(4):
                w = widx[:, qt, 4 * r4 + 2 * (j % 2) + j // 2:4 * r4 + 2 * (j % 2) + j // 2 + 1]
                if r4 == 0 and j == 0:
                    ins = dve.tensor_scalar(isc[:, qt, :], relu_s[:, r % 2, j, :], w, None, ALU.mult)
                else:
                    ins = dve.scalar_tensor_tensor(isc[:, qt, :], relu_s[:, r % 2, j, :], w, isc[:, qt, :],
                                                   ALU.mult, ALU.add)
                if j < 3:
                    link(ins)
            ins.then_inc(ix_sum, 1)
            dve.wait_ge(ix_sum, r + 1)
        link(dve.tensor_tensor(isc[:, :, :], isc[:, :, :], shut[:, :, :], ALU.add))
        for qt in range(TT):
            for r in range(TOPK // 8):
                link(dve.max(top8[:, :], isc[:, qt, :]))
                link(dve.match_replace(isc[:, qt, :], top8[:, :], isc[:, qt, :], NEG_TAKEN))
                split_to(s_uq.u0 + AHEAD + 8 * qt + r + 1)
        link(dve.tensor_scalar(isc[:, :, :], isc[:, :, :], -2.0e38, NEG, ALU.is_gt, ALU.mult))
        dve.tensor_tensor(mask[:, :, :], isc[:, :, :], shut[:, :, :], ALU.add).then_inc(mask_ready, 1)
        for n in range(NTILE + 4):
            if n < NTILE:
                dve.wait_ge(lt_mm, n + 1)
                if n >= 4:
                    dve.wait_ge(lt_exp, n - 3)
                dve.tensor_reduce(st3[:, n % 4, 0:1], bank[2 + n % 2][:, 0:S], AX.X, ALU.max, negate=True
                                  ).then_inc(lt_max, 1)
            if 1 <= n <= NTILE:
                m = n - 1
                dve.wait_ge(lt_exp, m + 1)
                link(dve.reciprocal(st3[:, m % 4, 2:3], st3[:, m % 4, 1:2]))
                dve.tensor_scalar(p2buf[m % 4], p2buf[m % 4], st3[:, m % 4, 2:3], None, ALU.mult
                                  ).then_inc(lt_p, 1)
            if n >= 4:
                m = n - 4
                dve.wait_ge(lt_pv, m + 1)
                dve.tensor_copy(oT[:, :, QT * m:QT * m + QT],
                                bank[6 + m % 2][:, 0:P].rearrange("p (q h) -> p h q", q=QT)
                                ).then_inc(lt_o, 1)
            if n % 4 == 0 and n < NTILE:
                split_to(s_z2.u0 + n // 4 + 1 + AHEAD)
        for b in range(4):
            dve.wait_ge(uv_hi, b + 1)
            lo_of(ff_lo[:, 8 + 2 * b:10 + 2 * b, :], bank3[2 + b], ff_hi[:, 8 + 2 * b:10 + 2 * b, :]
                  ).then_inc(uv_lo, 1)
        follow(s_ga)
        for b in range(s_oa.n):
            before_block(s_oa, b)
            if b == 0:
                dve.wait_ge(act_read, s_ga.act0 + s_ga.n)
            dve.tensor_tensor(mT[:, 2 * b:2 * b + 2, :], bank3[(s_oa.b0 + b) % 2], mT[:, 2 * b:2 * b + 2, :],
                              ALU.mult).then_inc(dve_read, 1)
        for b in range(s_xbc.n):
            before_block(s_xbc, b)
            src = bank3[(s_xbc.b0 + b) % 2]
            dst = xbc_tiles(b)
            dve.wait_ge(tap_ready, b + 1)
            for w in range(CONV - 2, -1, -1):
                if w < CONV - 2:
                    link(ins)
                back = CONV - 1 - w
                for s in range(2):
                    ins = dve.scalar_tensor_tensor(dst[:, s, back:S], src[:, s, 0:S - back],
                                                   col(1, w * KX + 2 * b + s), dst[:, s, back:S],
                                                   ALU.mult, ALU.add)
            ins.then_inc(dve_read, 1)
        dve.wait_ge(dt_b, 1)
        link(dve.tensor_tensor(dtd[:, 0, :, :], dt_sc[:, 0, :, :], dt_sc[:, 1, :, :], ALU.add))
        dve.scalar_tensor_tensor(dtd[:, 1, :, :], dtd[:, 0, :, :], -1.0,
                                 a_row[:, :].unsqueeze(1).broadcast_to([P, TT, HS]), ALU.mult, ALU.mult
                                 ).then_inc(dt_ready, 1)
        for n in range(8):
            t, q = n // 4, n % 4
            dve.wait_ge(xs_T, n + 1)
            dve.tensor_tensor(x_dt[:, t, 512 * q:512 * q + 512].rearrange("p (h d) -> p h d", h=8),
                              bank[4 + n % 2][:, :].rearrange("p (h d) -> p h d", h=8),
                              dtd[:, 0, t, 8 * q:8 * q + 8].unsqueeze(2).broadcast_to([P, 8, 64]), ALU.mult
                              ).then_inc(xs_ready, 1)
        dve.wait_ge(sz_ready, 1)
        for h in range(HS + 2):
            if h < HS:
                g = h // 4
                if h % 4 == 0:
                    dve.wait_ge(cb_mm, g + 1)
                    dve.tensor_tensor(cbm, bank[6][:, 0:384], tri_ones_tri, ALU.mult
                                      ).then_inc(cb_ready, 1)
                    dve.wait_ge(cb_ready, g + 1)
                dve.wait_ge(dec_ready, h + 1)
                if h >= 2:
                    dve.wait_ge(y_mm, h - 1)
                dve.tensor_tensor(m_buf[:, h % 2, :], decay[:, h % 2, :], cbm, ALU.mult
                                  ).then_inc(m_mat, 1)
            if h >= 3 and h % 2 == 1:
                i = (h - 3) // 2
                dve.wait_ge(y_mm, 2 * i + 2)
                link(dve.scalar_tensor_tensor(xsT[:, i, :], xsT[:, i, :], skip[:, i:i + 1],
                                              bank[4 + i % 2][:, 0:S], ALU.mult, ALU.add))
                dve.tensor_tensor(szT[:, i, :], szT[:, i, :], xsT[:, i, :], ALU.mult).then_inc(y_ready, 1)
        dve.wait_ge(sq_ready, SQ0[6] + KI // CT)
        for k in range(KI):
            ins = dve.tensor_scalar(szT[:, k, :], szT[:, k, :], col(0, C_SSD + k), None, ALU.mult)
        ins.then_inc(y_gain, 1)
        rstd_of(6)
        dve.wait_ge(y_hi, 1)
        lo_of(ff_lo[:, 0:KI, :], szT[:, :, :], ff_hi[:, 0:KI, :]).then_inc(y_lo, 1)
        follow(s_gb)
        for b in range(s_os.n):
            before_block(s_os, b)
            if b == 0:
                dve.wait_ge(act_read, s_gb.act0 + s_gb.n)
            part = work[:, 2 * b:2 * b + 2, :]
            dve.tensor_tensor(part, bank3[(s_os.b0 + b) % 2], part, ALU.mult).then_inc(dve_read, 1)
            dve.wait_ge(dve_read, s_os.dve0 + b + 1)
            link(dve.tensor_tensor(part, part, rstd[:, :].unsqueeze(1).broadcast_to([P, 2, S]), ALU.mult))
            dve.tensor_tensor(mT[:, 2 * b:2 * b + 2, :], mT[:, 2 * b:2 * b + 2, :], part, ALU.add
                              ).then_inc(mix2_ready, 1)
        for c in range(NCH):
            operand_lo(c, 5, mT)
        follow(s_wo2)
        rstd_of(7)
        post_norm(lambda k: gains[:, 1, k:k + 1])
        rstd_of(8)
        pre_norm(6, lambda k: gains[:, 2, k:k + 1], lambda k: mod[:, 24 + k:25 + k])
        multiply_pairs(s_gu2, 11)
        split_to(n_units)
        rstd_of(9)
        post_norm(lambda k: gains[:, 3, k:k + 1])
        dve.wait_ge(out_T, 2)
        for t in range(TT):
            dve.tensor_copy(out_tok[:, t, 512:1024], bank[3 + 2 * t][:, :]).then_inc(out_ready, 1)

    @block.tensor
    def _(pe):
        def free_bank(st, n, i=None):
            b = st.b0 + n
            if i is None and n >= 2 or i is not None:
                for s, e0 in ((act_read, st.act0), (dve_read, st.dve0)):
                    if (st.reader == "act") == (s is act_read) and st.reader != "pair":
                        pe.wait_ge(s, at(i, 2, e0 + n - 1))
                if st.reader == "pair":
                    if n % 2 == 0:
                        pe.wait_ge(act_read, at(i, 1, st.act0 + n // 2))
                    else:
                        pe.wait_ge(dve_read, at(i, 1, st.dve0 + n // 2))

        def enter(st):
            if st.act0:
                pe.wait_ge(act_read, st.act0)
            if st.dve0:
                pe.wait_ge(dve_read, st.dve0)

        def fm_block(st, n, x_hi, x_lo, i=None, turn=2, k0=0, lo0=None):
            for k in range(sum(st.ks)):
                fm_tile(st, n, k, x_hi, x_lo, i, turn, k0, lo0)

        def fm_tile(st, n, k, x_hi, x_lo, i=None, turn=2, k0=0, lo0=None):
            if k == 0:
                free_bank(st, n, i)
            out_b = bank3[(st.b0 + n) % 2]
            j = k // st.ks[0]
            kk, nk, u = k - j * st.ks[0], st.ks[j], st.u0 + n * len(st.ks) + j
            if kk == 0:
                pe.wait_ge(lo_ready, at(i, turn * len(st.ks), u + 1))
            if lo0 is not None and k % CT == 0:
                pe.wait_ge(h_lo_ready, lo0 + k // CT + 1)
            hi = w_hi[:, u % RING, 0:nk * 256].rearrange("p (k c) -> p k c", k=nk)
            lo = w_lo[:, u % RING, 0:nk * 256].rearrange("p (k c) -> p k c", k=nk)
            for s in range(2):
                c = slice(s * P, s * P + P)
                for w, x, step in ((hi, x_hi, 0), (hi, x_lo, 1), (lo, x_hi, 2)):
                    ins = pe.matmul(out_b[:, s, :], w[:, kk, c], x[:, k0 + k, :],
                                    start=k == 0 and s == 0 and step == 0,
                                    stop=k == sum(st.ks) - 1 and s == 1 and step == 2,
                                    skip_group_check=True)
            if kk == nk - 1:
                ins.then_inc(unit_used, 1)

        def tm_block(st, n, x_hi, x_lo, ncol=256):
            free_bank(st, n)
            out_b = bank3[(st.b0 + n) % 2]
            u, k, first = st.u0 + n * len(st.ks), 0, True
            for nk in st.ks:
                pe.wait_ge(lo_ready, u + 1)
                hi = w_hi[:, u % RING, 0:nk * ncol].rearrange("p (k c) -> p k c", k=nk)
                lo = w_lo[:, u % RING, 0:nk * ncol].rearrange("p (k c) -> p k c", k=nk)
                for kk in range(nk):
                    end = kk == nk - 1 and u == st.u0 + (n + 1) * len(st.ks) - 1
                    for t in range(TT):
                        c = slice(t * P, t * P + P)
                        for w, x, last in ((hi, x_hi, False), (hi, x_lo, False), (lo, x_hi, True)):
                            ins = pe.matmul(out_b[:, t, 0:ncol], x[:, k, c], w[:, kk, :], start=first,
                                            stop=end and last and t == 1, skip_group_check=True)
                            first = False
                    k += 1
                ins.then_inc(unit_used, 1)
                u += 1

        def kv_block(st, n):
            free_bank(st, n)
            out_b = bank3[(st.b0 + n) % 2]
            first = True
            for j in range(2):
                u = st.u0 + 2 * n + j
                pe.wait_ge(lo_ready, u + 1)
                hi = w_hi[:, u % RING, :].rearrange("p (k c) -> p k c", k=4)
                lo = w_lo[:, u % RING, :].rearrange("p (k c) -> p k c", k=4)
                for kk in range(4):
                    k = 4 * j + kk
                    for w, x in ((hi, h_hi), (hi, h_lo), (lo, h_hi)):
                        pe.matmul(out_b[:, 0, :], w[:, kk, 0:P], x[:, k, :], start=first, stop=False,
                                  skip_group_check=True)
                        first = False
                    for t in range(TT):
                        c = slice(t * P, t * P + P)
                        for w, x, last in ((hi, h_hi, False), (hi, h_lo, False), (lo, h_hi, True)):
                            ins = pe.matmul(out_b[:, 1, c], x[:, k, c], w[:, kk, P:2 * P], start=False,
                                            stop=k == KD - 1 and t == 1 and last, skip_group_check=True)
                ins.then_inc(unit_used, 1)

        def fm_stream(st, x_hi, x_lo, k0=0, lo0=None):
            enter(st)
            if lo0 is not None:
                fm_block(st, 0, x_hi, x_lo, lo0=lo0)
                fm_block(st, 1, x_hi, x_lo)
            with pe.Fori(0 if lo0 is None else 1, st.n // 2) as i:
                for n in range(2):
                    fm_block(st, n, x_hi, x_lo, i, 2, k0)

        def sum_squares(n, sq, tiles=KD):
            for k in range(tiles):
                if k % CT == 0:
                    pe.wait_ge(sq_ready, SQ0[n] + k // CT + 1)
                ins = pe.matmul(bank[7][:, 0:S], ones, sq[:, k, :], start=k == 0, stop=k == tiles - 1)
            ins.then_inc(ss_ready, 1)

        pe.wait_ge(consts_in, 16)
        pe.wait_ge(x_in, 16 * TT)
        for j in range(4):
            for k in (0, 1):
                for t in range(TT):
                    ins = pe.transpose(bank[2 + j][:, k * S + t * P:k * S + (t + 1) * P],
                                       x_tok[:, t, (2 * j + k) * P:(2 * j + k + 1) * P], ident)
            ins.then_inc(x_T, 1)
        pe.wait_ge(rows_in, 16 * n_rows_dma)
        for t in range(3):
            ins = pe.transpose(bank[6][:, t * P:t * P + R_USED[t]], rows[0:R_USED[t], t, :],
                               ident[0:R_USED[t], 0:R_USED[t]])
        ins.then_inc(rows_T, 1)
        sum_squares(1, work)
        pe.wait_ge(hot_in, 32)
        pe.matmul(bank[1][0:H1, :], table1[:, :], hot[:, :], start=True, stop=True).then_inc(bias_mm, 1)
        fm_block(s_kc, 0, h_hi, h_lo, lo0=0)
        pe.wait_ge(bias_ready, 1)
        kv_block(s_in, 0)
        pe.wait_ge(dve_read, 1)
        fm_block(s_in, 1, h_hi, h_lo)
        fm_block(s_in, 2, h_hi, h_lo)
        pe.wait_ge(toep_in, 32)
        for h in range(H1):
            if h >= 4:
                pe.wait_ge(toep_ready, h - 3)
            pe.matmul(bank[2 + h % 4][:, 0:TOEP], flip, hankel_a[:, h, :] if h < 5 else hankel_b[:, h - 5, :],
                      start=True, stop=True).then_inc(toep_mm, 1)
        kv_block(s_in, 3)
        pe.wait_ge(gates_in, 16)
        for t in range(TT):
            for k in range(KD):
                ins = pe.matmul(bank[7][:, 24 * t:24 * t + 24], work[:, k, t * P:(t + 1) * P],
                                w_gates[:, k, :], start=k == 0, stop=k == KD - 1)
        ins.then_inc(gate_mm, 1)
        tm_block(s_in, 4, h_hi, h_lo)
        tm_block(s_in, 5, h_hi, h_lo)
        pe.wait_ge(gmlp_in, 48)
        pe.wait_ge(toep_ready, H1)
        for g in range(8):
            ins = pe.transpose(bank[2 + g // 4][:, (g % 4) * P:(g % 4 + 1) * P], ws[:, g, :], ident)
        ins.then_inc(ws_T, 1)
        enter(s_cmp)
        pe.wait_ge(tblk_lo_ready, 1)
        for n in range(2):
            out_b = bank[(s_cmp.b0 + n) % 2][0:2 * NCMP, 0:256]
            for k in range(16):
                u, kk = s_cmp.u0 + 4 * n + k // 4, k % 4
                if kk == 0:
                    pe.wait_ge(lo_ready, u + 1)
                hi = w_hi[:, u % RING, :].rearrange("p (k c) -> p k c", k=4)
                lo = w_lo[:, u % RING, :].rearrange("p (k c) -> p k c", k=4)
                for w, x, step in ((hi, tblk_hi, 0), (hi, tblk_lo, 1), (lo, tblk_hi, 2)):
                    ins = pe.matmul(out_b, x[:, n, k, :], w[:, kk, :], start=k == 0 and step == 0,
                                    stop=k == 15 and step == 2)
                if kk == 3:
                    ins.then_inc(unit_used, 1)
        enter(s_u)
        fm_block(s_u, 0, h_hi, h_lo)
        for n in range(2):
            for m in range(2):
                ins = pe.transpose(bank[4][:, (2 * n + m) * 2 * NCMP:(2 * n + m + 1) * 2 * NCMP],
                                   hid_tok[:, n, m * P:(m + 1) * P], ident[0:2 * NCMP, 0:2 * NCMP])
        ins.then_inc(hid_T, 1)
        fm_block(s_u, 1, h_hi, h_lo)
        pe.wait_ge(hid_ready, 1)
        pe.wait_ge(mlp_in, 32)
        for half in range(2):
            for m in range(2):
                pe.matmul(bank[6][64 * half:64 * half + 64, 0:2 * NCMP], w2[:, 0, m, :], hid[:, 0, m, :],
                          start=m == 0, stop=m == 1)
        for g in range(G1):
            for m in range(2):
                ins = pe.matmul(bank[6][0:NCMP, P + 64 * g:P + 64 * g + 64],
                                hid[:, 1, m, g * NCMP:(g + 1) * NCMP], w2[:, 1, m, :],
                                start=m == 0, stop=m == 1)
        ins.then_inc(kcvc_mm, 1)
        pe.wait_ge(kcvc_ready, 1)
        pe.wait_ge(gates_ready, 1)
        for n in range(len(TILES1) + 3):
            if n < len(TILES1):
                h, qt = TILES1[n]
                half, g, nk = h % 2, h // 4, P * (qt + 1)
                r64 = slice(64 * half, 64 * half + 64)
                q = qT[r64, h // 2, qt * P:(qt + 1) * P]
                if n >= 2:
                    pe.wait_ge(max_ready, n - 1)
                for br in range(2):
                    pe.matmul(bank3[2 + n % 2][:, br, 0:nk], q, kdup[r64, g, br, 0:nk], start=True, stop=True)
                pe.matmul(bank[4 + n % 2][:, 0:NCMP], q, kc_dup[r64, g * NCMP:(g + 1) * NCMP],
                          start=True, stop=True).then_inc(lg_mm, 1)
            if n == 1:
                pe.wait_ge(wsT_ready, 1)
                pe.wait_ge(zv_ready, 1)
                pe.wait_ge(act_read, s_u.act0 + s_u.n)
                for g in range(8):
                    for t in range(TT):
                        c0 = (g // 2 % 2) * S + t * P
                        ins = pe.matmul(bank[g // 4][64 * (g % 2):64 * (g % 2) + 64, c0:c0 + P],
                                        gv[:, t, 64 * g:64 * g + 64], wsT[:, g, :], start=True, stop=True)
                ins.then_inc(sv_mm, 1)
            if 2 <= n <= len(TILES1) + 1:
                m = n - 2
                h, qt = TILES1[m]
                pe.wait_ge(pn_ready, m + 1)
                if m == 0:
                    pe.wait_ge(mix_gm, 1)
                else:
                    pe.wait_ge(pT_ready, m)
                for br in range(2):
                    for kt in range(qt + 1):
                        c0 = (br * (qt + 1) + kt) * P
                        k0 = NCP + br * S + kt * P
                        pe.transpose(bank[m % 2][:, c0:c0 + P], probs[m % 4][:, k0:k0 + P], ident)
                pe.transpose(bank[6][0:NCMP, 0:P], probs[m % 4][:, 0:NCMP], ident).then_inc(pT_mm, 1)
            if n >= 3:
                m = n - 3
                h, qt = TILES1[m]
                half, g, hp = h % 2, h // 4, m // 4
                pe.wait_ge(pT_ready, m + 1)
                if m % 4 == 0 and hp >= 1:
                    pe.wait_ge(att_ready, hp)
                o = bank[7][64 * half:64 * half + 64, (hp % 2) * S + qt * P:(hp % 2) * S + (qt + 1) * P]
                pe.matmul(o, vc[:, g, :], pT[0:NCMP, m % 2, 0, :], start=True, stop=False)
                for br in range(2):
                    for kt in range(qt + 1):
                        ins = pe.matmul(o, v_tok[:, kt, br * KV1 + 64 * g:br * KV1 + 64 * g + 64],
                                        pT[:, m % 2, 1 + br * (qt + 1) + kt, :], start=False,
                                        stop=br == 1 and kt == qt)
                ins.then_inc(pv_mm, 1)
        fm_stream(s_wo, h_hi, h_lo, lo0=NCH)
        sum_squares(2, work)
        sum_squares(3, work)
        fm_stream(s_gu, h_hi, h_lo, lo0=2 * NCH)
        pe.wait_ge(ff_lo_ready, 11)
        enter(s_dn)
        for n in range(s_dn.n):
            fm_block(s_dn, n, ff_hi, ff_lo)
            if n == 1:
                pe.wait_ge(row_ready, 1)
                pe.wait_ge(ada_used, 8 * (6 * D // MCOL))
                for c in range(48):
                    ins = pe.matmul(bank[6][0:48, 0:P], row_of[:, 47 - c:95 - c], ada_acc[:, c * P:(c + 1) * P],
                                    start=c == 0, stop=c == 47)
                ins.then_inc(mod_mm, 1)
            if n == 2:
                pe.wait_ge(mod_copied, 1)
                pe.transpose(bank[5][:, 0:48], mod_rows[:, :], ident[0:48, 0:48]).then_inc(ada_mm, 1)
        sum_squares(4, work)

        sum_squares(5, work)
        pe.wait_ge(tab_in, 32)
        pe.matmul(bank[5][:, 0:H2], steps[:, :], tab2[:, :], start=True, stop=True).then_inc(step_mm, 1)
        pe.wait_ge(h_lo_ready, 4 * NCH)
        enter(s_lat)
        tm_block(s_lat, 0, h_hi, h_lo)
        tm_block(s_lat, 1, h_hi, h_lo, ncol=208)
        pe.wait_ge(ssd_in, 80)
        for t in range(TT):
            for k in range(KD):
                ins = pe.matmul(bank[6][:, HS * t:HS * t + HS], work[:, k, t * P:(t + 1) * P],
                                w_dt[:, k, :], start=k == 0, stop=k == KD - 1)
        ins.then_inc(dt_mm, 1)
        pe.wait_ge(dve_read, s_lat.dve0 + 2)
        for t in range(TT):
            for k in range(2):
                pe.transpose(bank[2][:, k * S + t * P:k * S + (t + 1) * P], qn[:, t, k * P:(k + 1) * P], ident)
            pe.transpose(bank[3][:, t * P:(t + 1) * P], kv[:, t, :], ident)
            ins = pe.transpose(bank[3][:, S + t * P:S + (t + 1) * P],
                               kin[:, t, :, :].rearrange("p a d -> p (a d)"), ident)
        ins.then_inc(lat_T, 1)
        pe.wait_ge(qn_lo, 1)
        enter(s_qi)
        for b in range(s_qi.n):
            fm_block(s_qi, b, ff_hi, ff_lo)
        pe.wait_ge(ki_ready, 1)
        pe.wait_ge(act_read, s_qi.act0 + s_qi.n)
        for r in range(8):
            qt, r4 = r // 4, r % 4
            if r >= 2:
                pe.wait_ge(ix_relu, r - 1)
            for j in range(4):
                half, h = j // 2, 4 * r4 + 2 * (j % 2) + j // 2
                r64 = slice(64 * half, 64 * half + 64)
                ins = pe.matmul(bank3[2 + 2 * (r % 2) + half][:, j % 2, :],
                                qi[r64, h // 2, qt * P:(qt + 1) * P], kiT[r64, :], start=True, stop=True)
            ins.then_inc(ix_mm, 1)
        enter(s_uq)
        for b in range(s_uq.n):
            fm_block(s_uq, b, ff_hi, ff_lo)
        fm_stream(s_z, h_hi, h_lo)
        pe.wait_ge(mask_ready, 1)
        pe.wait_ge(pick_ready, 1)
        pe.wait_ge(tab_ready, 1)
        enter(s_z2)
        for n in range(NTILE + 3):
            if n < NTILE:
                lg = bank[2 + n % 2][:, 0:S]
                pe.wait_ge(reach_ready, n + 1)
                if n >= 2:
                    pe.wait_ge(lt_exp, n - 1)
                pe.matmul(lg, uq[:, QT * n:QT * n + QT, :].rearrange("p q h -> p (q h)"), kvT[:, :],
                          start=True, stop=False)
                for c in range(2):
                    for part in range(3):
                        pe.matmul(lg, tab_b[:, c, part, :], reached[:, n % 2, c, :], start=False, stop=False)
                pe.matmul(lg, pick[:, (n % 16) * P:(n % 16 + 1) * P], mask[:, n // 16, :],
                          start=False, stop=True).then_inc(lt_mm, 1)
            if 2 <= n <= NTILE + 1:
                m = n - 2
                pe.wait_ge(lt_p, m + 1)
                if m >= 2:
                    pe.wait_ge(lt_pT, m - 1)
                for k in range(2):
                    ins = pe.transpose(bank[4 + m % 2][:, k * P:(k + 1) * P],
                                       p2buf[m % 4][:, k * P:(k + 1) * P], ident)
                ins.then_inc(lt_T, 1)
            if n < NTILE:
                fm_tile(s_z2, n // KD, n % KD, h_hi, h_lo)
            if n >= 3:
                m = n - 3
                pe.wait_ge(lt_pT, m + 1)
                if m >= 2:
                    pe.wait_ge(lt_o, m - 1)
                for k in range(2):
                    ins = pe.matmul(bank[6 + m % 2][:, 0:P], kv[:, k, :], p2T[:, m % 2, k, :],
                                    start=k == 0, stop=k == 1)
                ins.then_inc(lt_pv, 1)
        pe.wait_ge(uv_in, 16)
        pe.wait_ge(lt_o, NTILE)
        for h in range(H2):
            half = h % 2
            ins = pe.matmul(bank3[2 + h // 4][64 * half:64 * half + 64, h // 2 % 2, :], w_uv[:, h, :],
                            oT[:, h, :], start=True, stop=True)
            if h % 4 == 3:
                ins.then_inc(uv_mm, 1)
        fm_stream(s_ga, h_hi, h_lo)
        pe.wait_ge(uv_lo, 4)
        enter(s_oa)
        fm_stream(s_oa, ff_hi, ff_lo, k0=8)
        fm_stream(s_xbc, h_hi, h_lo)
        pe.wait_ge(act_read, s_ga.act0 + s_ga.n)
        pe.wait_ge(xbc_ready, 8)
        for n in range(8):
            t, q = n // 4, n % 4
            if n >= 2:
                pe.wait_ge(xs_ready, n - 1)
            for j in range(4):
                ins = pe.transpose(bank[4 + n % 2][:, j * P:(j + 1) * P],
                                   xsT[:, 4 * q + j, t * P:(t + 1) * P], ident)
            ins.then_inc(xs_T, 1)
        pe.wait_ge(xbc_ready, s_xbc.n)
        pe.wait_ge(xs_ready, 8)
        for h in range(HS + 1):
            if h < HS:
                g = h // 4
                if h % 4 == 0:
                    if g >= 1:
                        pe.wait_ge(cb_ready, g)
                    pe.matmul(bank[6][:, 0:S], bT[:, g, 0:P], cT[:, g, :], start=True, stop=True)
                    pe.matmul(bank[6][:, S:S + P], bT[:, g, P:S], cT[:, g, P:S], start=True, stop=True
                              ).then_inc(cb_mm, 1)
                pe.wait_ge(ud_ready, h + 1)
                if h >= 2:
                    pe.wait_ge(dec_ready, h - 1)
                sg = bank[2 + h % 2]
                pe.matmul(sg[:, 0:S], ud[:, h % 2, 0, :], tri_ones, start=True, stop=False,
                          skip_group_check=True)
                pe.matmul(sg[:, P:S], dtd[:, 1, 1, h:h + 1].broadcast_to([P, P]), tri, start=False,
                          stop=False, skip_group_check=True)
                pe.matmul(sg[:, S:S + P], ud[:, h % 2, 1, :], tri, start=False, stop=True,
                          skip_group_check=True).then_inc(seg_mm, 1)
            if h >= 1:
                m = h - 1
                i, half = m // 2, m % 2
                pe.wait_ge(m_mat, m + 1)
                if half == 0 and i >= 2:
                    pe.wait_ge(y_ready, i - 1)
                r64 = slice(64 * half, 64 * half + 64)
                pe.matmul(bank[4 + i % 2][r64, 0:S], x_dt[:, 0, 64 * m:64 * m + 64], m_buf[:, m % 2, 0:S],
                          start=True, stop=False)
                pe.matmul(bank[4 + i % 2][r64, P:S], x_dt[:, 1, 64 * m:64 * m + 64],
                          m_buf[:, m % 2, S:S + P], start=False, stop=True).then_inc(y_mm, 1)
        sum_squares(6, xsT, KI)
        fm_stream(s_gb, h_hi, h_lo)
        pe.wait_ge(y_lo, 1)
        enter(s_os)
        fm_stream(s_os, ff_hi, ff_lo)
        fm_stream(s_wo2, h_hi, h_lo, lo0=4 * NCH)
        sum_squares(7, work)
        sum_squares(8, work)
        fm_stream(s_gu2, h_hi, h_lo, lo0=5 * NCH)
        pe.wait_ge(ff_lo_ready, 22)
        fm_stream(s_dn2, ff_hi, ff_lo)
        sum_squares(9, work)
        for k in range(KD):
            if k % CT == 0:
                pe.wait_ge(x_ready, 3 * NCH + k // CT + 1)
            for t in range(TT):
                ins = pe.transpose(bank[2 + 2 * t + k // 4][:, (k % 4) * P:(k % 4 + 1) * P],
                                   xT[:, k, t * P:(t + 1) * P], ident)
            if k % 4 == 3:
                ins.then_inc(out_T, 1)


def kernel(**inputs):
    import concourse.bacc as bacc
    from concourse.bass_utils import run_bass_kernel_spmd

    nc = bacc.Bacc("TRN2", target_bir_lowering=False, num_devices=1)
    mats, hot = shape_constants()
    arrays = {name: np.ascontiguousarray(x) for name, x in inputs.items()}
    arrays["shape_mats"], arrays["shape_hot"] = mats, hot
    a = {name: nc.dram_tensor(f"in_{name}", x.shape, mybir.dt.from_np(x.dtype),
                              kind="ExternalInput").ap() for name, x in arrays.items()}
    out = nc.dram_tensor("out", (1, S, D), F32, kind="ExternalOutput").ap()
    two_block_kernel(nc, a, out)
    r = run_bass_kernel_spmd(nc, [{f"in_{name}": x for name, x in arrays.items()}], core_ids=[0])
    return r.results[0]["out"]
```

```python
from contextlib import ExitStack

import numpy as np

import concourse.bass as bass
from concourse import mybir

F32 = mybir.dt.float32
F32R = mybir.dt.float32r
BF16 = mybir.dt.bfloat16
I32 = mybir.dt.int32
ALU = mybir.AluOpType
ACT = mybir.ActivationFunctionType
AX = mybir.AxisListType

P = 128
S = 256
TT = S // P
D = 1024
KD = D // P
MCOL = 384
CT = 2
NCH = KD // CT
RMS_EPS = 1.0e-6
NEG = -1.0e30
NEG_TAKEN = -3.0e38
H1, G1, DH = 8, 2, 64
KV1 = G1 * DH
NCMP, CSTRIDE, CBLOCK = 15, 16, 32
NCP = 16
FF = 2816
KF = FF // P
GW = 512
T5_FIRST = (0, 1, 2, 3, 4, 5, 6, 7, 8, 9, 10, 11, 12, 13, 14, 15, 16, 19, 21, 24, 27, 31, 35, 40,
            46, 52, 59, 67, 77, 87, 99, 113)
TOEP = 384
H2, CKV = 16, 128
QR = 256
TOPK = 64
T5B_FIRST = (0, 1, 2, 3, 4, 5, 6, 7, 8, 12, 16, 23, 32, 46, 64, 91)
QT = 8
NTILE = S // QT
DI = 2048
KI = DI // P
HS, NG, DS = 32, 8, 128
KX = 4096 // P
CONV = 4
RING = 4
UNIT = 1024
AHEAD = 2


def shape_constants():
    r = np.arange(P)
    ident = np.eye(P, dtype=np.float32)
    tri = (r[:, None] <= r[None, :]).astype(np.float32)
    upper = (r[:, None] > r[None, :]).astype(np.float32)
    ones = np.ones((P, P), np.float32)
    first, steps = np.zeros(32), np.zeros((32, 32), np.float32)
    for n in range(16):
        first[n] = -(T5B_FIRST[n + 1] - 1) if n < 15 else -1.0e9
        first[16 + n] = T5B_FIRST[n]
        steps[n, n] = steps[16 + n, 16 + n] = 1.0
        if n < 15:
            steps[n + 1, n] = -1.0
        if n:
            steps[15 + n if n > 1 else 0, 16 + n] = -1.0
    first[16], steps[:, 16] = 2.0e9, 0.0
    steps = np.tile(steps, (4, 4))
    cols = np.zeros((P, 4), np.float32)
    cols[:, 0] = np.tile(first, 4)
    cols[:, 2] = r >= CBLOCK - 1
    cols[:, 3] = RMS_EPS
    own_query = np.concatenate([r[:, None] // 32 + 4 * c == np.arange(QT)[None, :] for c in range(2)], axis=1)
    mats = np.concatenate([ident, upper, tri, ones, tri, ident[::-1], cols, own_query, steps], axis=1)
    hot = np.zeros((32, 2 * S), np.float32)
    for c in range(S):
        hot[max(b for b in range(32) if T5_FIRST[b] <= S - 1 - c), c] = 1.0
    return np.ascontiguousarray(mats, np.float32), hot


def at(i, per, const):
    return const if i is None else i * per + const


def two_block_kernel(nc, a, out):
    ctx = ExitStack()
    with ctx:
        _emit(nc, ctx, a, out)


def _emit(nc, ctx, a, out):
    def sem(name):
        return ctx.enter_context(nc.semaphore(name))

    def sb(name, shape, dt=F32, where=ctx):
        return where.enter_context(nc.sbuf_tensor(name, shape, dt))

    bank = [ctx.enter_context(nc.psum_tensor(f"bank{i}", [P, 512], F32)) for i in range(8)]
    bank3 = [b[:, :].rearrange("p (a n) -> p a n", a=2) for b in bank]

    w_raw = sb("w_raw", [P, RING, UNIT])
    w_hi = sb("w_hi", [P, RING, UNIT], F32R)
    w_lo = sb("w_lo", [P, RING, UNIT], F32R)
    h_hi = sb("h_hi", [P, KD, S], F32R)
    h_lo = sb("h_lo", [P, KD, S], F32R)
    ff_hi = sb("ff_hi", [P, KF, S], F32R)
    ff_lo = sb("ff_lo", [P, KF, S], F32R)
    xT = sb("xT", [P, KD, S])
    work = sb("work", [P, KD, S])
    mT = sb("mT", [P, KD, S])
    mats = sb("mats", [P, 6 * P + 4 + 2 * QT])
    ident, upper, tri, ones = (mats[:, i * P:(i + 1) * P] for i in range(4))
    tri_ones, tri_ones_tri, flip = mats[:, 2 * P:4 * P], mats[:, 2 * P:5 * P], mats[:, 5 * P:6 * P]
    reach_from, _, has_block, eps = (mats[:, 6 * P + i:6 * P + i + 1] for i in range(4))
    own_query = mats[:, 6 * P + 4:]
    cols = sb("cols", [P, 3, P])
    rstd = sb("rstd", [P, S])
    var_sd = sb("var_sd", [P, 2, S])
    sd = var_sd[:, 1, :]
    warm = sb("warm", [P, 16])
    mod = sb("mod", [P, 48])
    gains = sb("gains", [P, 4, KD])
    c_silu = sb("c_silu", [P, KD])

    p1 = ExitStack()
    x_tok = sb("x_tok", [P, TT, D], F32, p1)
    table1 = sb("table1", [32, H1], F32, p1)
    toep = sb("toep", [P, H1, TOEP], F32, p1)
    w_gates = sb("w_gates", [P, KD, 24], F32, p1)
    gates = sb("gates", [P, TT, 24], F32, p1)
    qT = sb("qT", [P, H1 // 2, S], F32, p1)
    kdup = sb("kdup", [P, G1, 2, S], F32, p1)
    v_tok = sb("v_tok", [P, TT, 2 * KV1], F32, p1)
    tblk_hi = sb("tblk_hi", [P, 2, 16, 2 * NCMP], F32R, p1)
    tblk_lo = sb("tblk_lo", [P, 2, 16, 2 * NCMP], F32R, p1)
    tblk = sb("tblk", [P, 2, 16, 2 * NCMP], F32, p1)
    hid = sb("hid", [P, 2, 2, 2 * NCMP], F32, p1)
    w2 = sb("w2", [P, 2, 2, DH], F32, p1)
    kc_dup = sb("kc_dup", [P, 2 * NCMP], F32, p1)
    vc = sb("vc", [NCMP, G1, DH], F32, p1)
    zu = sb("zu", [P, 4, S], F32, p1)
    gv = sb("gv", [P, TT, GW], F32, p1)
    ln_st = sb("ln_st", [P, TT, 8], F32, p1)
    ln_bn = sb("ln_bn", [P, TT, 6], F32, p1)
    wsT = sb("wsT", [P, 8, P], F32, p1)
    bs = sb("bs", [P, 4, P], F32, p1)
    probs01 = sb("probs01", [P, 2, NCP + 2 * S], F32, p1)
    pT = sb("pT", [P, 2, 5, P], F32, p1)
    rows = tblk[:, :, :, :].rearrange("p n t j -> p (n t j)")[:, 0:3 * P].rearrange("p (t n) -> p t n", t=3)
    hot = zu[:, :, :].rearrange("p t s -> p (t s)")[0:32, 0:2 * S]
    bias_row = wsT[:, :, :].rearrange("p g t -> p (g t)")[0:H1, 0:2 * S]
    probs = [probs01[:, 0, :], probs01[:, 1, :],
             gv[:, :, :].rearrange("p t n -> p (t n)")[:, 0:NCP + 2 * S],
             tblk[:, :, :, :].rearrange("p n t j -> p (n t j)")[:, 0:NCP + 2 * S]]
    hid_tok = tblk[:, :, :, :].rearrange("p n t j -> p (n t j)")[0:2 * NCMP, 0:512].rearrange(
        "p (n c) -> p n c", n=2)
    ln_g, ln_b = (probs01[:, :, :].rearrange("p b n -> p (b n)")[:, i * GW:(i + 1) * GW] for i in (0, 1))
    ws = pT[:, :, :, :].rearrange("p b k q -> p (b k) q")[:, 0:8, :]
    st1 = sb("st1", [P, 4, 4, 4], F32, p1)
    mix = x_tok[:, :, :].rearrange("p t d -> p (t d)").rearrange("p (k s) -> p k s", k=KD)
    hankel_a = mT[:, :, :].rearrange("p k s -> p (k s)")[:, 0:5 * TOEP].rearrange("p (h f) -> p h f", h=5)
    hankel_b = x_tok[:, :, :].rearrange("p t d -> p (t d)")[:, 0:3 * TOEP].rearrange("p (h f) -> p h f", h=3)
    bias_dram = nc.dram_tensor("bias_dram", [H1, 2 * S], F32, kind="Internal").ap()
    p1.close()

    pf = ExitStack()
    ada_raw = sb("ada_raw", [P, 4, UNIT], F32, pf)
    ada_acc = sb("ada_acc", [P, 6 * D], F32, pf)
    row_of = sb("row_of", [P, 2 * 48 - 1], F32, pf)
    mod_rows = sb("mod_rows", [48, P], F32, pf)
    silu_g = sb("silu_g", [P, 2, S], F32, pf)
    ffv = sb("ffv", [P, 2, S], F32, pf)
    pf.close()

    p2 = ExitStack()
    szT = sb("szT", [P, KI, S], F32, p2)
    dtd = sb("dtd", [P, 2, TT, HS], F32, p2)
    dt_sc = sb("dt_sc", [P, 3, TT, HS], F32, p2)
    dt_bias = sb("dt_bias", [P, HS], F32, p2)
    a_row = sb("a_row", [P, HS], F32, p2)
    w_dt = sb("w_dt", [P, KD, HS], F32, p2)
    skip = sb("skip", [P, KI], F32, p2)
    pa = ExitStack()
    uq = sb("uq", [P, S, H2], F32, pa)
    oT = sb("oT", [P, H2, S], F32, pa)
    qi = mT
    oT_flat = oT[:, :, :].rearrange("p h s -> p (h s)")
    qn = oT_flat[:, 0:512].rearrange("p (t n) -> p t n", t=TT)
    rn = oT_flat[:, 512:1024].rearrange("p (k s) -> p k s", k=2)
    kin = oT_flat[:, 1024:1280].rearrange("p (t a d) -> p t a d", t=TT, a=2)
    junk = oT_flat[:, 1280:1280 + 6 * QR].rearrange("p (n k) -> p n k", n=6)
    mT_flat = mT[:, :, :].rearrange("p k s -> p (k s)")
    pick = mT_flat[:, 0:1024].bitcast(BF16)
    reached = ff_hi[:, 16:20, :].rearrange("p (b c) s -> p b c s", b=2)
    tab_hi, tab_lo = (ff_lo[:, 16 + i, :].rearrange("p (c m) -> p c m", c=2) for i in range(2))
    work_flat = work[:, :, :].rearrange("p k s -> p (k s)")
    p2T = work_flat[:, 512:1024].rearrange("p (b k r) -> p b k r", b=2, k=2)
    w_uv = work_flat[:, 1024:2048].rearrange("p (h d) -> p h d", h=H2)
    relu_s = work[:, :, :].rearrange("p (b h) k -> p b h k", b=2)
    kv = sb("kv", [P, TT, CKV], F32, pa)
    kv_gain = sb("kv_gain", [P, CKV], F32, pa)
    st2 = sb("st2", [P, TT, 12], F32, pa)
    widx = sb("widx", [P, TT, 16], F32, pa)
    kvT = sb("kvT", [P, S], F32, pa)
    kiT = sb("kiT", [P, S], F32, pa)
    isc = sb("isc", [P, TT, S], F32, pa)
    p2buf = [work_flat[:, 0:S], work_flat[:, S:2 * S], isc[:, 0, :], isc[:, 1, :]]
    top8 = sb("top8", [P, 8], F32, pa)
    pos_i = sb("pos_i", [P, S + TT], I32, pa)
    pos_f = sb("pos_f", [P, S + TT], F32, pa)
    last_i = sb("last_i", [P, TT], I32, pa)
    last_f = sb("last_f", [P, TT], F32, pa)
    shut = sb("shut", [P, TT, S], F32, pa)
    mask = sb("mask", [P, TT, S], BF16, pa)
    own_pos = sb("own_pos", [P, S // 4], F32, pa)
    tab2 = sb("tab2", [32, H2], F32, pa)
    steps = sb("steps", [32, P], F32, pa)
    tab_f = sb("tab_f", [P, 2 * QT, H2], F32, pa)
    st3 = sb("st3", [P, 4, 4], F32, pa)
    pa.close()
    pb = ExitStack()
    xsT = sb("xsT", [P, KI, S], F32, pb)
    x_dt = sb("x_dt", [P, TT, DI], F32, pb)
    bT = sb("bT", [P, NG, S], F32, pb)
    cT = sb("cT", [P, NG, S], F32, pb)
    cbm = var_sd[:, :, :].rearrange("p a s -> p (a s)")[:, 0:384]
    pb.close()
    p2.close()
    ud = work_flat[:, 0:512].rearrange("p (b t s) -> p b t s", b=2, t=2)
    decay = work_flat[:, 512:1280].rearrange("p (b n) -> p b n", b=2)
    m_buf = work_flat[:, 1280:2048].rearrange("p (b n) -> p b n", b=2)
    out_tok = w_raw[:, 0:TT, :]

    tab_f_cm = tab_f[:, :, :].rearrange("p (c q) h -> p c (q h)", c=2)

    class Stream:

        units, blocks, act_blocks, dve_blocks = 0, 0, 0, 0
        sizes = []

        def __init__(self, n, ks, reader):
            self.n, self.ks, self.reader = n, ks, reader
            self.u0, self.b0 = Stream.units, Stream.blocks
            self.act0, self.dve0 = Stream.act_blocks, Stream.dve_blocks
            Stream.units += n * len(ks)
            Stream.sizes += [256 * nk for nk in ks] * n
            Stream.blocks += n
            Stream.act_blocks += n * (reader == "act") + (n // 2) * (reader == "pair")
            Stream.dve_blocks += n * (reader == "dve") + (n // 2) * (reader == "pair")

    s_kc = Stream(1, (4, 4), "dve")
    s_in = Stream(6, (4, 4), "act")
    s_cmp = Stream(2, (4, 4, 4, 4), "act")
    s_u = Stream(2, (4, 4), "act")
    s_wo = Stream(4, (4, 4), "act")
    s_gu = Stream(22, (4, 4), "pair")
    s_dn = Stream(4, (4, 4, 4, 4, 4, 2), "act")
    s_lat = Stream(2, (4, 4), "dve")
    s_qi = Stream(4, (2,), "act")
    s_uq = Stream(8, (2,), "act")
    s_z = Stream(4, (4, 4), "act")
    s_z2 = Stream(4, (4, 4), "act")
    s_ga = Stream(4, (4, 4), "act")
    s_oa = Stream(4, (4, 4), "dve")
    s_xbc = Stream(16, (4, 4), "dve")
    s_gb = Stream(4, (4, 4), "act")
    s_os = Stream(4, (4, 4, 4, 4), "dve")
    s_wo2 = Stream(4, (4, 4), "act")
    s_gu2 = Stream(22, (4, 4), "pair")
    s_dn2 = Stream(4, (4, 4, 4, 4, 4, 2), "act")
    n_units = Stream.units
    pool_topk = range(s_z.u0 + AHEAD, s_z2.u0)
    pool_conv = range(s_xbc.u0 + 3, s_gb.u0, 2)

    landed = [sem(f"landed{i}") for i in range(RING)]
    hi_ready, lo_ready, unit_used = sem("hi_ready"), sem("lo_ready"), sem("unit_used")
    act_read, dve_read = sem("act_read"), sem("dve_read")
    act_own, dve_own, pool_own = sem("act_own"), sem("dve_own"), sem("pool_own")
    mats_in, more_rows_in = sem("mats_in"), sem("more_rows_in")
    consts_in, rows_in, x_in, hot_in = sem("consts_in"), sem("rows_in"), sem("x_in"), sem("hot_in")
    gates_in, mlp_in, gmlp_in, ln_in = sem("gates_in"), sem("mlp_in"), sem("gmlp_in"), sem("ln_in")
    bias_out, toep_in, toep_mm, toep_ready = (sem("bias_out"), sem("toep_in"), sem("toep_mm"),
                                              sem("toep_ready"))
    ada_in = [sem(f"ada_in{i}") for i in range(4)]
    lat_in, pos_in, tab_in, ssd_in, uv_in = (sem("lat_in"), sem("pos_in"), sem("tab_in"),
                                             sem("ssd_in"), sem("uv_in"))
    out_done = sem("out_done")
    rows_T, x_T, x_dve = sem("rows_T"), sem("x_T"), sem("x_dve")
    bias_mm, bias_ready = sem("bias_mm"), sem("bias_ready")
    sq_ready, folded, ss_ready, sd_ready, rstd_ready = (
        sem("sq_ready"), sem("folded"), sem("ss_ready"), sem("sd_ready"), sem("rstd_ready"))
    h_ready, h_hi_ready, h_lo_ready = sem("h_ready"), sem("h_hi_ready"), sem("h_lo_ready")
    x_ready = sem("x_ready")
    gate_mm, gates_act, gates_ready = sem("gate_mm"), sem("gates_act"), sem("gates_ready")
    tblk_hi_ready, tblk_lo_ready = sem("tblk_hi_ready"), sem("tblk_lo_ready")
    hid_T, hid_ready, kcvc_mm, kcvc_ready = (sem("hid_T"), sem("hid_ready"), sem("kcvc_mm"),
                                             sem("kcvc_ready"))
    ws_T, wsT_ready, ln_var, ln_sd, zv_ready, sv_mm, mix_gm = (
        sem("ws_T"), sem("wsT_ready"), sem("ln_var"), sem("ln_sd"), sem("zv_ready"), sem("sv_mm"),
        sem("mix_gm"))
    lg_mm, max_ready, exp_ready, pn_ready, pT_mm, pT_ready, pv_mm, att_ready = (
        sem("lg_mm"), sem("max_ready"), sem("exp_ready"), sem("pn_ready"), sem("pT_mm"),
        sem("pT_ready"), sem("pv_mm"), sem("att_ready"))
    sv_read = sem("sv_read")
    row_ready, mod_mm, mod_copied = sem("row_ready"), sem("mod_mm"), sem("mod_copied")
    ff_hi_ready, ff_lo_ready = sem("ff_hi_ready"), sem("ff_lo_ready")
    ada_used, ada_mm, c_ready, mod_ready = sem("ada_used"), sem("ada_mm"), sem("c_ready"), sem("mod_ready")
    lat_sq, lat_var, lat_sd, lat_T, qn_ready, qn_hi, qn_lo, ki_ready = (
        sem("lat_sq"), sem("lat_var"), sem("lat_sd"), sem("lat_T"),
        sem("qn_ready"), sem("qn_hi"), sem("qn_lo"), sem("ki_ready"))
    ix_mm, ix_relu, ix_sum, mask_ready, pick_ready, tab_ready = (
        sem("ix_mm"), sem("ix_relu"), sem("ix_sum"), sem("mask_ready"), sem("pick_ready"),
        sem("tab_ready"))
    reach_ready, lt_mm, lt_max, lt_exp, lt_p, lt_T, lt_pT, lt_pv, lt_o = (
        sem("reach_ready"), sem("lt_mm"), sem("lt_max"), sem("lt_exp"), sem("lt_p"), sem("lt_T"),
        sem("lt_pT"), sem("lt_pv"), sem("lt_o"))
    step_mm, tab_own, tab_split = sem("step_mm"), sem("tab_own"), sem("tab_split")
    uv_mm, uv_hi, uv_lo = sem("uv_mm"), sem("uv_hi"), sem("uv_lo")
    dt_mm, dt_a, dt_b, dt_ready, xbc_ready = (
        sem("dt_mm"), sem("dt_a"), sem("dt_b"), sem("dt_ready"), sem("xbc_ready"))
    xs_T, xs_ready, cb_mm, cb_ready, ud_ready, seg_mm, dec_ready, m_mat, y_mm, y_ready = (
        sem("xs_T"), sem("xs_ready"), sem("cb_mm"), sem("cb_ready"), sem("ud_ready"),
        sem("seg_mm"), sem("dec_ready"), sem("m_mat"), sem("y_mm"), sem("y_ready"))
    ud_act, tap_ready, sz_ready, sig_ready = (sem("ud_act"), sem("tap_ready"), sem("sz_ready"),
                                              sem("sig_ready"))
    y_gain, y_hi, y_lo, mix2_ready = sem("y_gain"), sem("y_hi"), sem("y_lo"), sem("mix2_ready")
    out_T, out_act, out_ready = sem("out_T"), sem("out_act"), sem("out_ready")

    C_MIX, C_MIXP, C_FFN, C_FFNP, C_MIX2, C_MIXP2, C_FFN2, C_FFNP2, C_C = (8 * i for i in range(9))
    C_SSD, C_CONVB, C_QN, C_KI = 72, 88, 120, 122
    R_USED = (123, 128, 80)
    ADA_B, POS_K, POS_V = 0, 48, 64

    SQ0 = (None, 0, 4, 8, 12, 16, 20, 28, 32, 36)

    FOLD0, fold_count = {}, 0
    for n, chunks in ((2, NCH), (4, NCH), (6, KI // CT), (7, NCH), (9, NCH)):
        FOLD0[n] = fold_count
        fold_count += chunks - 2

    def xbc_tiles(b):
        return (xsT[:, 2 * b:2 * b + 2, :] if b < 8 else bT[:, 2 * b - 16:2 * b - 14, :] if b < 12
                else cT[:, 2 * b - 24:2 * b - 22, :])

    def chunk(c):
        return slice(CT * c, CT * c + CT)

    def col(tile, c):
        return cols[:, tile, c:c + 1]

    def fill_rows():
        def v(name):
            x = a[name]
            return (x if len(x.shape) == 1 else x.rearrange("a n -> (a n)")).rearrange(
                "(t p) -> t p", p=P)
        for c, name in ((C_MIX, "norm_mix_pre"), (C_MIXP, "norm_mix_post"), (C_FFN, "norm_ffn_pre"),
                        (C_FFNP, "norm_ffn_post"), (C_MIX2, "pre_norm_mix_2"),
                        (C_MIXP2, "post_norm_mix_2"), (C_FFN2, "pre_norm_ffn_2"),
                        (C_FFNP2, "post_norm_ffn_2"), (C_C, "c_2"), (C_SSD, "ssd_norm_2"),
                        (C_CONVB, "conv_b_2"), (C_QN, "q_norm_2")):
            x = v(name)
            yield rows[c:c + x.shape[0], 0, :], x
        ki = a["kidx_norm_2"].rearrange("(a n) -> a n", a=1)
        yield rows[C_KI:C_KI + 1, 0, 0:64], ki
        yield rows[C_KI:C_KI + 1, 0, 64:128], ki
        yield rows[:, 1, :], a["conv_w_2"].rearrange("w (t p) -> (w t) p", p=P)
        yield rows[0:48, 2, :], v("ada_b_2")
        yield rows[POS_K:POS_K + 16, 2, :], a["cmp_pos_k"][0].rearrange("(t a) d -> t (a d)", a=2)
        yield rows[POS_V:POS_V + 16, 2, :], a["cmp_pos_v"][0].rearrange("(t a) d -> t (a d)", a=2)

    n_rows_dma, SP_ROWS = 18, 12

    w_in, w_in2 = a["w_in"][0], a["w_in_2"]
    TILES1 = [(h, qt) for hp in range(H1 // 2) for qt in range(TT) for h in (2 * hp, 2 * hp + 1)]

    MIX_ORDER = (2, 3, 0, 1)
    MIX_AT = {8: 2, 9: 3, 13: 0}

    block = ctx.enter_context(nc.Block())

    @block.sync
    def _(sp):
        for t in range(TT):
            sp.dma_start(x_tok[:, t, :], a["x"][0, t * P:(t + 1) * P, :]).then_inc(x_in, 16)
        for dst, src in list(fill_rows())[:SP_ROWS]:
            sp.dma_start(dst, src).then_inc(rows_in, 16)

        def load(i, per, u, src, nk, ncol, part=None):
            dst = w_raw[:, u % RING, 0:nk * ncol].rearrange("p (k c) -> p k c", k=nk)
            if u >= RING:
                sp.wait_ge(hi_ready, at(i, per, u - RING + 1))
                sp.wait_ge(lo_ready, at(i, per, u - RING + 1))
            sp.dma_start(dst, src.rearrange("(k p) c -> p k c", p=P)).then_inc(landed[u % RING], 16)

        def load_block(st, b, w, c0, i=None, per=0, ci=0, ncol=256):
            k, u = 0, st.u0 + b * len(st.ks)
            for nk in st.ks:
                load(i, per, u, w[k * P:(k + nk) * P, bass.ds(at(i, ci, c0), ncol)], nk, ncol)
                k += nk
                u += 1

        def load_stream(st, w, c0):
            n = 2 * len(st.ks)
            with sp.Fori(0, st.n // 2) as i:
                load_block(st, 0, w, c0, i, n, 512)
                load_block(st, 1, w, c0 + 256, i, n, 512)

        def load_pairs(st, w, half):
            with sp.Fori(0, st.n // 2) as i:
                load_block(st, 0, w, 0, i, 2 * len(st.ks), 256)
                load_block(st, 1, w, half, i, 2 * len(st.ks), 256)

        load_block(s_kc, 0, w_in, 512)
        load_block(s_in, 0, w_in, 0)
        load_block(s_in, 1, w_in, 256)
        for j in range(2):
            for br in range(2):
                load(None, 0, s_in.u0 + 4 + 2 * j + br,
                     w_in[4 * P * j:4 * P * (j + 1), 768 + 256 * br:1024 + 256 * br], 4, 256)
        load_block(s_in, 4, w_in, 1816)
        load_block(s_in, 5, w_in, 2072)
        load_block(s_cmp, 0, a["cmp_w1_k"][0], 0)
        load_block(s_cmp, 1, a["cmp_w1_v"][0], 0)
        load_block(s_u, 0, w_in, 1304)
        load_block(s_u, 1, w_in, 1560)
        load_stream(s_wo, a["w_out"][0], 0)
        load_pairs(s_gu, a["w_gate_up"][0], FF)
        load_stream(s_dn, a["w_down"][0], 0)
        load_block(s_lat, 0, w_in2, 0)
        load_block(s_lat, 1, w_in2, 256, ncol=208)
        for b in range(s_qi.n):
            load_block(s_qi, b, a["w_qidx_2"], 256 * b)
        for b in range(s_uq.n):
            load_block(s_uq, b, a["w_uq_2"], 256 * b)
        load_stream(s_z, w_in2, 464)
        load_stream(s_z2, w_in2, 464 + 256 * s_z.n)
        load_stream(s_ga, w_in2, 6640)
        load_stream(s_oa, a["w_o_attn_2"], 0)
        load_stream(s_xbc, w_in2, 2512)
        load_stream(s_gb, w_in2, 7664)
        load_stream(s_os, a["w_o_ssd_2"], 0)
        load_stream(s_wo2, a["w_out_2"], 0)
        load_pairs(s_gu2, a["w_ffn_in_2"], FF)
        load_stream(s_dn2, a["w_ffn_out_2"], 0)
        for half in range(2):
            for t, ready in ((0, out_act), (1, out_ready)):
                sp.wait_ge(ready, half + 1)
                c = slice(512 * half, 512 * half + 512)
                sp.dma_start(out[0, t * P:(t + 1) * P, c], out_tok[:, t, c]).then_inc(out_done, 16)
        sp.wait_ge(out_done, 2 * 16 * TT)

    @block.gpsimd
    def _(pool):
        for dst, src in list(fill_rows())[SP_ROWS:]:
            pool.dma_start(dst, src).then_inc(more_rows_in, 16)
        pool.dma_start(hot[:, :], a["shape_hot"]).then_inc(hot_in, 16)
        pool.dma_start(table1[:, :], a["rel_bias"]).then_inc(hot_in, 16)
        pool.dma_start(w_gates[:, :, :], w_in[:, 1280:1304].rearrange("(k p) c -> p k c", p=P)
                       ).then_inc(gates_in, 16)
        for n, name in enumerate(("cmp_w2_k", "cmp_w2_v")):
            pool.dma_start(w2[:, n, :, :], a[name][0].rearrange("(k p) c -> p k c", p=P)
                           ).then_inc(mlp_in, 16)
        pool.dma_start(ws[:, :, :], a["gmlp_w_s"][0].rearrange("g t s -> t g s")).then_inc(gmlp_in, 16)
        for j in range(2):
            pool.dma_start(bs[j * 64:j * 64 + 64, :, :],
                           bass.AP(a["gmlp_b_s"].tensor, j * P, [[0, 64], [2 * P, 4], [1, P]])
                           ).then_inc(gmlp_in, 16)
        for t, name in ((ln_g, "gmlp_ln_g"), (ln_b, "gmlp_ln_b")):
            pool.dma_start(t[:, :], bass.AP(a[name].tensor, 0, [[0, P], [1, GW]])).then_inc(ln_in, 16)
        pool.wait_ge(bias_ready, 1)
        pool.dma_start(bias_dram, bias_row[:, :]).then_inc(bias_out, 16)
        pool.wait_ge(bias_out, 16)
        pool.wait_ge(x_T, 2)
        for h0, h1, dst in ((0, 5, hankel_a), (5, H1, hankel_b)):
            pool.dma_start(dst, bass.AP(bias_dram.tensor, h0 * 2 * S, [[1, P], [2 * S, h1 - h0], [1, TOEP]])
                           ).then_inc(toep_in, 16)
        def fold(n, sq, c):
            pool.wait_ge(sq_ready, SQ0[n] + c + 1)
            if c >= 2:
                pool.wait_ge(folded, FOLD0[n] + c - 1)
            pool.tensor_tensor(sq[:, chunk(0), :], sq[:, chunk(0), :], sq[:, chunk(c), :], ALU.add
                               ).then_inc(folded, 1)

        pool.wait_ge(sv_read, 1)
        pool.tensor_tensor(mix[:, 4:8, :], mix[:, 4:8, :], zu[:, :, :], ALU.mult).then_inc(mix_gm, 1)
        for c in (1, 2):
            fold(2, work, c)
        pool.wait_ge(x_ready, NCH)
        ada = a["ada_w_2"].rearrange("(k p) c -> p k c", p=P)

        def load_ada(i, per, c):
            for j in range(4):
                if c or i is not None:
                    pool.wait_ge(ada_used, at(i, per, 8 * c + 2 * j - 6))
                pool.dma_start(ada_raw[:, j, 0:2 * MCOL].rearrange("p (k c) -> p k c", k=2),
                               ada[:, 2 * j:2 * j + 2, bass.ds(at(i, MCOL, MCOL * c), MCOL)]
                               ).then_inc(ada_in[j], 16)

        pool.memset(row_of[:, 0:47], 0.0)
        pool.memset(row_of[:, 48:95], 0.0)
        pool.memset(row_of[:, 47:48], 1.0).then_inc(row_ready, 1)
        def split(i, per, u):
            r = u % RING
            pool.wait_ge(hi_ready, at(i, per, u + 1))
            pool.wait_ge(lo_ready, at(i, per, u))
            pool.tensor_tensor(w_lo[:, r, :], w_raw[:, r, :], w_hi[:, r, :].bitcast(F32), ALU.subtract
                               ).then_inc(lo_ready, 1)

        load_ada(None, 0, 0)
        with pool.Fori(0, s_gu.n // 2) as i:
            split(i, 4, s_gu.u0 + AHEAD + 2)
            load_ada(i, 8, 1)
        for c in range(12, 6 * D // MCOL):
            load_ada(None, 0, c)
        for c in (1, 2):
            fold(4, work, c)
        pool.wait_ge(x_ready, 2 * NCH)
        pool.wait_ge(mod_ready, 1)
        pool.dma_start(kv_gain[:, :], bass.AP(a["kv_norm_2"].tensor, 0, [[0, P], [1, CKV]])).then_inc(lat_in, 16)
        pool.dma_start(pos_i[:, 0:S], bass.AP(a["positions_2"].tensor, 0, [[0, P], [1, S]])).then_inc(pos_in, 16)
        pool.dma_start(pos_i[:, S:S + TT], a["positions_2"][0].rearrange("(t p) -> p t", p=P),
                       allow_slow_non_contiguous=True).then_inc(pos_in, 16)
        pool.dma_start(tab2[:, :], a["rel_bias_2"]).then_inc(tab_in, 16)
        pool.dma_start(steps[:, :], a["shape_mats"][0:32, 6 * P + 4 + 2 * QT:]).then_inc(tab_in, 16)
        pool.dma_start(w_dt[:, :, :], w_in2[:, 6608:6640].rearrange("(k p) c -> p k c", p=P)).then_inc(ssd_in, 16)
        pool.dma_start(dt_bias[:, :], bass.AP(a["dt_bias_2"].tensor, 0, [[0, P], [1, HS]])).then_inc(ssd_in, 16)
        pool.dma_start(a_row[:, :], bass.AP(a["a_log_2"].tensor, 0, [[0, P], [1, HS]])).then_inc(ssd_in, 16)
        for j in range(2):
            pool.dma_start(skip[64 * j:64 * j + 64, :],
                           bass.AP(a["d_skip_2"].tensor, j, [[0, 64], [2, KI]]),
                           allow_slow_non_contiguous=True).then_inc(ssd_in, 16)
        pool.wait_ge(ix_sum, 8)
        pool.dma_start(w_uv[:, :, :], a["w_uv_2"].rearrange("h c d -> c h d")).then_inc(uv_in, 16)
        pool.memset(pick[:, :], 1.0).then_inc(pool_own, 1)
        pool.wait_ge(pool_own, 1)
        pool.affine_select(out=pick[:, :], in_=pick[:, :], pattern=[[1, 16 * P]], compare_op=ALU.is_ge,
                           fill=0.0, base=0, channel_multiplier=-16).then_inc(pool_own, 1)
        pool.wait_ge(pool_own, 2)
        pool.affine_select(out=pick[:, :], in_=pick[:, :], pattern=[[-1, 16 * P]], compare_op=ALU.is_ge,
                           fill=0.0, base=15, channel_multiplier=16).then_inc(pick_ready, 1)
        for u in pool_topk:
            split(None, 0, u)
        pool.wait_ge(tab_ready, 1)
        for n in range(NTILE):
            if n >= 2:
                pool.wait_ge(lt_mm, n - 1)
            for c in range(2):
                ins = pool.tensor_scalar(reached[:, n % 2, c, :], pos_f[:, 0:S],
                                         own_pos[:, 2 * n + c:2 * n + c + 1], None, ALU.is_ge)
            ins.then_inc(reach_ready, 1)
        for u in pool_conv:
            split(None, 0, u)
        pool.wait_ge(dt_ready, 1)
        for h in range(HS):
            if h >= 2:
                pool.wait_ge(seg_mm, h - 1)
            pool.tensor_scalar(ud[:, h % 2, 0, :], upper, dtd[:, 1, 0, h:h + 1], None, ALU.mult
                               ).then_inc(ud_ready, 1)
            if h % 4 == 2 and h >= 14:
                fold(6, xsT, (h - 10) // 4)
        fold(6, xsT, KI // CT - 2)
        pool.wait_ge(rstd_ready, 6)
        for b in range(s_gb.n):
            pool.wait_ge(act_read, s_gb.act0 + b + 1)
            pool.tensor_tensor(work[:, chunk(b), :], work[:, chunk(b), :],
                               rstd[:, :].unsqueeze(1).broadcast_to([P, CT, S]), ALU.mult).then_inc(sig_ready, 1)
        for n in (7, 9):
            for c in (1, 2):
                fold(n, work, c)

    @block.scalar
    def _(act):
        own, done_units = [0], [0]

        def link(ins):
            own[0] += 1
            ins.then_inc(act_own, 1)
            act.wait_ge(act_own, own[0])

        def split(i, per, u):
            n = UNIT if i is not None else Stream.sizes[u]
            act.wait_ge(landed[u % RING], at(i, 4 * per, 16 * (u // RING + 1)))
            if u >= RING:
                act.wait_ge(unit_used, at(i, per, u - RING + 1))
            act.activation(w_hi[:, u % RING, 0:n], w_raw[:, u % RING, 0:n], ACT.Copy).then_inc(hi_ready, 1)

        def split_to(u_end):
            while done_units[0] < min(u_end, n_units):
                split(None, 0, done_units[0])
                done_units[0] += 1

        def before_block(st, b):
            end = st.u0 + (b + 1) * len(st.ks)
            split_to(end + AHEAD)
            act.wait_ge(unit_used, end)

        def loop_block(st, b, i, blocks_per_turn=2):
            n = len(st.ks)
            for j in range(n):
                split(i, n * blocks_per_turn, st.u0 + b * n + AHEAD + j)
            act.wait_ge(unit_used, at(i, n * blocks_per_turn, st.u0 + (b + 1) * n))

        def end_loop(st):
            done_units[0] = st.u0 + st.n * len(st.ks) + AHEAD

        def square_x(m):
            for c in range(NCH):
                act.wait_ge(x_ready, NCH * (m - 1) + c + 1)
                act.activation(work[:, chunk(c), :], xT[:, chunk(c), :], ACT.Square).then_inc(sq_ready, 1)

        def root(n, count=D):
            act.activation(warm[:, n:n + 1], eps, ACT.Sqrt)
            act.wait_ge(ss_ready, n)
            act.activation(sd, bank[7][:, 0:S], ACT.Sqrt, bias=eps, scale=1.0 / count).then_inc(sd_ready, 1)

        def operand_hi(n, src, ready, base):
            for c in range(NCH):
                act.wait_ge(ready, base + c + 1)
                act.activation(h_hi[:, chunk(c), :], src[:, chunk(c), :], ACT.Copy).then_inc(h_hi_ready, 1)

        def read_m(st, gain):
            for b in range(st.n):
                before_block(st, b)
                act.activation(work[:, chunk(b), :], bank3[(st.b0 + b) % 2], ACT.Square).then_inc(sq_ready, 1)
                for k in range(CT):
                    ins = act.activation(mT[:, CT * b + k, :], bank3[(st.b0 + b) % 2][:, k, :], ACT.Copy,
                                         scale=gain(CT * b + k))
                ins.then_inc(act_read, 1)

        def read_pairs(st):
            with act.Fori(0, st.n // 2) as i:
                loop_block(st, 0, i)
                act.wait_ge(dve_read, at(i, 1, st.dve0))
                act.activation(silu_g[:, :, :], bank3[st.b0 % 2], ACT.Silu).then_inc(act_read, 1)
                for j in range(2):
                    split(i, 4, st.u0 + 4 + j)
                act.wait_ge(dve_read, at(i, 1, st.dve0 + 1))
                act.activation(ff_hi[:, bass.ds(at(i, 2, 0), 2), :], ffv[:, :, :], ACT.Copy
                               ).then_inc(ff_hi_ready, 1)
            end_loop(st)

        act.dma_start(ident, a["shape_mats"][:, 0:P]).then_inc(consts_in, 16)
        act.dma_start(mats[:, P:], a["shape_mats"][:, P:6 * P + 4 + 2 * QT]).then_inc(mats_in, 16)
        act.wait_ge(consts_in, 16)
        act.activation(warm[:, 0:1], ident[:, 0:1], ACT.Square)
        for j in (0, 1):
            act.wait_ge(x_T, j + 1)
            act.activation(xT[:, chunk(j), :], bank3[2 + j], ACT.Copy)
            act.activation(work[:, chunk(j), :], bank3[2 + j], ACT.Square).then_inc(sq_ready, 1)
        act.wait_ge(mats_in, 16)
        for j in (2, 3):
            act.wait_ge(x_dve, j - 1)
            act.activation(work[:, chunk(j), :], xT[:, chunk(j), :], ACT.Square).then_inc(sq_ready, 1)
        root(1)
        split_to(AHEAD)
        operand_hi(1, work, h_ready, 0)
        split_to(s_kc.u0 + 2 + AHEAD)
        for b in range(2):
            before_block(s_in, b)
            act.activation(qT[:, 2 * b:2 * b + 2, :], bank3[(s_in.b0 + b) % 2], ACT.Copy,
                           scale=DH ** -0.5).then_inc(act_read, 1)
            if b == 0:
                act.wait_ge(dve_read, 1)
                act.activation(tblk_hi[:, :, :, :], tblk[:, :, :, :], ACT.Copy).then_inc(tblk_hi_ready, 1)
        before_block(s_in, 3)
        k_bank, v_bank = bank3[(s_in.b0 + 2) % 2], bank3[(s_in.b0 + 3) % 2]
        for g in range(G1):
            for half in range(2):
                ins = act.activation(kdup[64 * half:64 * half + 64, g, :, :],
                                     k_bank[64 * g:64 * g + 64, :, :], ACT.Copy)
        ins.then_inc(act_read, 1)
        act.activation(v_tok[:, :, :], v_bank, ACT.Copy).then_inc(act_read, 1)
        for b in (4, 5):
            before_block(s_in, b)
            act.activation(gv[:, :, 256 * (b - 4):256 * (b - 3)], bank3[(s_in.b0 + b) % 2],
                           ACT.Gelu_apprx_tanh).then_inc(act_read, 1)
        split_to(s_cmp.u0 + 4)
        act.wait_ge(ln_var, 1)
        act.activation(ln_st[:, :, 2:3], ln_st[:, :, 1:2], ACT.Sqrt).then_inc(ln_sd, 1)
        act.wait_ge(gate_mm, 1)
        act.activation(gates[:, :, :], bank[7][:, 0:48].rearrange("p (t n) -> p t n", t=TT),
                       ACT.Sigmoid).then_inc(gates_act, 1)
        for b in range(2):
            before_block(s_cmp, b)
            act.activation(hid_tok[:, b, :], bank[(s_cmp.b0 + b) % 2][0:2 * NCMP, 0:256],
                           ACT.Gelu_apprx_tanh).then_inc(act_read, 1)
        for b in range(s_u.n):
            if b == 1:
                act.wait_ge(hid_T, 1)
                act.activation(hid[:, :, :, :].rearrange("p n m j -> p (n m j)"), bank[4][:, 0:8 * NCMP],
                               ACT.Copy).then_inc(hid_ready, 1)
            before_block(s_u, b)
            act.activation(zu[:, 2 * b:2 * b + 2, :], bank3[(s_u.b0 + b) % 2],
                           ACT.Gelu_apprx_tanh).then_inc(act_read, 1)
        act.wait_ge(kcvc_mm, 1)
        act.activation(kc_dup[:, :], bank[6][:, 0:2 * NCMP], ACT.Copy)
        act.activation(vc[:, :, :], bank[6][0:NCMP, 128:256].rearrange("p (g d) -> p g d", g=2),
                       ACT.Copy).then_inc(kcvc_ready, 1)
        def mix_hi(c):
            if c < 2:
                act.wait_ge(att_ready, 2 * c + 2)
            else:
                act.wait_ge(mix_gm, 1)
            act.activation(h_hi[:, chunk(c), :], mix[:, chunk(c), :], ACT.Copy).then_inc(h_hi_ready, 1)

        for n in range(len(TILES1) + 2):
            if n in MIX_AT:
                mix_hi(MIX_AT[n])
            if n < len(TILES1):
                nk = P * (TILES1[n][1] + 1)
                act.wait_ge(max_ready, n + 1)
                for br, (c0, cn) in enumerate(((0, NCMP), (NCP, nk), (NCP + S, nk))):
                    ins = act.activation(probs[n % 4][:, c0:c0 + cn], probs[n % 4][:, c0:c0 + cn], ACT.Exp,
                                         bias=st1[:, n % 4, 0, br:br + 1],
                                         accum_out=st1[:, n % 4, 1, br:br + 1])
                ins.then_inc(exp_ready, 1)
            if n >= 2:
                m = n - 2
                qt = TILES1[m][1]
                act.wait_ge(pT_mm, m + 1)
                if m >= 2:
                    act.wait_ge(pv_mm, m - 1)
                act.activation(pT[0:NCMP, m % 2, 0, :], bank[6][0:NCMP, 0:P], ACT.Copy)
                act.activation(pT[:, m % 2, 1:3 + 2 * qt, :],
                               bank[m % 2][:, 0:2 * (qt + 1) * P].rearrange("p (k q) -> p k q", q=P),
                               ACT.Copy).then_inc(pT_ready, 1)
        mix_hi(1)
        read_m(s_wo, lambda k: col(0, C_MIXP + k))
        root(2)
        square_x(1)
        root(3)
        act.activation(c_silu[:, :], cols[:, 0, C_C:C_C + KD], ACT.Silu).then_inc(c_ready, 1)
        operand_hi(3, work, h_ready, NCH)
        read_pairs(s_gu)
        read_m(s_dn, lambda k: col(0, C_FFNP + k))
        root(4)

        square_x(2)
        root(5)
        operand_hi(4, work, h_ready, 2 * NCH)
        split_to(s_lat.u0 + 4)
        act.wait_ge(tab_own, 1)
        act.activation(tab_hi, tab_f_cm, ACT.Copy).then_inc(tab_split, 1)
        for b in range(2):
            before_block(s_lat, b)
            for t in range(TT):
                if b == 0:
                    act.activation(junk[:, t, :], bank3[s_lat.b0 % 2][:, t, :], ACT.Square,
                                   accum_out=st2[:, t, 0:1])
                else:
                    act.activation(junk[:, 2 + t, 0:CKV], bank3[(s_lat.b0 + 1) % 2][:, t, 0:CKV], ACT.Square,
                                   accum_out=st2[:, t, 1:2])
                    ins = act.activation(junk[:, 4 + t, 0:64], bank3[(s_lat.b0 + 1) % 2][:, t, CKV:CKV + 64],
                                         ACT.Square, accum_out=st2[:, t, 2:3])
        ins.then_inc(lat_sq, 1)
        act.wait_ge(lat_var, 1)
        act.activation(st2[:, :, 6:9], st2[:, :, 3:6], ACT.Sqrt).then_inc(lat_sd, 1)
        act.wait_ge(qn_ready, 1)
        act.activation(ff_hi[:, 0:2, :], rn[:, :, :], ACT.Copy).then_inc(qn_hi, 1)
        for b in range(s_qi.n):
            before_block(s_qi, b)
            act.activation(qi[:, 2 * b:2 * b + 2, :], bank3[(s_qi.b0 + b) % 2], ACT.Copy
                           ).then_inc(act_read, 1)
        for r in range(8):
            if r == 4:
                split_to(s_uq.u0 + RING)
            act.wait_ge(ix_mm, r + 1)
            if r >= 2:
                act.wait_ge(ix_sum, r - 1)
            for j in range(2):
                ins = act.activation(relu_s[:, r % 2, 2 * j:2 * j + 2, :], bank3[2 + 2 * (r % 2) + j],
                                     ACT.Relu)
            ins.then_inc(ix_relu, 1)
        for b in range(s_uq.n):
            before_block(s_uq, b)
            act.activation(uq[:, :, 2 * b:2 * b + 2].rearrange("p q h -> p h q"),
                           bank3[(s_uq.b0 + b) % 2], ACT.Copy, scale=CKV ** -0.5).then_inc(act_read, 1)

        def read_z(st, b, tile):
            before_block(st, b)
            act.activation(szT[:, tile:tile + 2, :], bank3[(st.b0 + b) % 2], ACT.Copy).then_inc(act_read, 1)

        for b in range(s_z.n):
            read_z(s_z, b, 2 * b)
        for n in range(NTILE + 2):
            if n < NTILE:
                act.wait_ge(lt_max, n + 1)
                if n >= 4:
                    act.wait_ge(lt_T, n - 3)
                act.activation(p2buf[n % 4], bank[2 + n % 2][:, 0:S], ACT.Exp,
                               bias=st3[:, n % 4, 0:1], accum_out=st3[:, n % 4, 1:2]).then_inc(lt_exp, 1)
            if n >= 2:
                m = n - 2
                act.wait_ge(lt_T, m + 1)
                if m >= 2:
                    act.wait_ge(lt_pv, m - 1)
                act.activation(p2T[:, m % 2, :, :],
                               bank[4 + m % 2][:, 0:S].rearrange("p (k r) -> p k r", k=2),
                               ACT.Copy).then_inc(lt_pT, 1)
            if n % 4 == 0 and n < NTILE:
                split_to(s_z2.u0 + n // 4 + 1 + AHEAD)
            if n % 8 == 1 and n > 8:
                read_z(s_z2, n // 8 - 1, 2 * s_z.n + 2 * (n // 8 - 1))
        for b in range(4):
            act.wait_ge(uv_mm, b + 1)
            act.activation(ff_hi[:, 8 + 2 * b:10 + 2 * b, :], bank3[2 + b], ACT.Copy).then_inc(uv_hi, 1)
        with act.Fori(0, s_ga.n // 2) as i:
            for b in range(2):
                loop_block(s_ga, b, i)
                act.activation(mT[:, bass.ds(at(i, 4, 2 * b), 2), :], bank3[(s_ga.b0 + b) % 2],
                               ACT.Sigmoid).then_inc(act_read, 1)
        end_loop(s_ga)
        for b in range(s_oa.n):
            split_to(s_oa.u0 + (b + 1) * 2 + AHEAD)
        act.wait_ge(act_read, s_z2.act0 + s_z2.n)
        act.activation(szT[:, :, :], szT[:, :, :], ACT.Silu).then_inc(sz_ready, 1)
        act.wait_ge(dt_a, 1)
        link(act.activation(dt_sc[:, 1, :, :], dt_sc[:, 1, :, :], ACT.Exp, scale=-1.0))
        link(act.activation(dt_sc[:, 1, :, :], dt_sc[:, 1, :, :], ACT.Ln, bias=1.0))
        act.activation(a_row[:, :], a_row[:, :], ACT.Exp).then_inc(dt_b, 1)
        def upper_of(h):
            act.activation(ud[:, h % 2, 1, :], upper, ACT.Copy, scale=dtd[:, 1, 1, h:h + 1]).then_inc(ud_act, 1)

        for b in range(s_xbc.n + 1):
            if b < s_xbc.n:
                before_block(s_xbc, b)
                for s in range(2):
                    ins = act.activation(xbc_tiles(b)[:, s, :], bank3[(s_xbc.b0 + b) % 2][:, s, :], ACT.Identity,
                                         scale=col(1, (CONV - 1) * KX + 2 * b + s),
                                         bias=col(0, C_CONVB + 2 * b + s))
                ins.then_inc(tap_ready, 1)
            if b == 8:
                act.wait_ge(dt_ready, 1)
                upper_of(0)
                upper_of(1)
            if b >= 1:
                act.wait_ge(dve_read, s_xbc.dve0 + b)
                act.activation(xbc_tiles(b - 1), xbc_tiles(b - 1), ACT.Silu).then_inc(xbc_ready, 1)
        def square_y(i):
            act.wait_ge(y_ready, i + 1)
            ins = act.activation(xsT[:, i, :], szT[:, i, :], ACT.Square)
            if i % CT == CT - 1:
                ins.then_inc(sq_ready, 1)

        for h in range(HS):
            act.wait_ge(seg_mm, h + 1)
            if h + 2 < HS:
                upper_of(h + 2)
            if h >= 2:
                act.wait_ge(m_mat, h - 1)
            act.activation(decay[:, h % 2, :], bank[2 + h % 2][:, 0:384], ACT.Exp).then_inc(dec_ready, 1)
            if h >= 4 and h % 2 == 0:
                square_y((h - 4) // 2)
        square_y(KI - 2)
        square_y(KI - 1)
        root(6, DI)
        act.wait_ge(y_gain, 1)
        for b in range(s_gb.n):
            split_to(s_gb.u0 + 2 * b + 2 + AHEAD)
            act.activation(ff_hi[:, 4 * b:4 * b + 4, :], szT[:, 4 * b:4 * b + 4, :], ACT.Copy).then_inc(y_hi, 1)
            before_block(s_gb, b)
            act.activation(work[:, chunk(b), :], bank3[(s_gb.b0 + b) % 2], ACT.Sigmoid).then_inc(act_read, 1)
        for b in range(s_os.n):
            split_to(s_os.u0 + (b + 1) * 4 + AHEAD)
        operand_hi(5, mT, mix2_ready, 0)
        read_m(s_wo2, lambda k: gains[:, 1, k:k + 1])
        root(7)
        square_x(3)
        root(8)
        operand_hi(6, work, h_ready, 3 * NCH)
        read_pairs(s_gu2)
        read_m(s_dn2, lambda k: gains[:, 3, k:k + 1])
        root(9)
        for half in range(2):
            act.wait_ge(out_T, half + 1)
            act.activation(out_tok[:, 0, 512 * half:512 * half + 512], bank[2 + half][:, :], ACT.Copy
                           ).then_inc(out_act, 1)

    @block.vector
    def _(dve):
        own, done_units = [0], [0]

        def link(ins):
            own[0] += 1
            ins.then_inc(dve_own, 1)
            dve.wait_ge(dve_own, own[0])

        def lo_of(dst, src, hi):
            return dve.tensor_tensor(dst, src, hi.bitcast(F32), ALU.subtract)

        def split(i, per, u):
            r, n = u % RING, UNIT if i is not None else Stream.sizes[u]
            dve.wait_ge(hi_ready, at(i, per, u + 1))
            lo_of(w_lo[:, r, 0:n], w_raw[:, r, 0:n], w_hi[:, r, 0:n]).then_inc(lo_ready, 1)

        def split_to(u_end):
            while done_units[0] < min(u_end, n_units):
                u = done_units[0]
                if u not in pool_topk and u not in pool_conv:
                    if u - 1 in pool_topk or u - 1 in pool_conv:
                        dve.wait_ge(lo_ready, u)
                    split(None, 0, u)
                done_units[0] += 1

        def before_block(st, b):
            end = st.u0 + (b + 1) * len(st.ks)
            split_to(end + AHEAD)
            dve.wait_ge(unit_used, end)

        def end_loop(st):
            done_units[0] = st.u0 + st.n * len(st.ks) + AHEAD

        def follow(st):
            n = 2 * len(st.ks)
            with dve.Fori(0, st.n // 2) as i:
                for j in range(n):
                    split(i, n, st.u0 + AHEAD + j)
            end_loop(st)

        def rstd_of(n):
            dve.wait_ge(sd_ready, n)
            dve.reciprocal(rstd[:, :], sd).then_inc(rstd_ready, 1)
            dve.wait_ge(rstd_ready, n)

        def normed(c, src, gain):
            for k in range(CT * c, CT * c + CT):
                ins = dve.scalar_tensor_tensor(work[:, k, :], src[:, k, :], gain(k), rstd[:, :],
                                               ALU.mult, ALU.mult)
            return ins

        def operand_lo(c, n, src, turn=None):
            dve.wait_ge(h_hi_ready, NCH * (n - 1) + (c if turn is None else turn) + 1)
            lo_of(h_lo[:, chunk(c), :], src[:, chunk(c), :], h_hi[:, chunk(c), :]).then_inc(h_lo_ready, 1)

        def pre_norm(n, gain, shift=None, units=0):
            for c in range(NCH + 1):
                if c < NCH:
                    ins = normed(c, xT, gain)
                    if shift is not None:
                        link(ins)
                        for k in range(CT * c, CT * c + CT):
                            ins = dve.tensor_scalar(work[:, k, :], work[:, k, :], shift(k), None, ALU.add)
                    ins.then_inc(h_ready, 1)
                if c < units:
                    split_to(c + 1)
                    operand_lo(c, n, work)
                elif c > units:
                    operand_lo(c - 1, n, work)

        def post_norm():
            for c in range(NCH):
                link(dve.tensor_tensor(work[:, chunk(c), :], mT[:, chunk(c), :],
                                       rstd[:, :].unsqueeze(1).broadcast_to([P, CT, S]), ALU.mult))
                dve.tensor_tensor(xT[:, chunk(c), :], xT[:, chunk(c), :], work[:, chunk(c), :], ALU.add
                                  ).then_inc(x_ready, 1)

        def multiply_pairs(st, ff0, extra=None):
            with dve.Fori(0, st.n // 2) as i:
                for j in range(4):
                    if extra and j == 2:
                        extra(i)
                        dve.wait_ge(lo_ready, at(i, 4, st.u0 + AHEAD + j + 1))
                    else:
                        split(i, 4, st.u0 + AHEAD + j)
                dve.wait_ge(unit_used, at(i, 4, st.u0 + 4))
                dve.wait_ge(act_read, at(i, 1, st.act0 + 1))
                dve.tensor_tensor(ffv[:, :, :], silu_g[:, :, :], bank3[(st.b0 + 1) % 2], ALU.mult
                                  ).then_inc(dve_read, 1)
                dve.wait_ge(ff_hi_ready, at(i, 1, ff0 + 1))
                lo_of(ff_lo[:, bass.ds(at(i, 2, 0), 2), :], ffv[:, :, :],
                      ff_hi[:, bass.ds(at(i, 2, 0), 2), :]).then_inc(ff_lo_ready, 1)
            end_loop(st)

        for j in (2, 3):
            dve.wait_ge(x_T, j + 1)
            dve.tensor_copy(xT[:, chunk(j), :], bank3[2 + j]).then_inc(x_dve, 1)
        rstd_of(1)
        dve.wait_ge(rows_T, 1)
        for t in range(3):
            ins = dve.tensor_copy(cols[:, t, 0:R_USED[t]], bank[6][:, t * P:t * P + R_USED[t]])
        link(ins)
        pre_norm(1, lambda k: col(0, C_MIX + k), units=AHEAD)
        dve.wait_ge(bias_mm, 1)
        dve.tensor_copy(bias_row[:, 0:S], bank[1][0:H1, 0:S])
        dve.memset(bias_row[:, S:2 * S], NEG).then_inc(bias_ready, 1)
        before_block(s_kc, 0)
        for n, pos in ((0, POS_K), (1, POS_V)):
            for g in range(G1):
                tok = bank3[s_kc.b0 % 2][64 * g:64 * g + 64, n, :].rearrange("p (j t a) -> p t j a", t=8, a=2)
                for par in range(2):
                    rows64 = slice(64 * par, 64 * par + 64)
                    for c in range(2):
                        ins = dve.tensor_tensor(
                            tblk[rows64, n, 8 * c:8 * c + 8, g * NCMP:(g + 1) * NCMP],
                            tok[:, :, c:c + NCMP, par],
                            cols[rows64, 2, pos + 8 * c:pos + 8 * c + 8].unsqueeze(2).broadcast_to(
                                [64, 8, NCMP]), ALU.add)
        ins.then_inc(dve_read, 1)
        split_to(s_in.u0 + 6 + AHEAD)
        for h in range(H1):
            dve.wait_ge(toep_mm, h + 1)
            dve.tensor_copy(toep[:, h, :], bank[2 + h % 4][:, 0:TOEP]).then_inc(toep_ready, 1)
        split_to(s_in.u0 + 8 + AHEAD)
        dve.wait_ge(tblk_hi_ready, 1)
        lo_of(tblk_lo[:, :, :, :], tblk[:, :, :, :], tblk_hi[:, :, :, :]).then_inc(tblk_lo_ready, 1)
        split_to(s_in.u0 + 12 + AHEAD)
        dve.wait_ge(act_read, s_in.act0 + 6)
        for t in range(TT):
            ins = dve.bn_stats(ln_bn[:, t, :], gv[:, t, :])
        link(ins)
        for t in range(TT):
            ins = dve.bn_aggr(ln_st[:, t, 0:2], ln_bn[:, t, :])
        link(ins)
        dve.tensor_scalar(ln_st[:, :, 1:2], ln_st[:, :, 1:2], 1e-5, None, ALU.add).then_inc(ln_var, 1)
        split_to(s_cmp.u0 + 4)
        dve.wait_ge(ln_sd, 1)
        link(dve.reciprocal(ln_st[:, :, 3:4], ln_st[:, :, 2:3]))
        for t in range(TT):
            ins = dve.tensor_scalar(gv[:, t, :], gv[:, t, :], ln_st[:, t, 0:1], ln_st[:, t, 3:4],
                                    ALU.subtract, ALU.mult)
        link(ins)
        dve.wait_ge(gates_act, 1)
        gate_c = gates[:, 0, 0:24:3]
        dve.tensor_scalar(gate_c, gate_c, has_block, None, ALU.mult).then_inc(gates_ready, 1)
        split_to(s_cmp.u0 + 6)
        dve.wait_ge(ws_T, 1)
        for j in range(2):
            ins = dve.tensor_tensor(wsT[:, 4 * j:4 * j + 4, :],
                                    bank[2 + j][:, :].rearrange("p (g t) -> p g t", g=4),
                                    tri.unsqueeze(1).broadcast_to([P, 4, P]), ALU.mult)
        ins.then_inc(wsT_ready, 1)
        split_to(s_cmp.u0 + 8)
        dve.wait_ge(ln_in, 32)
        link(dve.tensor_tensor(gv[:, :, :], gv[:, :, :], ln_g[:, :].unsqueeze(1).broadcast_to([P, TT, GW]),
                               ALU.mult))
        split_to(s_u.u0 + 2)
        dve.tensor_tensor(gv[:, :, :], gv[:, :, :], ln_b[:, :].unsqueeze(1).broadcast_to([P, TT, GW]),
                          ALU.add).then_inc(zv_ready, 1)
        split_to(s_u.u0 + 4 + AHEAD)
        dve.wait_ge(zv_ready, 1)
        for n in range(len(TILES1) + 4):
            if n - 1 in MIX_AT:
                operand_lo(MIX_AT[n - 1], 2, mix, MIX_ORDER.index(MIX_AT[n - 1]))
            if n >= 7 and (n - 7) % 4 == 0:
                hp = (n - 7) // 4
                dve.wait_ge(pv_mm, 4 * hp + 4)
                dve.tensor_copy(mix[:, hp, :], bank3[7][:, hp % 2, :]).then_inc(att_ready, 1)
            if n < len(TILES1):
                h, qt = TILES1[n]
                nk, off = P * (qt + 1), P * (1 - qt)
                dve.wait_ge(lg_mm, n + 1)
                if n >= 4:
                    dve.wait_ge(pT_mm, n - 3)
                sw = probs[n % 4][:, NCP:NCP + 2 * S].rearrange("p (b k) -> p b k", b=2)[:, :, 0:nk]
                dve.tensor_tensor(sw, bank3[2 + n % 2][:, :, 0:nk],
                                  toep[:, h, off:off + nk].unsqueeze(1).broadcast_to([P, 2, nk]), ALU.add)
                first = off + CBLOCK - 1
                link(dve.tensor_tensor(probs[n % 4][:, 0:NCMP], bank[4 + n % 2][:, 0:NCMP],
                                       toep[:, h, first:first + CSTRIDE * (NCMP - 1) + 1:CSTRIDE], ALU.add))
                dve.tensor_reduce(st1[:, n % 4, 0, 1:3], sw, AX.X, ALU.max, negate=True)
                dve.tensor_reduce(st1[:, n % 4, 0, 0:1], probs[n % 4][:, 0:NCMP], AX.X, ALU.max,
                                  negate=True).then_inc(max_ready, 1)
            if 1 <= n <= len(TILES1):
                m = n - 1
                h, qt = TILES1[m]
                nk = P * (qt + 1)
                dve.wait_ge(exp_ready, m + 1)
                link(dve.reciprocal(st1[:, m % 4, 2, 0:3], st1[:, m % 4, 1, 0:3]))
                link(dve.tensor_tensor(st1[:, m % 4, 3, 0:3], st1[:, m % 4, 2, 0:3],
                                       gates[:, qt, 3 * h:3 * h + 3], ALU.mult))
                for br, (c0, cn) in enumerate(((0, NCMP), (NCP, nk), (NCP + S, nk))):
                    ins = dve.tensor_scalar(probs[m % 4][:, c0:c0 + cn], probs[m % 4][:, c0:c0 + cn],
                                            st1[:, m % 4, 3, br:br + 1], None, ALU.mult)
                ins.then_inc(pn_ready, 1)
            if n == 1:
                dve.wait_ge(sv_mm, 1)
                for i in range(4):
                    ins = dve.tensor_tensor(mix[:, 4 + i, :].rearrange("p (n t) -> p n t", n=2),
                                            bank[i // 2][:, (i % 2) * S:(i % 2 + 1) * S].rearrange(
                                                "p (n t) -> p n t", n=2),
                                            bs[:, i, :].unsqueeze(1).broadcast_to([P, 2, P]), ALU.add)
                ins.then_inc(sv_read, 1)
        operand_lo(1, 2, mix, NCH - 1)
        follow(s_wo)
        rstd_of(2)
        post_norm()
        rstd_of(3)
        pre_norm(3, lambda k: col(0, C_FFN + k))

        def modulate(i, per, c):
            acc = ada_acc[:, bass.ds(at(i, MCOL, MCOL * c), MCOL)]
            for k in range(KD):
                src = ada_raw[:, k // 2, (k % 2) * MCOL:(k % 2 + 1) * MCOL]
                if k % 2 == 0:
                    dve.wait_ge(ada_in[k // 2], at(i, 16, 16 * (c + 1)))
                if k == 0:
                    ins = dve.tensor_scalar(acc, src, c_silu[:, 0:1], None, ALU.mult)
                else:
                    dve.wait_ge(ada_used, at(i, 8, 8 * c + k))
                    ins = dve.scalar_tensor_tensor(acc, src, c_silu[:, k:k + 1], acc, ALU.mult, ALU.add)
                ins.then_inc(ada_used, 1)

        dve.wait_ge(c_ready, 1)
        multiply_pairs(s_gu, 0, extra=lambda i: modulate(i, 8, 0))
        for c in range(11, 6 * D // MCOL):
            split_to(s_dn.u0 + AHEAD + 3 * (c - 10))
            modulate(None, 0, c)
        split_to(s_dn.u0 + 18 + AHEAD)
        dve.wait_ge(mod_mm, 1)
        dve.tensor_copy(mod_rows[:, :], bank[6][0:48, 0:P]).then_inc(mod_copied, 1)
        split_to(s_dn.u0 + 24 + AHEAD)
        dve.wait_ge(ada_mm, 1)
        link(dve.tensor_tensor(mod[:, :], bank[5][:, 0:48], cols[:, 2, ADA_B:ADA_B + 48], ALU.add))
        for n, (m0, c0, plus) in enumerate(((8, C_MIX2, 1.0), (16, C_MIXP2, 0.0), (32, C_FFN2, 1.0),
                                            (40, C_FFNP2, 0.0))):
            ins = dve.scalar_tensor_tensor(gains[:, n, :], mod[:, m0:m0 + 8], plus, cols[:, 0, c0:c0 + 8],
                                           ALU.add, ALU.mult)
        ins.then_inc(mod_ready, 1)
        split_to(s_dn.u0 + 24 + AHEAD)
        rstd_of(4)
        post_norm()

        rstd_of(5)
        pre_norm(4, lambda k: gains[:, 0, k:k + 1], lambda k: mod[:, k:k + 1])
        split_to(s_lat.u0 + 4)
        dve.wait_ge(pos_in, 32)
        dve.tensor_copy(pos_f[:, :], pos_i[:, :])
        link(dve.tensor_scalar(last_i[:, :], pos_i[:, S:S + TT], -64, None, ALU.bitwise_and))
        link(dve.tensor_copy(last_f[:, :], last_i[:, :]))
        link(dve.tensor_scalar(last_f[:, :], last_f[:, :], 64.0, None, ALU.add))
        for t in range(TT):
            dve.tensor_scalar(shut[:, t, :], pos_f[:, 0:S], last_f[:, t:t + 1], NEG, ALU.is_ge, ALU.mult)
        for q in range(4):
            r32 = slice(32 * q, 32 * q + 32)
            dve.tensor_scalar(own_pos[r32, :], pos_f[r32, q:S:4], reach_from[r32, :], None, ALU.add)
        dve.wait_ge(step_mm, 1)
        dve.tensor_tensor(tab_f[:, :, :], bank[5][:, 0:H2].unsqueeze(1).broadcast_to([P, 2 * QT, H2]),
                          own_query.unsqueeze(2).broadcast_to([P, 2 * QT, H2]), ALU.mult).then_inc(tab_own, 1)
        dve.wait_ge(tab_split, 1)
        lo_of(tab_lo, tab_f_cm, tab_hi).then_inc(tab_ready, 1)
        before_block(s_lat, 0)
        before_block(s_lat, 1)
        dve.wait_ge(lat_sq, 1)
        for n, count in enumerate((QR, CKV, 64)):
            ins = dve.tensor_scalar(st2[:, :, 3 + n:4 + n], st2[:, :, n:n + 1], 1.0 / count, 1e-6,
                                    ALU.mult, ALU.add)
        ins.then_inc(lat_var, 1)
        dve.wait_ge(lat_sd, 1)
        link(dve.reciprocal(st2[:, :, 9:12], st2[:, :, 6:9]))
        dve.wait_ge(lat_in, 16)
        b_q, b_k = bank3[s_lat.b0 % 2], bank3[(s_lat.b0 + 1) % 2]
        for t in range(TT):
            ins = dve.tensor_scalar(qn[:, t, :], b_q[:, t, :], st2[:, t, 9:10], None, ALU.mult)
        ins.then_inc(dve_read, 1)
        for t in range(TT):
            dve.scalar_tensor_tensor(kv[:, t, :], b_k[:, t, 0:CKV], st2[:, t, 10:11], kv_gain[:, :],
                                     ALU.mult, ALU.mult)
            dve.tensor_scalar(kin[:, t, :, :], b_k[:, t, CKV:CKV + 64].unsqueeze(1).broadcast_to([P, 2, 64]),
                              st2[:, t, 11:12], None, ALU.mult)
        dve.tensor_scalar(widx[:, :, :], b_k[:, :, 192:208], 16 ** -0.5 * 64 ** -0.5, None, ALU.mult
                          ).then_inc(dve_read, 1)
        dve.wait_ge(lat_T, 1)
        for k in range(2):
            ins = dve.tensor_scalar(rn[:, k, :], bank3[2][:, k, :], col(0, C_QN + k), None, ALU.mult)
        ins.then_inc(qn_ready, 1)
        dve.tensor_copy(kvT[:, :], bank[3][:, 0:S])
        dve.tensor_scalar(kiT[:, :], bank[3][:, S:2 * S], col(0, C_KI), None, ALU.mult).then_inc(ki_ready, 1)
        dve.wait_ge(qn_hi, 1)
        lo_of(ff_lo[:, 0:2, :], rn[:, :, :], ff_hi[:, 0:2, :]).then_inc(qn_lo, 1)
        dve.wait_ge(dt_mm, 1)
        dve.wait_ge(ssd_in, 80)
        link(dve.tensor_tensor(dt_sc[:, 0, :, :], bank[6][:, 0:2 * HS].rearrange("p (t h) -> p t h", t=TT),
                               dt_bias[:, :].unsqueeze(1).broadcast_to([P, TT, HS]), ALU.add))
        link(dve.scalar_tensor_tensor(dt_sc[:, 1, :, :], dt_sc[:, 0, :, :], -1.0, dt_sc[:, 0, :, :],
                                      ALU.mult, ALU.max))
        dve.tensor_scalar(dt_sc[:, 0, :, :], dt_sc[:, 0, :, :], 0.0, None, ALU.max).then_inc(dt_a, 1)
        split_to(s_uq.u0 + AHEAD)
        for r in range(8):
            qt, r4 = r // 4, r % 4
            if r == 6:
                split_to(s_uq.u0 + RING)
            dve.wait_ge(ix_relu, r + 1)
            for j in range(4):
                w = widx[:, qt, 4 * r4 + 2 * (j % 2) + j // 2:4 * r4 + 2 * (j % 2) + j // 2 + 1]
                if r4 == 0 and j == 0:
                    ins = dve.tensor_scalar(isc[:, qt, :], relu_s[:, r % 2, j, :], w, None, ALU.mult)
                else:
                    ins = dve.scalar_tensor_tensor(isc[:, qt, :], relu_s[:, r % 2, j, :], w, isc[:, qt, :],
                                                   ALU.mult, ALU.add)
                if j < 3:
                    link(ins)
            ins.then_inc(ix_sum, 1)
            dve.wait_ge(ix_sum, r + 1)
        link(dve.tensor_tensor(isc[:, :, :], isc[:, :, :], shut[:, :, :], ALU.add))
        for qt in range(TT):
            for r in range(TOPK // 8):
                link(dve.max(top8[:, :], isc[:, qt, :]))
                link(dve.match_replace(isc[:, qt, :], top8[:, :], isc[:, qt, :], NEG_TAKEN))
                split_to(min(s_uq.u0 + RING + 2 * (8 * qt + r + 1), s_z.u0 + AHEAD))
        link(dve.tensor_scalar(isc[:, :, :], isc[:, :, :], -2.0e38, NEG, ALU.is_gt, ALU.mult))
        dve.tensor_tensor(mask[:, :, :], isc[:, :, :], shut[:, :, :], ALU.add).then_inc(mask_ready, 1)
        split_to(s_z2.u0)
        for n in range(NTILE + 4):
            if n < NTILE:
                dve.wait_ge(lt_mm, n + 1)
                if n >= 4:
                    dve.wait_ge(lt_exp, n - 3)
                dve.tensor_reduce(st3[:, n % 4, 0:1], bank[2 + n % 2][:, 0:S], AX.X, ALU.max, negate=True
                                  ).then_inc(lt_max, 1)
            if 1 <= n <= NTILE:
                m = n - 1
                dve.wait_ge(lt_exp, m + 1)
                link(dve.reciprocal(st3[:, m % 4, 2:3], st3[:, m % 4, 1:2]))
                dve.tensor_scalar(p2buf[m % 4], p2buf[m % 4], st3[:, m % 4, 2:3], None, ALU.mult
                                  ).then_inc(lt_p, 1)
            if n >= 4:
                m = n - 4
                dve.wait_ge(lt_pv, m + 1)
                dve.tensor_copy(oT[:, :, QT * m:QT * m + QT],
                                bank[6 + m % 2][:, 0:P].rearrange("p (q h) -> p h q", q=QT)
                                ).then_inc(lt_o, 1)
            if n % 4 == 0 and n < NTILE:
                split_to(s_z2.u0 + n // 4 + 1 + AHEAD)
        for b in range(4):
            dve.wait_ge(uv_hi, b + 1)
            lo_of(ff_lo[:, 8 + 2 * b:10 + 2 * b, :], bank3[2 + b], ff_hi[:, 8 + 2 * b:10 + 2 * b, :]
                  ).then_inc(uv_lo, 1)
        follow(s_ga)
        for b in range(s_oa.n):
            before_block(s_oa, b)
            if b == 0:
                dve.wait_ge(act_read, s_ga.act0 + s_ga.n)
            dve.tensor_tensor(mT[:, 2 * b:2 * b + 2, :], bank3[(s_oa.b0 + b) % 2], mT[:, 2 * b:2 * b + 2, :],
                              ALU.mult).then_inc(dve_read, 1)
        dve.wait_ge(dt_b, 1)
        link(dve.tensor_tensor(dtd[:, 0, :, :], dt_sc[:, 0, :, :], dt_sc[:, 1, :, :], ALU.add))
        dve.scalar_tensor_tensor(dtd[:, 1, :, :], dtd[:, 0, :, :], -1.0,
                                 a_row[:, :].unsqueeze(1).broadcast_to([P, TT, HS]), ALU.mult, ALU.mult
                                 ).then_inc(dt_ready, 1)
        def times_dt(n):
            t, q = n // 4, n % 4
            dve.wait_ge(xs_T, n + 1)
            dve.tensor_tensor(x_dt[:, t, 512 * q:512 * q + 512].rearrange("p (h d) -> p h d", h=8),
                              bank[4 + n % 2][:, :].rearrange("p (h d) -> p h d", h=8),
                              dtd[:, 0, t, 8 * q:8 * q + 8].unsqueeze(2).broadcast_to([P, 8, 64]), ALU.mult
                              ).then_inc(xs_ready, 1)

        for b in range(s_xbc.n):
            before_block(s_xbc, b)
            src = bank3[(s_xbc.b0 + b) % 2]
            dst = xbc_tiles(b)
            dve.wait_ge(tap_ready, b + 1)
            for w in range(CONV - 2, -1, -1):
                if w < CONV - 2:
                    link(ins)
                back = CONV - 1 - w
                for s in range(2):
                    ins = dve.scalar_tensor_tensor(dst[:, s, back:S], src[:, s, 0:S - back],
                                                   col(1, w * KX + 2 * b + s), dst[:, s, back:S],
                                                   ALU.mult, ALU.add)
            ins.then_inc(dve_read, 1)
            if b >= 9:
                times_dt(b - 9)
        times_dt(7)
        dve.wait_ge(sz_ready, 1)
        for h in range(HS + 2):
            if h < HS:
                g = h // 4
                if h % 4 == 0:
                    dve.wait_ge(cb_mm, g + 1)
                    dve.tensor_tensor(cbm, bank[6][:, 0:384], tri_ones_tri, ALU.mult
                                      ).then_inc(cb_ready, 1)
                    dve.wait_ge(cb_ready, g + 1)
                dve.wait_ge(dec_ready, h + 1)
                if h >= 2:
                    dve.wait_ge(y_mm, h - 1)
                dve.tensor_tensor(m_buf[:, h % 2, :], decay[:, h % 2, :], cbm, ALU.mult
                                  ).then_inc(m_mat, 1)
            if h >= 3 and h % 2 == 1:
                i = (h - 3) // 2
                dve.wait_ge(y_mm, 2 * i + 2)
                link(dve.scalar_tensor_tensor(xsT[:, i, :], xsT[:, i, :], skip[:, i:i + 1],
                                              bank[4 + i % 2][:, 0:S], ALU.mult, ALU.add))
                dve.tensor_tensor(szT[:, i, :], szT[:, i, :], xsT[:, i, :], ALU.mult).then_inc(y_ready, 1)
        dve.wait_ge(sq_ready, SQ0[6] + KI // CT)
        for k in range(KI):
            ins = dve.tensor_scalar(szT[:, k, :], szT[:, k, :], col(0, C_SSD + k), None, ALU.mult)
        ins.then_inc(y_gain, 1)
        rstd_of(6)
        for b in range(s_gb.n):
            split_to(s_gb.u0 + 2 * b + 2 + AHEAD)
            dve.wait_ge(y_hi, b + 1)
            lo_of(ff_lo[:, 4 * b:4 * b + 4, :], szT[:, 4 * b:4 * b + 4, :], ff_hi[:, 4 * b:4 * b + 4, :]
                  ).then_inc(y_lo, 1)
        for b in range(s_os.n):
            before_block(s_os, b)
            dve.wait_ge(sig_ready, b + 1)
            part = work[:, 2 * b:2 * b + 2, :]
            dve.tensor_tensor(part, bank3[(s_os.b0 + b) % 2], part, ALU.mult).then_inc(dve_read, 1)
            dve.wait_ge(dve_read, s_os.dve0 + b + 1)
            dve.tensor_tensor(mT[:, 2 * b:2 * b + 2, :], mT[:, 2 * b:2 * b + 2, :], part, ALU.add
                              ).then_inc(mix2_ready, 1)
        for c in range(NCH):
            operand_lo(c, 5, mT)
        follow(s_wo2)
        rstd_of(7)
        post_norm()
        rstd_of(8)
        pre_norm(6, lambda k: gains[:, 2, k:k + 1], lambda k: mod[:, 24 + k:25 + k])
        multiply_pairs(s_gu2, 11)
        split_to(n_units)
        rstd_of(9)
        post_norm()
        for half in range(2):
            dve.wait_ge(out_T, half + 1)
            dve.tensor_copy(out_tok[:, 1, 512 * half:512 * half + 512], bank[4 + half][:, :]
                            ).then_inc(out_ready, 1)

    @block.tensor
    def _(pe):
        def free_bank(st, n, i=None):
            b = st.b0 + n
            if i is None and n >= 2 or i is not None:
                for s, e0 in ((act_read, st.act0), (dve_read, st.dve0)):
                    if (st.reader == "act") == (s is act_read) and st.reader != "pair":
                        pe.wait_ge(s, at(i, 2, e0 + n - 1))
                if st.reader == "pair":
                    if n % 2 == 0:
                        pe.wait_ge(act_read, at(i, 1, st.act0 + n // 2))
                    else:
                        pe.wait_ge(dve_read, at(i, 1, st.dve0 + n // 2))

        def enter(st):
            if st.act0:
                pe.wait_ge(act_read, st.act0)
            if st.dve0:
                pe.wait_ge(dve_read, st.dve0)

        def fm_block(st, n, x_hi, x_lo, i=None, turn=2, k0=0, ready=None):
            for k in range(sum(st.ks)):
                fm_tile(st, n, k, x_hi, x_lo, i, turn, k0, ready)

        def fm_tile(st, n, k, x_hi, x_lo, i=None, turn=2, k0=0, ready=None):
            if k == 0:
                free_bank(st, n, i)
            out_b = bank3[(st.b0 + n) % 2]
            j = k // st.ks[0]
            kk, nk, u = k - j * st.ks[0], st.ks[j], st.u0 + n * len(st.ks) + j
            if kk == 0:
                pe.wait_ge(lo_ready, at(i, turn * len(st.ks), u + 1))
            if ready is not None and ready(k):
                pe.wait_ge(*ready(k))
            hi = w_hi[:, u % RING, 0:nk * 256].rearrange("p (k c) -> p k c", k=nk)
            lo = w_lo[:, u % RING, 0:nk * 256].rearrange("p (k c) -> p k c", k=nk)
            for s in range(2):
                c = slice(s * P, s * P + P)
                for w, x, step in ((hi, x_hi, 0), (hi, x_lo, 1), (lo, x_hi, 2)):
                    ins = pe.matmul(out_b[:, s, :], w[:, kk, c], x[:, k0 + k, :],
                                    start=k == 0 and s == 0 and step == 0,
                                    stop=k == sum(st.ks) - 1 and s == 1 and step == 2,
                                    skip_group_check=True)
            if kk == nk - 1:
                ins.then_inc(unit_used, 1)

        def after(n):
            return lambda k: (h_lo_ready, n + k // CT + 1) if k % CT == 0 else None

        def ff_after(n):
            return lambda k: {0: (ff_lo_ready, n + KF // 2 - 1), KF - 2: (ff_lo_ready, n + KF // 2)}.get(k)

        def tm_block(st, n, x_hi, x_lo, ncol=256, ready=None):
            free_bank(st, n)
            out_b = bank3[(st.b0 + n) % 2]
            u, k, first = st.u0 + n * len(st.ks), 0, True
            for nk in st.ks:
                pe.wait_ge(lo_ready, u + 1)
                hi = w_hi[:, u % RING, 0:nk * ncol].rearrange("p (k c) -> p k c", k=nk)
                lo = w_lo[:, u % RING, 0:nk * ncol].rearrange("p (k c) -> p k c", k=nk)
                for kk in range(nk):
                    if ready is not None and ready(k):
                        pe.wait_ge(*ready(k))
                    end = kk == nk - 1 and u == st.u0 + (n + 1) * len(st.ks) - 1
                    for t in range(TT):
                        c = slice(t * P, t * P + P)
                        for w, x, last in ((hi, x_hi, False), (hi, x_lo, False), (lo, x_hi, True)):
                            ins = pe.matmul(out_b[:, t, 0:ncol], x[:, k, c], w[:, kk, :], start=first,
                                            stop=end and last and t == 1, skip_group_check=True)
                            first = False
                    k += 1
                ins.then_inc(unit_used, 1)
                u += 1

        def kv_blocks(st, n):
            free_bank(st, n)
            free_bank(st, n + 1)
            k_bank, v_bank = bank3[(st.b0 + n) % 2], bank3[(st.b0 + n + 1) % 2]
            for k in range(KD):
                u, kk = st.u0 + 2 * n + 2 * (k // 4), k % 4
                if kk == 0:
                    pe.wait_ge(lo_ready, u + 2)
                r, first, last = u % RING, k == 0, k == KD - 1
                hi = w_hi[:, r:r + 2, :].rearrange("p b (k c) -> p b k c", k=4)
                lo = w_lo[:, r:r + 2, :].rearrange("p b (k c) -> p b k c", k=4)
                for w, x, step in ((hi, h_hi, 0), (hi, h_lo, 1), (lo, h_hi, 2)):
                    for br in range(2):
                        pe.matmul(k_bank[:, br, :], w[:, br, kk, 0:P], x[:, k, :],
                                  start=first and step == 0 and br == 0, stop=last and step == 2 and br == 1,
                                  skip_group_check=True)
                for t in range(TT):
                    c = slice(t * P, t * P + P)
                    for w, x, step in ((hi, h_hi, 0), (hi, h_lo, 1), (lo, h_hi, 2)):
                        ins = pe.matmul(v_bank[:, t, :].rearrange("p (b c) -> p b c", b=2), x[:, k, c],
                                        w[:, :, kk, P:2 * P], start=first and step == 0 and t == 0,
                                        stop=last and step == 2 and t == 1, skip_group_check=True)
                if kk == 3:
                    ins.then_inc(unit_used, 2)

        def fm_stream(st, x_hi, x_lo, k0=0, ready=None, turns=None):
            enter(st)
            if ready is not None:
                fm_block(st, 0, x_hi, x_lo, ready=ready)
                fm_block(st, 1, x_hi, x_lo)
            with pe.Fori(0 if ready is None else 1, turns or st.n // 2) as i:
                for n in range(2):
                    fm_block(st, n, x_hi, x_lo, i, 2, k0)

        def sum_squares(n, sq, tiles=KD):
            chunks = tiles // CT
            for c in (0, chunks - 1) if n in FOLD0 else range(chunks):
                if n in FOLD0 and c == 0:
                    pe.wait_ge(folded, FOLD0[n] + chunks - 2)
                pe.wait_ge(sq_ready, SQ0[n] + c + 1)
                for k in range(CT * c, CT * c + CT):
                    ins = pe.matmul(bank[7][:, 0:S], ones, sq[:, k, :], start=k == 0, stop=k == tiles - 1)
            ins.then_inc(ss_ready, 1)

        def keep_warm(n, b=6):
            for _ in range(n):
                pe.matmul(bank[b][:, 0:S], ones, mats[:, 0:S], start=True, stop=True)

        pe.wait_ge(consts_in, 16)
        pe.wait_ge(x_in, 16 * TT)
        for j in range(4):
            for k in (0, 1):
                for t in range(TT):
                    ins = pe.transpose(bank[2 + j][:, k * S + t * P:k * S + (t + 1) * P],
                                       x_tok[:, t, (2 * j + k) * P:(2 * j + k + 1) * P], ident)
            ins.then_inc(x_T, 1)
        pe.wait_ge(mats_in, 16)
        sum_squares(1, work)
        pe.wait_ge(rows_in, 16 * SP_ROWS)
        pe.wait_ge(more_rows_in, 16 * (n_rows_dma - SP_ROWS))
        for t in range(3):
            ins = pe.transpose(bank[6][:, t * P:t * P + R_USED[t]], rows[0:R_USED[t], t, :],
                               ident[0:R_USED[t], 0:R_USED[t]])
        ins.then_inc(rows_T, 1)
        keep_warm(6, 0)
        pe.wait_ge(hot_in, 32)
        pe.matmul(bank[1][0:H1, :], table1[:, :], hot[:, :], start=True, stop=True).then_inc(bias_mm, 1)
        fm_block(s_kc, 0, h_hi, h_lo, ready=after(0))
        pe.wait_ge(bias_ready, 1)
        fm_block(s_in, 0, h_hi, h_lo)
        pe.wait_ge(dve_read, 1)
        fm_block(s_in, 1, h_hi, h_lo)
        kv_blocks(s_in, 2)
        pe.wait_ge(toep_in, 32)
        for h in range(H1):
            if h >= 4:
                pe.wait_ge(toep_ready, h - 3)
            pe.matmul(bank[2 + h % 4][:, 0:TOEP], flip, hankel_a[:, h, :] if h < 5 else hankel_b[:, h - 5, :],
                      start=True, stop=True).then_inc(toep_mm, 1)
        pe.wait_ge(gates_in, 16)
        for t in range(TT):
            for k in range(KD):
                ins = pe.matmul(bank[7][:, 24 * t:24 * t + 24], work[:, k, t * P:(t + 1) * P],
                                w_gates[:, k, :], start=k == 0, stop=k == KD - 1)
        ins.then_inc(gate_mm, 1)
        tm_block(s_in, 4, h_hi, h_lo)
        tm_block(s_in, 5, h_hi, h_lo)
        pe.wait_ge(gmlp_in, 48)
        pe.wait_ge(toep_ready, H1)
        for g in range(8):
            ins = pe.transpose(bank[2 + g // 4][:, (g % 4) * P:(g % 4 + 1) * P], ws[:, g, :], ident)
        ins.then_inc(ws_T, 1)
        enter(s_cmp)
        pe.wait_ge(tblk_lo_ready, 1)
        for n in range(2):
            out_b = bank[(s_cmp.b0 + n) % 2][0:2 * NCMP, 0:256]
            for k in range(16):
                u, kk = s_cmp.u0 + 4 * n + k // 4, k % 4
                if kk == 0:
                    pe.wait_ge(lo_ready, u + 1)
                hi = w_hi[:, u % RING, :].rearrange("p (k c) -> p k c", k=4)
                lo = w_lo[:, u % RING, :].rearrange("p (k c) -> p k c", k=4)
                for w, x, step in ((hi, tblk_hi, 0), (hi, tblk_lo, 1), (lo, tblk_hi, 2)):
                    ins = pe.matmul(out_b, x[:, n, k, :], w[:, kk, :], start=k == 0 and step == 0,
                                    stop=k == 15 and step == 2)
                if kk == 3:
                    ins.then_inc(unit_used, 1)
        enter(s_u)
        fm_block(s_u, 0, h_hi, h_lo)
        for n in range(2):
            for m in range(2):
                ins = pe.transpose(bank[4][:, (2 * n + m) * 2 * NCMP:(2 * n + m + 1) * 2 * NCMP],
                                   hid_tok[:, n, m * P:(m + 1) * P], ident[0:2 * NCMP, 0:2 * NCMP])
        ins.then_inc(hid_T, 1)
        fm_block(s_u, 1, h_hi, h_lo)
        pe.wait_ge(hid_ready, 1)
        pe.wait_ge(mlp_in, 32)
        for half in range(2):
            for m in range(2):
                pe.matmul(bank[6][64 * half:64 * half + 64, 0:2 * NCMP], w2[:, 0, m, :], hid[:, 0, m, :],
                          start=m == 0, stop=m == 1)
        for g in range(G1):
            for m in range(2):
                ins = pe.matmul(bank[6][0:NCMP, P + 64 * g:P + 64 * g + 64],
                                hid[:, 1, m, g * NCMP:(g + 1) * NCMP], w2[:, 1, m, :],
                                start=m == 0, stop=m == 1)
        ins.then_inc(kcvc_mm, 1)
        pe.wait_ge(kcvc_ready, 1)
        pe.wait_ge(gates_ready, 1)
        for n in range(len(TILES1) + 3):
            if n < len(TILES1):
                h, qt = TILES1[n]
                half, g, nk = h % 2, h // 4, P * (qt + 1)
                r64 = slice(64 * half, 64 * half + 64)
                q = qT[r64, h // 2, qt * P:(qt + 1) * P]
                if n >= 2:
                    pe.wait_ge(max_ready, n - 1)
                for br in range(2):
                    pe.matmul(bank3[2 + n % 2][:, br, 0:nk], q, kdup[r64, g, br, 0:nk], start=True, stop=True)
                pe.matmul(bank[4 + n % 2][:, 0:NCMP], q, kc_dup[r64, g * NCMP:(g + 1) * NCMP],
                          start=True, stop=True).then_inc(lg_mm, 1)
            if n == 1:
                pe.wait_ge(wsT_ready, 1)
                pe.wait_ge(zv_ready, 1)
                pe.wait_ge(act_read, s_u.act0 + s_u.n)
                for g in range(8):
                    for t in range(TT):
                        c0 = (g // 2 % 2) * S + t * P
                        ins = pe.matmul(bank[g // 4][64 * (g % 2):64 * (g % 2) + 64, c0:c0 + P],
                                        gv[:, t, 64 * g:64 * g + 64], wsT[:, g, :], start=True, stop=True)
                ins.then_inc(sv_mm, 1)
            if 2 <= n <= len(TILES1) + 1:
                m = n - 2
                h, qt = TILES1[m]
                if m >= 2:
                    pe.wait_ge(pT_ready, m - 1)
                if m >= 1:
                    keep_warm(2, m % 2)
                pe.wait_ge(pn_ready, m + 1)
                if m == 0:
                    pe.wait_ge(sv_read, 1)
                else:
                    pe.wait_ge(pT_ready, m)
                for br in range(2):
                    for kt in range(qt + 1):
                        c0 = (br * (qt + 1) + kt) * P
                        k0 = NCP + br * S + kt * P
                        pe.transpose(bank[m % 2][:, c0:c0 + P], probs[m % 4][:, k0:k0 + P], ident)
                pe.transpose(bank[6][0:NCMP, 0:P], probs[m % 4][:, 0:NCMP], ident).then_inc(pT_mm, 1)
            if n >= 3:
                m = n - 3
                h, qt = TILES1[m]
                half, g, hp = h % 2, h // 4, m // 4
                pe.wait_ge(pT_ready, m + 1)
                if m % 4 == 0 and hp >= 1:
                    pe.wait_ge(att_ready, hp)
                o = bank[7][64 * half:64 * half + 64, (hp % 2) * S + qt * P:(hp % 2) * S + (qt + 1) * P]
                pe.matmul(o, vc[:, g, :], pT[0:NCMP, m % 2, 0, :], start=True, stop=False)
                for br in range(2):
                    for kt in range(qt + 1):
                        ins = pe.matmul(o, v_tok[:, kt, br * KV1 + 64 * g:br * KV1 + 64 * g + 64],
                                        pT[:, m % 2, 1 + br * (qt + 1) + kt, :], start=False,
                                        stop=br == 1 and kt == qt)
                ins.then_inc(pv_mm, 1)
        fm_stream(s_wo, h_hi, h_lo, ready=lambda k: {0: (h_lo_ready, 2 * NCH - 1), 2: (h_lo_ready, 2 * NCH)}.get(k))
        sum_squares(2, work)
        keep_warm(8)
        sum_squares(3, work)
        keep_warm(8)
        fm_stream(s_gu, h_hi, h_lo, ready=after(2 * NCH))
        enter(s_dn)
        for n in range(s_dn.n):
            fm_block(s_dn, n, ff_hi, ff_lo, ready=ff_after(0) if n == 0 else None)
            if n == 2:
                pe.wait_ge(row_ready, 1)
                pe.wait_ge(ada_used, 8 * (6 * D // MCOL))
                for c in range(48):
                    ins = pe.matmul(bank[6][0:48, 0:P], row_of[:, 47 - c:95 - c], ada_acc[:, c * P:(c + 1) * P],
                                    start=c == 0, stop=c == 47)
                ins.then_inc(mod_mm, 1)
            if n == 3:
                pe.wait_ge(mod_copied, 1)
                pe.transpose(bank[5][:, 0:48], mod_rows[:, :], ident[0:48, 0:48]).then_inc(ada_mm, 1)
        sum_squares(4, work)
        keep_warm(8)

        sum_squares(5, work)
        keep_warm(8)
        pe.wait_ge(tab_in, 32)
        pe.matmul(bank[5][:, 0:H2], steps[:, :], tab2[:, :], start=True, stop=True).then_inc(step_mm, 1)
        enter(s_lat)
        tm_block(s_lat, 0, h_hi, h_lo, ready=after(3 * NCH))
        tm_block(s_lat, 1, h_hi, h_lo, ncol=208)
        pe.wait_ge(ssd_in, 80)
        for t in range(TT):
            for k in range(KD):
                ins = pe.matmul(bank[6][:, HS * t:HS * t + HS], work[:, k, t * P:(t + 1) * P],
                                w_dt[:, k, :], start=k == 0, stop=k == KD - 1)
        ins.then_inc(dt_mm, 1)
        keep_warm(5, 4)
        pe.wait_ge(dve_read, s_lat.dve0 + 2)
        for t in range(TT):
            for k in range(2):
                pe.transpose(bank[2][:, k * S + t * P:k * S + (t + 1) * P], qn[:, t, k * P:(k + 1) * P], ident)
            pe.transpose(bank[3][:, t * P:(t + 1) * P], kv[:, t, :], ident)
            ins = pe.transpose(bank[3][:, S + t * P:S + (t + 1) * P],
                               kin[:, t, :, :].rearrange("p a d -> p (a d)"), ident)
        ins.then_inc(lat_T, 1)
        keep_warm(5, 4)
        pe.wait_ge(qn_lo, 1)
        enter(s_qi)
        for b in range(s_qi.n):
            fm_block(s_qi, b, ff_hi, ff_lo)
        pe.wait_ge(ki_ready, 1)
        pe.wait_ge(act_read, s_qi.act0 + s_qi.n)
        for r in range(8):
            qt, r4 = r // 4, r % 4
            if r >= 2:
                pe.wait_ge(ix_relu, r - 1)
            for j in range(4):
                half, h = j // 2, 4 * r4 + 2 * (j % 2) + j // 2
                r64 = slice(64 * half, 64 * half + 64)
                ins = pe.matmul(bank3[2 + 2 * (r % 2) + half][:, j % 2, :],
                                qi[r64, h // 2, qt * P:(qt + 1) * P], kiT[r64, :], start=True, stop=True)
            ins.then_inc(ix_mm, 1)
        enter(s_uq)
        for b in range(s_uq.n):
            fm_block(s_uq, b, ff_hi, ff_lo)
        fm_stream(s_z, h_hi, h_lo)
        pe.wait_ge(mask_ready, 1)
        pe.wait_ge(pick_ready, 1)
        pe.wait_ge(tab_ready, 1)
        enter(s_z2)
        for n in range(NTILE + 3):
            if n < NTILE:
                lg = bank[2 + n % 2][:, 0:S]
                pe.wait_ge(reach_ready, n + 1)
                if n >= 2:
                    pe.wait_ge(lt_exp, n - 1)
                pe.matmul(lg, uq[:, QT * n:QT * n + QT, :].rearrange("p q h -> p (q h)"), kvT[:, :],
                          start=True, stop=False)
                for c in range(2):
                    for tab in (tab_hi, tab_lo):
                        pe.matmul(lg, tab[:, c, :], reached[:, n % 2, c, :], start=False, stop=False)
                pe.matmul(lg, pick[:, (n % 16) * P:(n % 16 + 1) * P], mask[:, n // 16, :],
                          start=False, stop=True).then_inc(lt_mm, 1)
            if 2 <= n <= NTILE + 1:
                m = n - 2
                pe.wait_ge(lt_p, m + 1)
                if m >= 2:
                    pe.wait_ge(lt_pT, m - 1)
                for k in range(2):
                    ins = pe.transpose(bank[4 + m % 2][:, k * P:(k + 1) * P],
                                       p2buf[m % 4][:, k * P:(k + 1) * P], ident)
                ins.then_inc(lt_T, 1)
            if n < NTILE:
                fm_tile(s_z2, n // KD, n % KD, h_hi, h_lo)
            if n >= 3:
                m = n - 3
                pe.wait_ge(lt_pT, m + 1)
                if m >= 2:
                    pe.wait_ge(lt_o, m - 1)
                for k in range(2):
                    ins = pe.matmul(bank[6 + m % 2][:, 0:P], kv[:, k, :], p2T[:, m % 2, k, :],
                                    start=k == 0, stop=k == 1)
                ins.then_inc(lt_pv, 1)
        pe.wait_ge(uv_in, 16)
        pe.wait_ge(lt_o, NTILE)
        for h in range(H2):
            half = h % 2
            ins = pe.matmul(bank3[2 + h // 4][64 * half:64 * half + 64, h // 2 % 2, :], w_uv[:, h, :],
                            oT[:, h, :], start=True, stop=True)
            if h % 4 == 3:
                ins.then_inc(uv_mm, 1)
        fm_stream(s_ga, h_hi, h_lo)
        pe.wait_ge(uv_lo, 4)
        enter(s_oa)
        fm_stream(s_oa, ff_hi, ff_lo, k0=8)
        fm_stream(s_xbc, h_hi, h_lo, turns=s_xbc.n // 4)
        for b in range(s_xbc.n // 2, s_xbc.n + 1):
            if b < s_xbc.n:
                fm_block(s_xbc, b, h_hi, h_lo)
            if b > s_xbc.n // 2:
                n = b - s_xbc.n // 2 - 1
                t, q = n // 4, n % 4
                if n == 0:
                    pe.wait_ge(xbc_ready, 8)
                if n >= 2:
                    pe.wait_ge(xs_ready, n - 1)
                for j in range(4):
                    ins = pe.transpose(bank[4 + n % 2][:, j * P:(j + 1) * P],
                                       xsT[:, 4 * q + j, t * P:(t + 1) * P], ident)
                ins.then_inc(xs_T, 1)
        for h in range(HS + 2):
            if h < HS:
                g = h // 4
                pe.wait_ge(ud_ready, h + 1)
                pe.wait_ge(ud_act, h + 1)
                if h >= 2:
                    pe.wait_ge(dec_ready, h - 1)
                sg = bank[2 + h % 2]
                pe.matmul(sg[:, 0:S], ud[:, h % 2, 0, :], tri_ones, start=True, stop=False,
                          skip_group_check=True)
                pe.matmul(sg[:, P:S], dtd[:, 1, 1, h:h + 1].broadcast_to([P, P]), tri, start=False,
                          stop=False, skip_group_check=True)
                pe.matmul(sg[:, S:S + P], ud[:, h % 2, 1, :], tri, start=False, stop=True,
                          skip_group_check=True).then_inc(seg_mm, 1)
                if h % 4 == 0:
                    if g >= 1:
                        pe.wait_ge(cb_ready, g)
                    pe.wait_ge(xbc_ready, 12 + g // 2 + 1)
                    pe.matmul(bank[6][:, 0:S], bT[:, g, 0:P], cT[:, g, :], start=True, stop=True)
                    pe.matmul(bank[6][:, S:S + P], bT[:, g, P:S], cT[:, g, P:S], start=True, stop=True
                              ).then_inc(cb_mm, 1)
            if h >= 2:
                m = h - 2
                i, half = m // 2, m % 2
                pe.wait_ge(m_mat, m + 1)
                pe.wait_ge(xs_ready, min(8, 4 + m // 8 + 1))
                if half == 0 and i >= 2:
                    pe.wait_ge(y_ready, i - 1)
                r64 = slice(64 * half, 64 * half + 64)
                pe.matmul(bank[4 + i % 2][r64, 0:S], x_dt[:, 0, 64 * m:64 * m + 64], m_buf[:, m % 2, 0:S],
                          start=True, stop=False)
                pe.matmul(bank[4 + i % 2][r64, P:S], x_dt[:, 1, 64 * m:64 * m + 64],
                          m_buf[:, m % 2, S:S + P], start=False, stop=True).then_inc(y_mm, 1)
        sum_squares(6, xsT, KI)
        fm_stream(s_gb, h_hi, h_lo)
        fm_stream(s_os, ff_hi, ff_lo, ready=lambda k: (y_lo, k // 4 + 1) if k % 4 == 0 else None)
        fm_stream(s_wo2, h_hi, h_lo, ready=after(4 * NCH))
        sum_squares(7, work)
        keep_warm(8)
        sum_squares(8, work)
        keep_warm(8)
        fm_stream(s_gu2, h_hi, h_lo, ready=after(5 * NCH))
        fm_stream(s_dn2, ff_hi, ff_lo, ready=ff_after(KF // 2))
        sum_squares(9, work)
        keep_warm(8)
        for k in range(KD):
            if k % CT == 0:
                pe.wait_ge(x_ready, 3 * NCH + k // CT + 1)
            for t in range(TT):
                ins = pe.transpose(bank[2 + 2 * t + k // 4][:, (k % 4) * P:(k % 4 + 1) * P],
                                   xT[:, k, t * P:(t + 1) * P], ident)
            if k % 4 == 3:
                ins.then_inc(out_T, 1)


def kernel(**inputs):
    import concourse.bacc as bacc
    from concourse.bass_utils import run_bass_kernel_spmd

    nc = bacc.Bacc("TRN2", target_bir_lowering=False, num_devices=1)
    mats, hot = shape_constants()
    arrays = {name: np.ascontiguousarray(x) for name, x in inputs.items()}
    arrays["shape_mats"], arrays["shape_hot"] = mats, hot
    a = {name: nc.dram_tensor(f"in_{name}", x.shape, mybir.dt.from_np(x.dtype),
                              kind="ExternalInput").ap() for name, x in arrays.items()}
    out = nc.dram_tensor("out", (1, S, D), F32, kind="ExternalOutput").ap()
    two_block_kernel(nc, a, out)
    r = run_bass_kernel_spmd(nc, [{f"in_{name}": x for name, x in arrays.items()}], core_ids=[0])
    return r.results[0]["out"]
```
